# Optimizing a Trainium2 kernel written in Bass

```python
import jax, jax.numpy as jnp
from jax import lax
import numpy as np

D_MODEL = 2048
BATCH = 1
SEQ = 256
DEPTH = 1

CTX_LEN = 256
GRID_W = 64
N_DIR = 2
MIX_WIDTH = D_MODEL
GLA_HEADS = 4
GLA_WIDTH = MIX_WIDTH // 2
GLA_DV = GLA_WIDTH // GLA_HEADS
GLA_DK = GLA_DV // 2
GLA_LR = 16
GLA_NORMALIZER = 16.0
MLSTM_HEADS = 4
MLSTM_WIDTH = MIX_WIDTH - GLA_WIDTH
MLSTM_DV = MLSTM_WIDTH // MLSTM_HEADS
MLSTM_DK = MLSTM_DV // 2
CHUNK = 64
D_FF = 128 * ((8 * D_MODEL // 3 + 127) // 128)
CONV_K = 3
EPS = 1e-6

PROJ_SIZES = (GLA_HEADS * GLA_DK, GLA_HEADS * GLA_DK, GLA_WIDTH, GLA_WIDTH, GLA_LR,
              MLSTM_HEADS * MLSTM_DK, MLSTM_HEADS * MLSTM_DK, MLSTM_WIDTH, MLSTM_WIDTH,
              N_DIR * 2 * MLSTM_HEADS)
PROJ_WIDTH = sum(PROJ_SIZES)
PROJ_SPLITS = tuple(int(s) for s in np.cumsum(PROJ_SIZES)[:-1])


def rmsnorm(x, g):
    xf = x.astype(jnp.float32)
    y = xf * lax.rsqrt(jnp.mean(jnp.square(xf), axis=-1, keepdims=True) + EPS)
    return (y * g.astype(jnp.float32)).astype(x.dtype)

def _rev(t, d):
    return jnp.flip(t, axis=1) if d == 1 else t

def _chunk(t):
    b, t_len = t.shape[:2]
    t = t.reshape((b, t_len // CHUNK, CHUNK) + t.shape[2:])
    return jnp.swapaxes(jnp.moveaxis(t, 1, 0), 2, 3)

def _unchunk(t):
    n, b, h, c, d = t.shape
    return jnp.moveaxis(jnp.swapaxes(t, 2, 3), 0, 1).reshape(b, n * c, h, d)

def gla_scan(k, v, log_a, s0, q=None):
    tril = jnp.tril(jnp.ones((CHUNK, CHUNK), dtype=bool))
    xs = (_chunk(k), _chunk(v), _chunk(log_a)) + ((_chunk(q),) if q is not None else ())

    def step(s, inp):
        kc, vc, ac = inp[:3]
        bcum = jnp.cumsum(ac, axis=2)
        b_end = bcum[:, :, -1, :]
        k_to_end = kc * jnp.exp(b_end[:, :, None, :] - bcum)
        s_new = jnp.exp(b_end)[..., None] * s + jnp.einsum('bhik,bhiv->bhkv', k_to_end, vc)
        if q is None:
            return s_new, None
        qc = inp[3]
        rel = jnp.where(tril[:, :, None], bcum[:, :, :, None, :] - bcum[:, :, None, :, :], -jnp.inf)
        scores = jnp.einsum('bhjk,bhik,bhjik->bhji', qc, kc, jnp.exp(rel))
        o = (jnp.einsum('bhji,bhiv->bhjv', scores, vc)
             + jnp.einsum('bhjk,bhkv->bhjv', qc * jnp.exp(bcum), s))
        return s_new, o

    s_fin, o = lax.scan(step, s0, xs)
    return s_fin, (None if q is None else _unchunk(o))

def mlstm_scan(k, v, log_i, log_f, state0, q=None):
    tril = jnp.tril(jnp.ones((CHUNK, CHUNK), dtype=bool))
    xs = (_chunk(k), _chunk(v), _chunk(log_i), _chunk(log_f)) + ((_chunk(q),) if q is not None else ())

    def step(carry, inp):
        c, n, m = carry
        kc, vc, ic, fc = inp[:4]
        fcum = jnp.cumsum(fc, axis=-1)
        f_end = fcum[..., -1]
        w_log = f_end[..., None] - fcum + ic
        m_new = jnp.maximum(f_end + m, jnp.max(w_log, axis=-1))
        carry_scale = jnp.exp(f_end + m - m_new)
        w = jnp.exp(w_log - m_new[..., None])
        c_new = carry_scale[..., None, None] * c + jnp.einsum('bhi,bhik,bhiv->bhkv', w, kc, vc)
        n_new = carry_scale[..., None] * n + jnp.einsum('bhi,bhik->bhk', w, kc)
        if q is None:
            return (c_new, n_new, m_new), None
        qc = inp[4]
        d_log = jnp.where(tril, fcum[..., :, None] - fcum[..., None, :] + ic[..., None, :], -jnp.inf)
        inter_log = fcum + m[..., None]
        m_q = jnp.maximum(inter_log, jnp.max(d_log, axis=-1))
        s = jnp.einsum('bhjk,bhik->bhji', qc, kc) * jnp.exp(d_log - m_q[..., None])
        inter = jnp.exp(inter_log - m_q)
        num = (jnp.einsum('bhji,bhiv->bhjv', s, vc)
               + inter[..., None] * jnp.einsum('bhjk,bhkv->bhjv', qc, c))
        den = jnp.sum(s, axis=-1) + inter * jnp.einsum('bhjk,bhk->bhj', qc, n)
        h = num / jnp.maximum(jnp.abs(den), jnp.exp(-m_q))[..., None]
        return (c_new, n_new, m_new), h

    st_fin, h = lax.scan(step, state0, xs)
    return st_fin, (None if q is None else _unchunk(h))

def project_heads(h, w_in, gla_w_lr, gla_b_lr, mlstm_b_gate):
    b, t, _ = h.shape
    f32 = jnp.float32
    z = jnp.einsum('btd,dp->btp', h, w_in)
    gq, gk, gv, gg, glr, mq, mk, mv, mo, mgate = jnp.split(z, PROJ_SPLITS, axis=-1)
    gla_q = gq.reshape(b, t, GLA_HEADS, GLA_DK).astype(f32) * (GLA_DK ** -0.5)
    gla_k = gk.reshape(b, t, GLA_HEADS, GLA_DK).astype(f32)
    gla_v = gv.reshape(b, t, GLA_HEADS, GLA_DV).astype(f32)
    gla_gate = gg.reshape(b, t, GLA_HEADS, GLA_DV)
    dec = jnp.einsum('btr,zrk->zbtk', glr, gla_w_lr) + gla_b_lr[:, None, None, :]
    gla_loga = (jax.nn.log_sigmoid(dec.astype(f32)) / GLA_NORMALIZER).reshape(N_DIR, b, t, GLA_HEADS, GLA_DK)
    ml_q = mq.reshape(b, t, MLSTM_HEADS, MLSTM_DK).astype(f32)
    ml_k = mk.reshape(b, t, MLSTM_HEADS, MLSTM_DK).astype(f32) * (MLSTM_DK ** -0.5)
    ml_v = mv.reshape(b, t, MLSTM_HEADS, MLSTM_DV).astype(f32)
    ml_ogate = mo.reshape(b, t, MLSTM_HEADS, MLSTM_DV)
    pre = (mgate.reshape(b, t, N_DIR, 2, MLSTM_HEADS) + mlstm_b_gate).astype(f32)
    ml_logi = jnp.moveaxis(pre[:, :, :, 0], 2, 0)
    ml_logf = jnp.moveaxis(jax.nn.log_sigmoid(pre[:, :, :, 1]), 2, 0)
    scan_in = (gla_q, gla_k, gla_v, gla_loga, ml_q, ml_k, ml_v, ml_logi, ml_logf)
    return scan_in, (gla_gate, ml_ogate)

def recurrent_groups(lat, ctx, with_ctx_out):
    gq, gk, gv, ga, mq, mk, mv, mi, mf = lat
    cq, ck, cv, ca, cmq, cmk, cmv, cmi, cmf = ctx
    b = gq.shape[0]
    f32 = jnp.float32
    gla_lat, ml_lat, gla_ctx, ml_ctx = [], [], [], []
    for d in range(N_DIR):
        s0 = jnp.zeros((b, GLA_HEADS, GLA_DK, GLA_DV), f32)
        s_ctx, o_ctx = gla_scan(_rev(ck, d), _rev(cv, d), _rev(ca[d], d), s0,
                                _rev(cq, d) if with_ctx_out else None)
        _, o_lat = gla_scan(_rev(gk, d), _rev(gv, d), _rev(ga[d], d), s_ctx, _rev(gq, d))
        gla_lat.append(_rev(o_lat, d))
        st0 = (jnp.zeros((b, MLSTM_HEADS, MLSTM_DK, MLSTM_DV), f32),
               jnp.zeros((b, MLSTM_HEADS, MLSTM_DK), f32),
               jnp.zeros((b, MLSTM_HEADS), f32))
        st_ctx, h_ctx = mlstm_scan(_rev(cmk, d), _rev(cmv, d), _rev(cmi[d], d), _rev(cmf[d], d), st0,
                                   _rev(cmq, d) if with_ctx_out else None)
        _, h_lat = mlstm_scan(_rev(mk, d), _rev(mv, d), _rev(mi[d], d), _rev(mf[d], d), st_ctx, _rev(mq, d))
        ml_lat.append(_rev(h_lat, d))
        if with_ctx_out:
            gla_ctx.append(_rev(o_ctx, d))
            ml_ctx.append(_rev(h_ctx, d))
    lat_out = (gla_lat[0] + gla_lat[1], ml_lat[0] + ml_lat[1])
    ctx_out = (gla_ctx[0] + gla_ctx[1], ml_ctx[0] + ml_ctx[1]) if with_ctx_out else None
    return lat_out, ctx_out

def merge_groups(gla_o, ml_h, gla_gate, ml_ogate, gla_g_norm, mlstm_g_norm, w_out, dtype):
    b, t = gla_o.shape[:2]
    f32 = jnp.float32
    y_gla = rmsnorm(gla_o, gla_g_norm) * jax.nn.silu(gla_gate.astype(f32))
    y_ml = jax.nn.sigmoid(ml_ogate.astype(f32)) * rmsnorm(ml_h, mlstm_g_norm)
    y = jnp.concatenate([y_gla.reshape(b, t, GLA_WIDTH), y_ml.reshape(b, t, MLSTM_WIDTH)], axis=-1)
    return jnp.einsum('btm,md->btd', y.astype(dtype), w_out)

def conv_ffn(h, rows, cols, w_up, conv_w, conv_b, w_down):
    b, t, _ = h.shape
    u = jnp.einsum('btd,df->btf', h, w_up)
    u_gate, u_val = jnp.split(u, 2, axis=-1)
    g = lax.conv_general_dilated(u_gate.reshape(b, rows, cols, D_FF), conv_w[:, :, None, :],
                                 window_strides=(1, 1), padding='SAME',
                                 dimension_numbers=('NHWC', 'HWIO', 'NHWC'),
                                 feature_group_count=D_FF)
    g = g.reshape(b, t, D_FF) + conv_b
    return jnp.einsum('btf,fd->btd', jax.nn.silu(g) * u_val, w_down)

def trunk_layer(x, ctx, c_act, cc_act, w_mod, b_mod, g_norm1, g_norm2, w_in, gla_w_lr, gla_b_lr,
                mlstm_b_gate, gla_g_norm, mlstm_g_norm, w_out, w_up, conv_w, conv_b, w_down, update_ctx):
    b, t, _ = x.shape
    rows = t // GRID_W
    mod = (c_act @ w_mod + b_mod)[:, None, :]
    mod_c = (cc_act @ w_mod + b_mod)[None, None, :]
    sh1, sc1, gt1, sh2, sc2, gt2 = jnp.split(mod, 6, axis=-1)
    csh1, csc1, cgt1, csh2, csc2, cgt2 = jnp.split(mod_c, 6, axis=-1)

    h = rmsnorm(x, g_norm1) * (1 + sc1) + sh1
    hc = rmsnorm(ctx, g_norm1) * (1 + csc1) + csh1
    lat_in, lat_gates = project_heads(h, w_in, gla_w_lr, gla_b_lr, mlstm_b_gate)
    ctx_in, ctx_gates = project_heads(hc, w_in, gla_w_lr, gla_b_lr, mlstm_b_gate)
    (lat_gla, lat_ml), ctx_out = recurrent_groups(lat_in, ctx_in, update_ctx)
    x = x + gt1 * merge_groups(lat_gla, lat_ml, lat_gates[0], lat_gates[1],
                               gla_g_norm, mlstm_g_norm, w_out, x.dtype)

    h2 = rmsnorm(x, g_norm2) * (1 + sc2) + sh2
    x = x + gt2 * conv_ffn(h2, rows, GRID_W, w_up, conv_w, conv_b, w_down)

    if update_ctx:
        ctx = ctx + cgt1 * merge_groups(ctx_out[0], ctx_out[1], ctx_gates[0], ctx_gates[1],
                                        gla_g_norm, mlstm_g_norm, w_out, ctx.dtype)
        hc2 = rmsnorm(ctx, g_norm2) * (1 + csc2) + csh2
        ctx = ctx + cgt2 * conv_ffn(hc2, 1, ctx.shape[1], w_up, conv_w, conv_b, w_down)
    return x, ctx

def first_inputs(seed: int = 0) -> dict:
    key = jax.random.key(seed)
    ks = jax.random.split(key, 20)
    f32 = jnp.float32
    L = DEPTH

    def nrm(k, shape, s):
        return jax.random.normal(k, shape, f32) * s

    gate_base = jnp.array([0.0, 3.0], f32)[None, None, :, None]
    return {
        'x': nrm(ks[0], (BATCH, SEQ, D_MODEL), 1.0),
        'c': nrm(ks[1], (BATCH, D_MODEL), 1.0),
        'ctx': nrm(ks[2], (BATCH, CTX_LEN, D_MODEL), 1.0),
        'c_ctx': nrm(ks[3], (D_MODEL,), 1.0),
        'w_mod': nrm(ks[4], (L, D_MODEL, 6 * D_MODEL), D_MODEL ** -0.5),
        'b_mod': nrm(ks[5], (L, 6 * D_MODEL), 0.01),
        'g_norm1': 1.0 + nrm(ks[6], (L, D_MODEL), 0.05),
        'g_norm2': 1.0 + nrm(ks[7], (L, D_MODEL), 0.05),
        'w_in': nrm(ks[8], (L, D_MODEL, PROJ_WIDTH), D_MODEL ** -0.5),
        'gla_w_lr': nrm(ks[9], (L, N_DIR, GLA_LR, GLA_HEADS * GLA_DK), GLA_LR ** -0.5),
        'gla_b_lr': nrm(ks[10], (L, N_DIR, GLA_HEADS * GLA_DK), 0.1),
        'mlstm_b_gate': gate_base + nrm(ks[11], (L, N_DIR, 2, MLSTM_HEADS), 0.1),
        'gla_g_norm': 1.0 + nrm(ks[12], (L, GLA_DV), 0.05),
        'mlstm_g_norm': 1.0 + nrm(ks[13], (L, MLSTM_DV), 0.05),
        'w_out': nrm(ks[14], (L, MIX_WIDTH, D_MODEL), MIX_WIDTH ** -0.5),
        'w_up': nrm(ks[15], (L, D_MODEL, 2 * D_FF), D_MODEL ** -0.5),
        'conv_w': nrm(ks[16], (L, CONV_K, CONV_K, D_FF), 1.0 / CONV_K),
        'conv_b': nrm(ks[17], (L, D_FF), 0.01),
        'w_down': nrm(ks[18], (L, D_FF, D_MODEL), D_FF ** -0.5),
        'g_final': 1.0 + nrm(ks[19], (D_MODEL,), 0.05),
    }

def first_block(x, c, ctx, c_ctx, w_mod, b_mod, g_norm1, g_norm2, w_in, gla_w_lr, gla_b_lr, mlstm_b_gate,
              gla_g_norm, mlstm_g_norm, w_out, w_up, conv_w, conv_b, w_down, g_final):
    c_act = jax.nn.silu(c)
    cc_act = jax.nn.silu(c_ctx)
    for l in range(DEPTH):
        x, ctx = trunk_layer(x, ctx, c_act, cc_act, w_mod[l], b_mod[l], g_norm1[l], g_norm2[l], w_in[l],
                             gla_w_lr[l], gla_b_lr[l], mlstm_b_gate[l], gla_g_norm[l], mlstm_g_norm[l],
                             w_out[l], w_up[l], conv_w[l], conv_b[l], w_down[l],
                             update_ctx=(l < DEPTH - 1))
    return rmsnorm(x, g_final)


DEPTH_2 = 2

PLE_DIM = 256
POOL_EXPAND = 2
E_POOL = POOL_EXPAND * D_MODEL
POOL_WINDOWS = (2, 4, 8, 16)
N_POOL_GROUPS = len(POOL_WINDOWS)
G_POOL = E_POOL // N_POOL_GROUPS
N_HEADS = D_MODEL // 128
Q_RANK = 512
KV_RANK = 512
NOPE_DIM = 128
ROPE_DIM = 64
V_DIM = 128
QK_DIM = NOPE_DIM + ROPE_DIM
E_MLA = N_HEADS * V_DIM
ROPE_THETA = 10000.0
Q_BLOCK = 128
SM_SCALE = QK_DIM ** -0.5
NEG_INF = -1e30
N_POOL_LAYERS = (DEPTH_2 + 1) // 2
N_MLA_LAYERS = DEPTH_2 // 2
MLA_IN_DIM = Q_RANK + KV_RANK + ROPE_DIM + E_MLA


def rms_norm(x, g):
    xf = x.astype(jnp.float32)
    y = xf * lax.rsqrt(jnp.mean(xf * xf, axis=-1, keepdims=True) + EPS)
    return (y * g.astype(jnp.float32)).astype(x.dtype)

def rope(x, cos, sin):
    x1, x2 = jnp.split(x.astype(jnp.float32), 2, axis=-1)
    out = jnp.concatenate([x1 * cos - x2 * sin, x2 * cos + x1 * sin], axis=-1)
    return out.astype(x.dtype)

def pool_mixer(xn, w_in, w_group, scale, w_out):
    B, S, _ = xn.shape
    z = xn @ w_in
    u, g = jnp.split(z, 2, axis=-1)
    uf = u.astype(jnp.float32)
    csum = jnp.concatenate([jnp.zeros((B, 1, E_POOL), jnp.float32), jnp.cumsum(uf, axis=1)], axis=1)
    t = jnp.arange(S)
    pooled = []
    for j, w in enumerate(POOL_WINDOWS):
        sl = slice(j * G_POOL, (j + 1) * G_POOL)
        c = csum[:, :, sl]
        lagged = jnp.concatenate([jnp.zeros((B, w - 1, G_POOL), jnp.float32), c[:, :S - w + 1]], axis=1)
        count = jnp.minimum(t + 1, w).astype(jnp.float32)[None, :, None]
        pooled.append((c[:, 1:] - lagged) / count - uf[:, :, sl])
    pooled = jnp.stack(pooled, axis=2).astype(xn.dtype)
    mixed = jnp.einsum('bsgc,gcd->bsgd', pooled, w_group).reshape(B, S, E_POOL)
    return (mixed * scale * jax.nn.silu(g)) @ w_out

def causal_block_attention(q, k, v):
    B, S, H, Dq = q.shape
    nb = S // Q_BLOCK
    qb = q.reshape(B, nb, Q_BLOCK, H, Dq).transpose(1, 0, 2, 3, 4)
    kpos = jnp.arange(S)

    def one_block(args):
        qi, blk = args
        qpos = blk * Q_BLOCK + jnp.arange(Q_BLOCK)
        s = jnp.einsum('bqhd,bkhd->bhqk', qi, k, preferred_element_type=jnp.float32) * SM_SCALE
        s = jnp.where(kpos[None, :] <= qpos[:, None], s, NEG_INF)
        pr = jax.nn.softmax(s, axis=-1).astype(v.dtype)
        return jnp.einsum('bhqk,bkhd->bqhd', pr, v)

    out = lax.map(one_block, (qb, jnp.arange(nb)))
    return out.transpose(1, 0, 2, 3, 4).reshape(B, S, H, V_DIM)

def mla_mixer(xn, cos, sin, w_in, q_norm, w_uq, kv_norm, w_ukv, w_out):
    B, S, _ = xn.shape
    z = xn @ w_in
    q_lat = z[..., :Q_RANK]
    kv_lat = z[..., Q_RANK:Q_RANK + KV_RANK]
    k_pe = z[..., Q_RANK + KV_RANK:Q_RANK + KV_RANK + ROPE_DIM]
    g = z[..., Q_RANK + KV_RANK + ROPE_DIM:]
    q = (rms_norm(q_lat, q_norm) @ w_uq).reshape(B, S, N_HEADS, QK_DIM)
    kv = (rms_norm(kv_lat, kv_norm) @ w_ukv).reshape(B, S, N_HEADS, NOPE_DIM + V_DIM)
    q_nope, q_pe = q[..., :NOPE_DIM], q[..., NOPE_DIM:]
    k_nope, v = kv[..., :NOPE_DIM], kv[..., NOPE_DIM:]
    q_pe = rope(q_pe, cos[:, :, None, :], sin[:, :, None, :])
    k_pe = rope(k_pe, cos, sin)
    q = jnp.concatenate([q_nope, q_pe], axis=-1)
    k = jnp.concatenate([k_nope, jnp.broadcast_to(k_pe[:, :, None, :], (B, S, N_HEADS, ROPE_DIM))], axis=-1)
    o = causal_block_attention(q, k, v).reshape(B, S, E_MLA)
    return (o * jax.nn.silu(g)) @ w_out

def second_inputs(seed: int = 0) -> dict:
    key = jax.random.key(seed)
    ks = jax.random.split(key, 24)
    f32 = jnp.float32

    def nrm(k, shape, fan_in):
        return jax.random.normal(k, shape, f32) * (fan_in ** -0.5)

    def gain(k, shape):
        return 1.0 + 0.02 * jax.random.normal(k, shape, f32)

    offs = jax.random.randint(ks[2], (BATCH, 1), 0, 1024, dtype=jnp.int32)
    positions = offs + jnp.arange(SEQ, dtype=jnp.int32)[None, :]
    return {
        "x": jax.random.normal(ks[0], (BATCH, SEQ, D_MODEL), f32),
        "p": jax.random.normal(ks[1], (DEPTH_2, BATCH, SEQ, PLE_DIM), f32),
        "positions": positions,
        "pre_norm": gain(ks[3], (DEPTH_2, D_MODEL)),
        "post_norm": gain(ks[4], (DEPTH_2, D_MODEL)),
        "pool_w_in": nrm(ks[5], (N_POOL_LAYERS, D_MODEL, 2 * E_POOL), D_MODEL),
        "pool_w_group": nrm(ks[6], (N_POOL_LAYERS, N_POOL_GROUPS, G_POOL, G_POOL), G_POOL),
        "pool_scale": gain(ks[7], (N_POOL_LAYERS, E_POOL)),
        "pool_w_out": nrm(ks[8], (N_POOL_LAYERS, E_POOL, D_MODEL), E_POOL),
        "mla_w_in": nrm(ks[9], (N_MLA_LAYERS, D_MODEL, MLA_IN_DIM), D_MODEL),
        "mla_q_norm": gain(ks[10], (N_MLA_LAYERS, Q_RANK)),
        "mla_w_uq": nrm(ks[11], (N_MLA_LAYERS, Q_RANK, N_HEADS * QK_DIM), Q_RANK),
        "mla_kv_norm": gain(ks[12], (N_MLA_LAYERS, KV_RANK)),
        "mla_w_ukv": nrm(ks[13], (N_MLA_LAYERS, KV_RANK, N_HEADS * (NOPE_DIM + V_DIM)), KV_RANK),
        "mla_w_out": nrm(ks[14], (N_MLA_LAYERS, E_MLA, D_MODEL), E_MLA),
        "ple_norm": gain(ks[15], (DEPTH_2, D_MODEL)),
        "ple_w_gate": nrm(ks[16], (DEPTH_2, D_MODEL, D_MODEL), D_MODEL),
        "ple_w_proj": nrm(ks[17], (DEPTH_2, PLE_DIM, D_MODEL), PLE_DIM),
    }

def second_block(x, p, positions, pre_norm, post_norm, pool_w_in, pool_w_group, pool_scale, pool_w_out,
              mla_w_in, mla_q_norm, mla_w_uq, mla_kv_norm, mla_w_ukv, mla_w_out,
              ple_norm, ple_w_gate, ple_w_proj):
    inv_freq = ROPE_THETA ** (-jnp.arange(0, ROPE_DIM, 2, dtype=jnp.float32) / ROPE_DIM)
    ang = positions.astype(jnp.float32)[..., None] * inv_freq
    cos, sin = jnp.cos(ang), jnp.sin(ang)
    h = x
    for i in range(DEPTH_2):
        xn = rms_norm(h, pre_norm[i])
        j = i // 2
        if i % 2 == 0:
            out = pool_mixer(xn, pool_w_in[j], pool_w_group[j], pool_scale[j], pool_w_out[j])
        else:
            out = mla_mixer(xn, cos, sin, mla_w_in[j], mla_q_norm[j], mla_w_uq[j],
                            mla_kv_norm[j], mla_w_ukv[j], mla_w_out[j])
        h = h + rms_norm(out, post_norm[i])
        gate = jax.nn.sigmoid(rms_norm(h, ple_norm[i]) @ ple_w_gate[i])
        h = h + (p[i] @ ple_w_proj[i]) * gate
    return h


def setup_inputs(seed=0):
    out = dict(first_inputs(seed))
    for name, value in second_inputs(seed + 1).items():
        if name != "x":
            out[name + "_2"] = value
    return out


def reference(
    x, c, ctx, c_ctx, w_mod, b_mod, g_norm1, g_norm2, w_in, gla_w_lr, gla_b_lr, mlstm_b_gate,
    gla_g_norm, mlstm_g_norm, w_out, w_up, conv_w, conv_b, w_down, g_final, p_2, positions_2,
    pre_norm_2, post_norm_2, pool_w_in_2, pool_w_group_2, pool_scale_2, pool_w_out_2,
    mla_w_in_2, mla_q_norm_2, mla_w_uq_2, mla_kv_norm_2, mla_w_ukv_2, mla_w_out_2, ple_norm_2,
    ple_w_gate_2, ple_w_proj_2,
):
    x = first_block(
        x, c, ctx, c_ctx, w_mod, b_mod, g_norm1, g_norm2, w_in, gla_w_lr, gla_b_lr,
        mlstm_b_gate, gla_g_norm, mlstm_g_norm, w_out, w_up, conv_w, conv_b, w_down, g_final,
    )
    return second_block(
        x, p_2, positions_2, pre_norm_2, post_norm_2, pool_w_in_2, pool_w_group_2, pool_scale_2,
        pool_w_out_2, mla_w_in_2, mla_q_norm_2, mla_w_uq_2, mla_kv_norm_2, mla_w_ukv_2,
        mla_w_out_2, ple_norm_2, ple_w_gate_2, ple_w_proj_2,
    )


_drawn_inputs = setup_inputs


def setup_inputs(seed=0):
    import zlib

    import numpy as np

    out = dict(_drawn_inputs(seed))
    spreads = {}
    factors = {'mlstm_g_norm': 3.092,
     'conv_b': 8.0,
     'post_norm_2': 2.855,
     'pool_scale_2': 3.519,
     'mla_q_norm_2': 6.518,
     'mla_kv_norm_2': 4.033,
     'ple_norm_2': 23.098}
    for name, (base, spread) in spreads.items():
        noise = np.random.default_rng([zlib.crc32(name.encode()), seed]).standard_normal(out[name].shape)
        drawn = base * np.exp(spread * noise) if base else spread * noise
        out[name] = __import__('jax').numpy.asarray(drawn.astype(out[name].dtype))
    for name, factor in factors.items():
        out[name] = (out[name] * factor).astype(out[name].dtype)
    return out
```

```python
from contextlib import ExitStack

import numpy as np
import concourse.bass as bass
from concourse import mybir

F32 = mybir.dt.float32
F32R = mybir.dt.float32r
I32 = mybir.dt.int32
I8 = mybir.dt.int8
ALU = mybir.AluOpType
ACT = mybir.ActivationFunctionType
AX = mybir.AxisListType.X

P = 128
D = 2048
KD = D // P
T = 256
HEADS = 4
DK, DV = 128, 256
FF = 5504
KF = FF // P
EPS = 1e-6
NEG = -1e30
GRID_W = 64
GRID_H = T // GRID_W
WINDOWS = (2, 4, 8, 16)
POOL = 4096
NH = 16
SM_SCALE = (128 + 64) ** -0.5
LEVELS = (128, 64, 32, 16, 8, 4, 2, 1)
BLOCKS = 16
SLOT = BLOCKS * P
RING, PAIR = 4, 2

PHASES = [("mod", 96, 0), ("lr", 1, 1), ("key", 8, 8), ("value", 16, 16), ("query", 8, 8),
          ("gate", 16, 16), ("mix_out", 16, 16), ("up", 2 * KF, 2 * KF), ("down", KF, 0),
          ("pool_in", 64, 64), ("group", 16, 16), ("pool_out", 32, 0), ("proj0", 2, 2),
          ("plegate0", 16, 16), ("mla_in", 26, 26), ("uq", 6, 6), ("uk", 4, 4), ("uv", 4, 4),
          ("mla_out", 16, 16), ("proj1", 2, 2), ("plegate1", 16, 16)]
BASE, COUNT, EVAC = {}, {}, {}
_s = _e = 0
for _n, _c, _v in PHASES:
    BASE[_n], COUNT[_n], EVAC[_n] = _s, _c, _e
    _s, _e = _s + _c, _e + _v
SLOTS = _s

VEC, _w = {}, 0
for _n, _c in [("c2", 2 * KD), ("b_mod", 96), ("g1", 16), ("g2", 16), ("gfin", 16), ("conv_w", 9 * KF),
               ("conv_b", KF), ("lr_b", 8), ("gla_g", 2), ("ml_g", 2), ("pre0", 16), ("pre1", 16),
               ("post0", 16), ("post1", 16), ("pscale", 32), ("ple0", 16), ("ple1", 16),
               ("q_norm", 4), ("kv_norm", 4), ("gate_b", 2), ("eps", 1), ("invf", 1), ("halfpi", 1),
               ("corr", 64)]:
    VEC[_n] = _w
    _w += _c
NVEC = _w

KB = 1024

TWO_PI = (6.28125, 0.00193500518798828125, float(2 * np.pi - 6.28125 - 0.00193500518798828125))


SHARED = {
    "sum": [(n, 1) for n in ("n1", "n2", "nf", "np", "post0", "ple0", "m", "q", "kv", "post1", "ple1")],
    "root": [(n, 1) for n in ("n1", "n2", "nf", "np", "post0", "ple0", "m", "q", "kv", "post1", "ple1")],
    "ssq": [("n1", 2)] + [(n, 1) for n in ("nf", "np", "post0", "ple0", "ple1")],
    "part": [(n, 4) for n in ("nf", "np", "ple0", "ple1")],
    "squares": [("n1", 2), ("nf", 4), ("np", 4), ("post0", 8), ("ple0", 4), ("ple1", 4)],
    "steps": [("n2", 32), ("m", 32), ("q", 8), ("kv", 8), ("post1", 32)],
}
for _k in ("made", "hi", "x"):
    SHARED[_k] = [("x1", 8), ("y", 4), ("n2", 4), ("np", 4), ("ple0", 4), ("m", 4), ("lat", 2), ("ple1", 4)]


def reached(kind, name, n=0):
    names = [a for a, _ in SHARED[kind]]
    return sum(c for _, c in SHARED[kind][:names.index(name)]) + n


class Steps:

    def __init__(self, eng, sem, base=0):
        self.eng, self.sem, self.base, self.n = eng, sem, base, 0

    def start(self):
        self.eng.wait_ge(self.sem, self.base)

    def done(self, ins):
        ins.then_inc(self.sem, 1)
        self.n += 1

    def wait(self):
        if self.n:
            self.eng.wait_ge(self.sem, self.base + self.n)


def turns(eng, n, tail=0):
    q = max((n - tail) // RING, 0)
    if q > 1:
        with eng.Fori(0, q) as i:
            for r in range(RING):
                yield i, r
    else:
        q = 0
    for j in range(RING * q, n):
        yield j // RING, j % RING


def build(nc, A, out):
    with ExitStack() as ctx:
        sems = {}

        def sem(name):
            if name not in sems:
                sems[name] = ctx.enter_context(nc.semaphore(name))
            return sems[name]

        arena0 = (nc.sbuf_base + 63) // 64 * 64
        ctx.enter_context(nc.sbuf_tensor("arena", [P, (nc.sbuf_usable_end - arena0 - 64) // 4], F32))

        def at(name, cols, kb, dt=F32, rows=P):
            return nc.alloc_sbuf_tensor_at(name, [rows, cols], dt, offset=arena0 + int(kb * KB))

        RAW = [at(f"raw{i}", SLOT, 8 * i) for i in range(RING)]
        HI = [at(f"hi{i}", SLOT, 32 + 8 * i, F32R) for i in range(PAIR)]
        LO = [at(f"lo{i}", SLOT, 48 + 8 * i, F32R) for i in range(PAIR)]
        vec = at("vec", NVEC, 64)
        mods = at("mods", 192, 67.5)
        eye = at("eye", P, 68.25)
        ones = at("ones", P, 68.75)
        ssq = at("ssq", T, 69.25)
        rs = at("rs", T, 70.25)
        amod = at("amod", 3 * KD, 71.25)
        ch = at("ch", 2 * KD, 71.5, F32R)
        cl = at("cl", 2 * KD, 71.625, F32R)
        csil = at("csil", 2 * KD, 71.75)
        W0 = 72
        wk = lambda name, cols, kb, dt=F32, rows=P: at(name, cols, W0 + kb, dt, rows)
        xh, xl = wk("xh", 2 * KD * T, 0, F32R), wk("xl", 2 * KD * T, 32, F32R)
        xf = wk("xf", 2 * KD * T, 64)
        sq = [wk("sq0", KD * T, 96), wk("sq1", KD * T, 112)]
        rsx = wk("rsx", 2 * T, 128)
        ssqx = wk("ssqx", 2 * T, 130)
        K = wk("K", 2 * 8 * T, 64)
        V = wk("V", 4 * 2048, 80)
        zlr = wk("zlr", 2 * T, 112)
        Q = wk("Q", 8 * T, 114)
        gates = wk("gates", 16 * T, 16)
        loga = wk("loga", 8 * 2 * T, 122)
        softp = wk("softp", 8 * 2 * T, 32)
        cumx = wk("cumx", 8 * T, 0)
        cumc = wk("cumc", 8 * T, 8)
        dec = [wk("dec0", 4 * T, 32), wk("dec1", 4 * T, 36)]
        qk = [wk("qk0", 4 * T, 40), wk("qk1", 4 * T, 44)]
        w_lr = wk("w_lr", 8 * P, 138, rows=16)
        att = [wk("att0", 8 * P, 48), wk("att1", 8 * P, 52)]
        cross = [wk("cross0", 4 * P, 56), wk("cross1", 4 * P, 58)]
        kend = wk("kend", 4 * T, 60)
        kend_t = wk("kend_t", 2 * 4 * P, 122)
        state = [wk("state0", 4 * DV, 126), wk("state1", 4 * DV, 130)]
        qb = [wk("qb0", 4 * T, 134), wk("qb1", 4 * T, 138)]
        rep_sel = wk("rep_sel", 8 * P, 142, rows=64)
        lvl_words = wk("lvl_words", 2 * 7 * P // 4, 146, I32)
        lvl = lvl_words[:, :].bitcast(I8)
        sel_if = wk("sel_if", P, 148, rows=32)
        osq = wk("osq", 8 * T, 32)
        rgrp = wk("rgrp", 4 * T, 40)
        yf = wk("yf", 16 * T, 48)
        neg_g = wk("neg_g", 8 * T, 0)
        em = wk("em", 8 * T, 8)
        maskn = wk("maskn", 4 * T, 32)
        wgt = [wk("wgt0", 4 * T, 36), wk("wgt1", 4 * T, 40)]
        ri = wk("ri", 2 * T, 122, rows=64)
        rf = wk("rf", 2 * T, 124, rows=64)
        rl = wk("rl", 2 * T, 126, rows=64)
        rg = wk("rg", 2 * T, 128, rows=64)
        rm = wk("rm", 2 * T, 130, rows=64)
        gtok = wk("gtok", 4 * 64, 132)
        rden = [wk("rden0", T, 44), wk("rden1", T, 45)]
        tmpo = wk("tmpo", 2 * T, 46)
        omix = wk("omix", 8 * T, 122)
        yh, yl = wk("yh", 16 * T, 64, F32R), wk("yl", 16 * T, 80, F32R)
        R = wk("R", KD * T, 134)
        tmpx = wk("tmpx", T, 118)
        tn = wk("tn", KD * T, 118)
        x2h, x2l = wk("x2h", KD * T, 86, F32R), wk("x2l", KD * T, 102, F32R)
        hh, hl = wk("hh", KF * T, 0, F32R), wk("hl", KF * T, 43, F32R)
        pad = [wk("pad0", 6 * 66, 118), wk("pad1", 6 * 66, 120)]
        acc = [wk("acc0", T, 122), wk("acc1", T, 123)]
        sil = [wk("sil0", T, 124), wk("sil1", T, 125)]
        ht = [wk("ht0", T, 126), wk("ht1", T, 127)]
        UPW = 16 + T
        pnt = wk("pnt", KD * T, 64)
        xph, xpl = wk("xph", KD * T, 96, F32R), wk("xpl", KD * T, 112, F32R)
        ph, pl = wk("ph", 32 * T, 0, F32R), wk("pl", 32 * T, 32, F32R)
        sg = wk("sg", 32 * T, 64)
        y2h, y2l = wk("y2h", 32 * T, 64, F32R), wk("y2l", 32 * T, 96, F32R)
        up = [wk("up0", UPW, 128), wk("up1", UPW, 129.0625)]
        ws = [wk("ws0", UPW, 130.125), wk("ws1", UPW, 131.1875)]
        pf = wk("pf", T, 132.25)
        gt = [wk("gt0", 2 * T, 128), wk("gt1", 2 * T, 130)]
        O = wk("O", KD * T, 0)
        ot = wk("ot", KD * T, 16)
        pj0 = wk("pj0", KD * T, 32)
        pth0, ptl0, ptr0 = wk("pth0", 2 * T, 48, F32R), wk("ptl0", 2 * T, 50, F32R), wk("ptr0", 2 * T, 52)
        gxh, gxl = wk("gxh", KD * T, 64, F32R), wk("gxl", KD * T, 80, F32R)
        sgt = [wk("sgt0", T, 54), wk("sgt1", T, 55)]
        mnt = wk("mnt", KD * T, 0)
        xmh, xml = wk("xmh", KD * T, 96, F32R), wk("xml", KD * T, 112, F32R)
        ql = wk("ql", 8 * T, 16)
        kpr = wk("kpr", 2 * T, 24)
        kp = wk("kp", 2 * T, 26)
        cs = wk("cs", 2 * T, 28)
        sg2 = wk("sg2", 16 * T, 32)
        lath, latl = wk("lath", 8 * T, 48, F32R), wk("latl", 8 * T, 56, F32R)
        ssqk = wk("ssqk", T, 30)
        rsk = wk("rsk", T, 31)
        qn = wk("qn", 16 * T, 64)
        qp = wk("qp", 8 * T, 16)
        rt = [wk(f"rt{i}", T, 128 + i) for i in range(4)]
        qraw = wk("qraw", 4 * T, 0)
        kn = wk("kn", 16 * T, 96)
        v2 = wk("v2", 2 * 2048, 112)
        tmpq = wk("tmpq", T, 30)
        tmpg = wk("tmpg", T, 53)
        s_ = [wk("s0", 384, 0), wk("s1", 384, 1.5)]
        p_ = [wk("p0", 384, 3), wk("p1", 384, 4.5)]
        pt = [wk("pt0", 384, 6), wk("pt1", 384, 7.5)]
        maska = wk("maska", 384, 9)
        yt = [wk("yt0", T, 11), wk("yt1", T, 12)]
        stat = wk("stat", 16 * 8, 13)
        y3h, y3l = wk("y3h", 16 * T, 48, F32R), wk("y3l", 16 * T, 80, F32R)
        pj1 = wk("pj1", KD * T, 16)
        ot1 = wk("ot1", KD * T, 32)
        fxh, fxl = wk("fxh", KD * T, 96, F32R), wk("fxl", KD * T, 112, F32R)
        pth1, ptl1, ptr1 = wk("pth1", 2 * T, 128, F32R), wk("ptl1", 2 * T, 130, F32R), wk("ptr1", 2 * T, 132)
        post = wk("post", T, 86, I32)
        ang = [wk(f"ang{i}", T, 87 + i) for i in range(4)]

        PS = [ctx.enter_context(nc.psum_tensor(f"ps{i}", [P, 512], F32)) for i in range(8)]

        raw_loaded = [sem(f"raw_loaded{i}") for i in range(RING)]
        hi_ready, lo_ready = sem("hi_ready"), sem("lo_ready")
        slot_used = sem("slot_used")
        evacuated = sem("evacuated")

        def v(name, j=0, n=1):
            return vec[:, bass.ds(VEC[name] + j, n)] if not isinstance(j, int) else \
                vec[:, VEC[name] + j:VEC[name] + j + n]

        def blk(t, j, n=1):
            return t[:, bass.ds(j * T, n * T)] if not isinstance(j, int) else t[:, j * T:(j + n) * T]

        def where(phase, i, r):
            return BASE[phase] + RING * i + r

        block = ctx.enter_context(nc.Block())

        @block.sync
        def _(sp):
            def load(s, i, r):
                if not isinstance(s, int) or s >= RING:
                    sp.wait_ge(lo_ready, 2 * s - 2 * RING + 2)
                sp.dma_start(RAW[r][:, :], A["weights"][bass.ds(s, 1)].rearrange("a p n -> (a p) n")
                             if not isinstance(s, int) else A["weights"][s]).then_inc(raw_loaded[r], 16)
            for r in range(RING):
                load(r, 0, r)
            turns_ = SLOTS // RING
            with sp.Fori(1, turns_) as i:
                for r in range(RING):
                    load(i * RING + r, i, r)
            for s in range(turns_ * RING, SLOTS):
                load(s, 0, s % RING)
            sp.wait_ge(sem("gate1_used"), 1 + KD)
            sp.dma_start(out, R[:, :]).then_inc(sem("stored"), 16)
            sp.wait_ge(sem("stored"), 16)

        @block.scalar
        def _(act):
            def split(phase, i, r, ahead=2):
                t = where(phase, i, r) + ahead
                if isinstance(t, int) and t >= SLOTS:
                    return
                p = BASE[phase] + r + ahead
                act.wait_ge(raw_loaded[p % RING], 16 * (i + p // RING + 1))
                if not isinstance(t, int) or t >= 2:
                    act.wait_ge(slot_used, t - 1)
                for h in range(2):
                    c = slice(h * SLOT // 2, (h + 1) * SLOT // 2)
                    act.activation(HI[p % PAIR][:, c], RAW[p % RING][:, c], ACT.Copy).then_inc(hi_ready, 1)

            def round_hi(name, dst, src, quads=4):
                for q in range(quads):
                    act.wait_ge(sem("operand_made"), reached("made", name, q + 1))
                    act.activation(blk(dst, 4 * q, 4), blk(src, 4 * q, 4), ACT.Copy).then_inc(sem("operand_hi"), 1)

            def root(name, dst, src, n):
                act.wait_ge(sem("norm_sum"), reached("sum", name, 1))
                act.activation(dst, src, ACT.Sqrt, bias=v("eps"), scale=1.0 / n).then_inc(sem("norm_root"), 1)

            def square(name, dst, src, quads=4):
                for q in range(quads):
                    act.wait_ge(sem("part_ready"), reached("part", name, q + 1))
                    act.activation(blk(dst, 4 * q, 4), blk(src, 4 * q, 4), ACT.Square).then_inc(sem("squares_ready"), 1)

            act.dma_start(vec[:, :], A["vec"]).then_inc(sem("vec_loaded"), 16)
            act.dma_start(eye[:, :], A["eye"]).then_inc(sem("eye_loaded"), 16)
            act.dma_start(xf[:, :], A["xt"]).then_inc(sem("x_loaded"), 16)
            for dst, name in ((lvl_words, "lvl"), (rep_sel, "rep_sel"), (sel_if, "sel_if"), (w_lr, "w_lr")):
                act.dma_start(dst[:, :], A[name]).then_inc(sem("tables_loaded"), 16)
            act.wait_ge(sem("vec_loaded"), 16)
            act.activation(csil[:, :], v("c2", 0, 2 * KD), ACT.Silu).then_inc(sem("c_act"), 1)
            act.wait_ge(sem("c_act"), 1)
            act.activation(ch[:, :], csil[:, :], ACT.Copy).then_inc(sem("c_hi"), 1)
            split("mod", 0, -2)
            split("mod", 0, -1)
            act.wait_ge(sem("x_loaded"), 16)
            for s in range(2):
                act.activation(sq[s][:, :], blk(xf, KD * s, KD), ACT.Square).then_inc(sem("squares_ready"), 1)
            root("n1", rsx[:, :], PS[2][:, :], D)
            for i, r in turns(act, 96):
                split("mod", i, r)
            round_hi("x1", xh, xf, 8)

            split("lr", 0, 0)
            act.wait_ge(slot_used, BASE["lr"] + 1)
            act.activation(zlr[:, :], PS[0][:, :], ACT.Copy).then_inc(evacuated, 1)
            kview = K[:, :].rearrange("p (s b t) -> p s b t", s=2, b=8)
            for half, scale in ((0, 1.0), (1, DK ** -0.5)):
                for r in range(4):
                    b = 4 * half + r
                    split("key", half, r)
                    act.wait_ge(slot_used, BASE["key"] + b + 1)
                    act.activation(kview[:, :, b, :], PS[b % 2][:, :].rearrange("p (s t) -> p s t", s=2),
                                   ACT.Copy, scale=scale).then_inc(evacuated, 1)
            with act.Fori(0, 2) as i:
                for r in range(8):
                    split("value", 2 * i, r)
                    if r % 4 == 3:
                        act.wait_ge(slot_used, BASE["value"] + 8 * i + r + 1)
                        for tt in range(4):
                            act.activation(V[:, bass.ds(i * 1024 + (tt * 2048 + (r // 4) * 512), 512)],
                                           PS[4 * (r // 4) + tt][:, :], ACT.Copy).then_inc(evacuated, 1)
            for half, scale in ((0, DK ** -0.5), (1, 1.0)):
                for r in range(4):
                    b = 4 * half + r
                    split("query", half, r)
                    act.wait_ge(slot_used, BASE["query"] + b + 1)
                    act.activation(blk(Q, b), PS[b % 2][:, 0:T], ACT.Copy, scale=scale).then_inc(evacuated, 1)
            for half, func in ((0, ACT.Silu), (1, ACT.Sigmoid)):
                with act.Fori(2 * half, 2 * half + 2) as i:
                    for r in range(4):
                        split("gate", i, r)
                        act.wait_ge(slot_used, where("gate", i, r) + 1)
                        act.activation(blk(gates, 4 * i + r), PS[r % 2][:, 0:T], func).then_inc(evacuated, 1)

            act.wait_ge(sem("dec_abs"), 1)
            act.activation(softp[:, :], softp[:, :], ACT.Exp, scale=-1.0).then_inc(sem("dec_exp"), 1)
            act.wait_ge(sem("dec_exp"), 1)
            act.activation(softp[:, :], softp[:, :], ACT.Ln, bias=1.0).then_inc(sem("dec_ln"), 1)
            for d in range(2):
                act.wait_ge(sem("kend_arg"), d + 1)
                act.activation(dec[0][:, :], dec[0][:, :], ACT.Exp, scale=1 / 16.0).then_inc(sem("kend_exp"), 1)
                if d:
                    act.wait_ge(sem("qb_ready"), d)
                act.activation(dec[1][:, :], blk(cumx, 4 * d, 4), ACT.Exp, scale=1 / 16.0).then_inc(sem("qb_exp"), 1)
                for t in range(2):
                    act.wait_ge(sem("kend_turned"), 2 * d + t + 1)
                    act.activation(kend_t[:, t * 512:(t + 1) * 512], PS[t][:, :], ACT.Copy).then_inc(sem("kend_t_ready"), 1)
                for g in range(2):
                    act.wait_ge(sem("state_done"), 2 * d + g + 1)
                    act.activation(state[d][:, g * 512:(g + 1) * 512], PS[2 + g][:, :], ACT.Copy).then_inc(sem("state_ready"), 1)
            NL = len(LEVELS)
            for n in range(2 * NL):
                act.wait_ge(sem("lvl_arg"), n + 1)
                act.activation(dec[n % 2][:, :], dec[n % 2][:, :], ACT.Exp, scale=1 / 16.0).then_inc(sem("lvl_exp"), 1)
                if n % NL == 0:
                    act.wait_ge(sem("lvl_scores"), n + 1)
                    act.activation(cross[n // NL][:, :], PS[4][:, :], ACT.Copy).then_inc(sem("cross_ready"), 1)
            for h in range(HEADS):
                act.wait_ge(sem("gla_out"), h + 1)
                act.activation(blk(osq, 2 * h, 2), PS[h][:, :], ACT.Square).then_inc(sem("gla_sq"), 1)
            for g in range(2):
                act.wait_ge(sem("gla_sum"), g + 1)
                act.activation(rgrp[:, g * 512:(g + 1) * 512], PS[4 + g][:, :], ACT.Sqrt, bias=v("eps"),
                               scale=1.0 / DV).then_inc(sem("gla_root"), 1)

            act.wait_ge(sem("operand_made"), reached("made", "y", 2))
            act.dma_start(maskn[:, :], A["maskn"]).then_inc(sem("maskn_loaded"), 16)
            act.wait_ge(sem("f_abs"), 1)
            act.activation(rl[:, :], rl[:, :], ACT.Exp, scale=-1.0).then_inc(sem("f_exp"), 1)
            act.wait_ge(sem("f_exp"), 1)
            act.activation(rl[:, :], rl[:, :], ACT.Ln, bias=1.0).then_inc(sem("f_ln"), 1)
            act.wait_ge(sem("m_rows"), 1)
            act.activation(rm[:, 0:T], rm[:, 0:T], ACT.Exp, scale=-1.0).then_inc(sem("em_rows"), 1)
            for n in range(4):
                act.wait_ge(sem("neg_g_rep"), n + 1)
                act.activation(neg_g[:, n * 512:(n + 1) * 512], PS[n][:, :], ACT.Copy).then_inc(sem("neg_g_ready"), 1)
            for n in range(4):
                act.wait_ge(sem("em_rep"), n + 1)
                act.activation(em[:, n * 512:(n + 1) * 512], PS[4 + n][:, :], ACT.Copy).then_inc(sem("em_ready"), 1)
            act.wait_ge(sem("g_turned"), 1)
            act.activation(gtok[:, :], PS[0][:, 0:256], ACT.Copy).then_inc(sem("gtok_ready"), 1)
            act.wait_ge(sem("gtok_ready"), 1)
            act.dma_start(R[:, :], A["xt"][:, 0:KD * T]).then_inc(sem("R_loaded"), 16)
            for n in range(9):
                h, d = n // 2, n % 2
                if n < 8:
                    W = wgt[n % 2]
                    if n >= 2:
                        act.wait_ge(sem("ml_done"), n - 1)
                    for t in range(2, 4):
                        c = t * 64 + 32 * d + h
                        act.activation(W[:, t * T:(t + 1) * T], blk(neg_g, 4 * d + h), ACT.Exp,
                                       bias=gtok[:, c:c + 1]).then_inc(sem("w_ctx"), 1)
                    act.wait_ge(sem("w_arg"), n + 1)
                    act.activation(W[:, 0:2 * T], W[:, 0:2 * T], ACT.Exp).then_inc(sem("w_x"), 1)
                if n >= 2 and d == 0:
                    act.wait_ge(sem("ml_h"), h)
                    act.activation(tmpo[:, :], blk(omix, 2 * h - 2, 2), ACT.Square).then_inc(sem("ml_sq"), 1)
                    act.wait_ge(sem("ml_sum"), h)
                    act.activation(rden[(h - 1) % 2][:, :], PS[7][:, 0:T], ACT.Sqrt, bias=v("eps"),
                                   scale=1.0 / DV).then_inc(sem("ml_root"), 1)
            act.wait_ge(sem("ml_done"), 8)
            round_hi("y", yh, yf)

            for i, r in turns(act, 16):
                split("mix_out", i, r)
            root("n2", rs[:, :], PS[2][:, 0:T], D)
            round_hi("n2", x2h, tn)
            for i, r in turns(act, 2 * KF):
                split("up", i, r)
                j, b = 2 * i + r // 2, (r // 2) % 2
                if r % 2 == 0:
                    act.wait_ge(slot_used, where("up", i, r) + 1)
                    if r == 0:
                        act.wait_ge(sem("pads_zeroed"), 1)
                    act.wait_ge(sem("conv"), 9 * j)
                    act.activation(pad[b][:, :].rearrange("p (y x) -> p y x", x=66)[:, 1:1 + GRID_H, 1:1 + GRID_W],
                                   PS[r % 2][:, 0:T].rearrange("p (y x) -> p y x", x=GRID_W), ACT.Copy).then_inc(evacuated, 1)
                else:
                    act.wait_ge(sem("conv"), 9 * j + 9)
                    act.activation(sil[b][:, :], acc[b][:, :], ACT.Silu, bias=v("conv_b", j)).then_inc(sem("ff_silu"), 1)
                    act.wait_ge(evacuated, EVAC["up"] + 2 * j + 2)
                    act.activation(blk(hh, j), ht[b][:, :], ACT.Copy).then_inc(sem("ff_hi"), 1)
            for i, r in turns(act, KF):
                split("down", i, r)
            square("nf", tn, R)
            root("nf", rs[:, :], PS[2][:, 0:T], D)
            square("np", tn, R)
            root("np", rs[:, :], PS[2][:, 0:T], D)
            round_hi("np", xph, pnt)

            for g in range(4):
                with act.Fori(2 * g, 2 * g + 2) as i:
                    for r in range(4):
                        split("pool_in", i, r)
                        u = 4 * i + r
                        act.wait_ge(slot_used, where("pool_in", i, r) + 1)
                        if g == 0 and r == 0:
                            act.wait_ge(sem("ups_zeroed"), 1)
                        act.activation(up[r % 2][:, 16:UPW], PS[r % 2][:, 0:T], ACT.Copy).then_inc(evacuated, 1)
                        act.wait_ge(sem("pool_made"), u + 1)
                        act.activation(blk(ph, u), pf[:, :], ACT.Copy).then_inc(sem("pool_hi"), 1)
            with act.Fori(8, 16) as i:
                for r in range(4):
                    split("pool_in", i, r)
                    act.wait_ge(slot_used, where("pool_in", i, r) + 1)
                    act.activation(blk(sg, 4 * i + (r - 32)), PS[r % 2][:, 0:T], ACT.Silu).then_inc(evacuated, 1)
            for i, r in turns(act, 16):
                split("group", i, r)
                s = 4 * i + r
                act.wait_ge(evacuated, EVAC["group"] + s + 1)
                act.activation(blk(y2h, 2 * s, 2), gt[r % 2][:, :], ACT.Copy).then_inc(sem("y2_hi"), 1)
            for i, r in turns(act, 32):
                split("pool_out", i, r)
            for b in range(8):
                act.wait_ge(sem("O_copied"), b + 1)
                act.activation(blk(ot, 2 * b, 2), blk(O, 2 * b, 2), ACT.Square).then_inc(sem("squares_ready"), 1)

            def p_operand(tag, ptr, pth):
                act.dma_start(ptr[:, :], A["pt"][:, tag * 2 * T:(tag + 1) * 2 * T]).then_inc(sem(f"p{tag}_loaded"), 16)
                act.wait_ge(sem(f"p{tag}_loaded"), 16)
                act.activation(pth[:, :], ptr[:, :], ACT.Copy).then_inc(sem(f"p{tag}_hi"), 1)

            def proj(tag, pj):
                for s in range(2):
                    split(f"proj{tag}", 0, s)
                    act.wait_ge(slot_used, BASE[f"proj{tag}"] + s + 1)
                    for b in range(4):
                        ins = act.activation(blk(pj, 8 * s + 2 * b, 2), PS[4 + b][:, :], ACT.Copy)
                    ins.then_inc(evacuated, 1)

            def gate(tag, tail=0):
                name = f"plegate{tag}"
                for i, r in turns(act, 16, tail):
                    split(name, i, r)
                    act.wait_ge(slot_used, where(name, i, r) + 1)
                    act.wait_ge(sem(f"gate{tag}_used"), 4 * i + r)
                    act.activation(sgt[r % 2][:, :], PS[r % 2][:, 0:T], ACT.Sigmoid).then_inc(evacuated, 1)

            p_operand(0, ptr0, pth0)
            proj(0, pj0)
            root("post0", rs[:, :], PS[2][:, 0:T], D)
            square("ple0", ot, R)
            root("ple0", rs[:, :], PS[2][:, 0:T], D)
            round_hi("ple0", gxh, ot)
            gate(0)

            act.dma_start(post[:, :], A["pos"]).then_inc(sem("pos_loaded"), 16)
            root("m", rs[:, :], PS[2][:, 0:T], D)
            round_hi("m", xmh, mnt)
            act.wait_ge(sem("ang_ready"), 1)
            act.activation(cs[:, T:2 * T], ang[0][:, :], ACT.Sin).then_inc(sem("rope_cs"), 1)
            act.activation(cs[:, 0:T], ang[1][:, :], ACT.Sin, bias=v("halfpi"), scale=-1.0).then_inc(sem("rope_cs"), 1)
            for j in range(10):
                split("mla_in", j // 4, j % 4)
                act.wait_ge(slot_used, BASE["mla_in"] + j + 1)
                act.activation(blk(ql, j) if j < 8 else blk(kpr, j - 8), PS[j % 2][:, 0:T], ACT.Copy).then_inc(evacuated, 1)
            for j in range(10, 26):
                split("mla_in", j // 4, j % 4)
                act.wait_ge(slot_used, BASE["mla_in"] + j + 1)
                act.activation(blk(sg2, j - 10), PS[j % 2][:, 0:T], ACT.Silu).then_inc(evacuated, 1)
            root("q", rs[:, :], PS[2][:, 0:T], 512)
            root("kv", rsk[:, :], PS[3][:, 0:T], 512)
            round_hi("lat", lath, ql, 2)
            for s in range(6):
                split("uq", s // 4, s % 4)
                act.wait_ge(slot_used, BASE["uq"] + s + 1)
                if s == 5:
                    act.wait_ge(sem("q_rot"), 1)
                for b in range(2):
                    dst = blk(qn, 4 * s + 2 * b, 2) if s < 4 else blk(qraw, 2 * b, 2)
                    ins = act.activation(dst, PS[2 * (s % 2) + b][:, :], ACT.Copy)
                ins.then_inc(evacuated, 1)
            for s in range(4):
                split("uk", 0, s)
                act.wait_ge(slot_used, BASE["uk"] + s + 1)
                for b in range(2):
                    ins = act.activation(blk(kn, 4 * s + 2 * b, 2), PS[2 * (s % 2) + b][:, :], ACT.Copy)
                ins.then_inc(evacuated, 1)
            for s in range(4):
                split("uv", 0, s)
                act.wait_ge(slot_used, BASE["uv"] + s + 1)
                for t in range(2):
                    ins = act.activation(v2[:, t * 2048 + s * 512:t * 2048 + (s + 1) * 512], PS[2 * (s % 2) + t][:, :], ACT.Copy)
                ins.then_inc(evacuated, 1)
            act.dma_start(maska[:, :], A["maska"]).then_inc(sem("maska_loaded"), 16)
            for n in range(NH + 2):
                if n < NH:
                    b = n % 2
                    act.wait_ge(sem("s_max"), n + 1)
                    if n >= 2:
                        act.wait_ge(sem("p_turned"), n - 1)
                    for t, c in ((0, slice(0, P)), (1, slice(P, 3 * P))):
                        act.activation(p_[b][:, c], s_[b][:, c], ACT.Exp, bias=stat[:, 8 * n + t:8 * n + t + 1],
                                       scale=SM_SCALE, accum_out=stat[:, 8 * n + 2 + t:8 * n + 3 + t]).then_inc(sem("p_exp"), 1)
                if 1 <= n <= NH:
                    h = n - 1
                    act.wait_ge(sem("p_turned"), h + 1)
                    if h >= 2:
                        act.wait_ge(sem("pv_done"), h - 1)
                    act.activation(pt[h % 2][:, :], PS[4 + h % 2][:, 0:3 * P], ACT.Copy).then_inc(sem("pt_ready"), 1)
                if n >= 2:
                    h = n - 2
                    act.wait_ge(sem("o_made"), h + 1)
                    act.activation(blk(y3h, h), yt[h % 2][:, :], ACT.Copy).then_inc(sem("y3_hi"), 1)
            for i, r in turns(act, 16):
                split("mla_out", i, r)
                act.wait_ge(slot_used, where("mla_out", i, r) + 1)
                act.activation(blk(O, 4 * i + r), PS[r % 2][:, 0:T], ACT.Copy).then_inc(evacuated, 1)
            p_operand(1, ptr1, pth1)
            proj(1, pj1)
            root("post1", rs[:, :], PS[2][:, 0:T], D)
            square("ple1", ot1, R)
            root("ple1", rs[:, :], PS[2][:, 0:T], D)
            round_hi("ple1", fxh, ot1)
            gate(1, tail=4)

        @block.vector
        def _(dve):
            own = Steps(dve, sem("vector_steps"))

            def split(phase, i, r, ahead=2):
                t = where(phase, i, r) + ahead
                if isinstance(t, int) and t >= SLOTS:
                    return
                p = BASE[phase] + r + ahead
                for h in range(2):
                    c = slice(h * SLOT // 2, (h + 1) * SLOT // 2)
                    dve.wait_ge(hi_ready, 2 * t + h + 1)
                    dve.tensor_tensor(LO[p % PAIR][:, c], RAW[p % RING][:, c], HI[p % PAIR][:, c].bitcast(F32),
                                      ALU.subtract).then_inc(lo_ready, 1)

            def recip(name, dst):
                dve.wait_ge(sem("norm_root"), reached("root", name, 1))
                own.done(dve.reciprocal(dst, dst))
                own.wait()

            def rest(name, q, hi, lo, src):
                dve.wait_ge(sem("operand_hi"), reached("hi", name, q + 1))
                dve.tensor_tensor(blk(lo, 4 * q, 4), blk(src, 4 * q, 4), blk(hi, 4 * q, 4).bitcast(F32),
                                  ALU.subtract).then_inc(sem("operand_rest"), 1)

            def normed(name, src, gain, dst, hi, lo, inv=None, shift=None, quads=4):
                for q in range(quads + 1):
                    if q < quads:
                        for b in range(4 * q, 4 * q + 4):
                            ins = dve.scalar_tensor_tensor(blk(dst, b), blk(src, b), gain(b),
                                                           (inv(b) if inv else rs)[:, :], ALU.mult, ALU.mult)
                            if shift:
                                own.done(ins)
                        if shift:
                            own.wait()
                            for b in range(4 * q, 4 * q + 4):
                                ins = dve.tensor_scalar(blk(dst, b), blk(dst, b), shift(b), None, ALU.add)
                        ins.then_inc(sem("operand_made"), 1)
                    if q:
                        rest(name, q - 1, hi, lo, dst)

            def accumulate(st, src, tmp, total=ssq):
                st.start()
                st.done(dve.tensor_tensor(tmp[:, :], src, src, ALU.mult))
                st.wait()
                st.done(dve.tensor_tensor(total[:, :], total[:, :], tmp[:, :], ALU.add))

            def add_squares(name, src, count=4):
                dve.wait_ge(sem("squares_ready"), reached("squares", name, count))
                dve.tensor_reduce(ssq[:, :], src[:, 0:KD * T].rearrange("p (k t) -> p t k", t=T), AX,
                                  ALU.add).then_inc(sem("ssq_ready"), 1)

            def clear_ssq():
                own.done(dve.memset(ssq[:, :], 0.0))
                own.wait()

            dve.memset(ones[:, :], 1.0).then_inc(sem("ones_ready"), 1)
            dve.wait_ge(sem("c_hi"), 1)
            dve.tensor_tensor(cl[:, :], csil[:, :], ch[:, :].bitcast(F32), ALU.subtract).then_inc(sem("c_lo"), 1)
            split("mod", 0, -2)
            split("mod", 0, -1)
            for s in range(2):
                dve.wait_ge(sem("squares_ready"), reached("squares", "n1", s + 1))
                dve.tensor_reduce(ssqx[:, s * T:(s + 1) * T], sq[s][:, :].rearrange("p (k t) -> p t k", t=T), AX,
                                  ALU.add).then_inc(sem("ssq_ready"), 1)
            recip("n1", rsx[:, :])
            for s in range(2):
                xs = blk(xf, KD * s, KD).rearrange("p (k t) -> p k t", t=T)
                own.done(dve.tensor_tensor(xs, xs, rsx[:, s * T:(s + 1) * T][:, None, :].to_broadcast([P, KD, T]), ALU.mult))
            for i, r in turns(dve, 96):
                split("mod", i, r)
            mview = mods[:, :].rearrange("p (j s) -> p j s", s=2)
            dve.wait_ge(slot_used, 96)
            own.done(dve.tensor_tensor(mview, PS[0][:, 0:192].rearrange("p (j s) -> p j s", s=2),
                                       v("b_mod", 0, 96)[:, :, None].to_broadcast([P, 96, 2]), ALU.add))
            own.wait()
            for n, (j, s, g) in enumerate([(16, 0, "g1"), (16, 1, "g1"), (64, 0, "g2")]):
                own.done(dve.scalar_tensor_tensor(amod[:, n * KD:(n + 1) * KD], mview[:, j:j + KD, s], 1.0,
                                                  v(g, 0, KD), ALU.add, ALU.mult))
            own.wait()
            for q in range(9):
                if q < 8:
                    for b in range(4 * q, 4 * q + 4):
                        s, k = b // KD, b % KD
                        ins = dve.tensor_scalar(blk(xf, b), blk(xf, b), amod[:, s * KD + k:s * KD + k + 1],
                                                mview[:, k, s:s + 1], ALU.mult, ALU.add)
                    ins.then_inc(sem("operand_made"), 1)
                if q:
                    rest("x1", q - 1, xh, xl, xf)
            for name in ("lr", "key", "value", "query", "gate"):
                for i, r in turns(dve, COUNT[name]):
                    split(name, i, r)

            for n in range(8):
                dve.wait_ge(sem("dec_z"), n + 1)
                own.done(dve.tensor_scalar(loga[:, n * 512:(n + 1) * 512], PS[n][:, :], v("lr_b", n), None, ALU.add))
            own.wait()
            dve.scalar_tensor_tensor(softp[:, :], loga[:, :], -1.0, loga[:, :], ALU.mult, ALU.max).then_inc(sem("dec_abs"), 1)
            dve.wait_ge(sem("dec_ln"), 1)
            own.done(dve.scalar_tensor_tensor(loga[:, :], loga[:, :], 0.0, softp[:, :], ALU.min, ALU.subtract))
            own.wait()
            for n in range(8):
                step = 1 if n < 4 else -1
                for s, dst in ((0, cumx), (1, cumc)):
                    src = loga[:, n * 512 + s * T:n * 512 + (s + 1) * T][:, ::step]
                    own.done(dve.tensor_tensor_scan(blk(dst, n)[:, ::step], src, src, 0.0, ALU.add, ALU.bypass))
            own.wait()
            qg, kg = Q[:, 0:4 * T], K[:, 0:4 * T]
            for d in range(2):
                end = T - 1 if d == 0 else 0
                if d:
                    dve.wait_ge(sem("kend_ready"), d)
                cc = blk(cumc, 4 * d, 4).rearrange("p (h t) -> p h t", t=T)
                dve.tensor_tensor(dec[0][:, :].rearrange("p (h t) -> p h t", t=T),
                                  cc[:, :, end:end + 1].to_broadcast([P, 4, T]), cc, ALU.subtract).then_inc(sem("kend_arg"), 1)
                dve.wait_ge(sem("kend_exp"), d + 1)
                if d:
                    dve.wait_ge(sem("kend_turned"), 2 * d)
                dve.tensor_tensor(kend[:, :], dec[0][:, :], K[:, 8 * T:12 * T], ALU.mult).then_inc(sem("kend_ready"), 1)
                dve.wait_ge(sem("qb_exp"), d + 1)
                dve.tensor_tensor(qb[d][:, :], dec[1][:, :], qg, ALU.mult).then_inc(sem("qb_ready"), 1)
            dve.wait_ge(sem("qb_ready"), 2)
            dve.wait_ge(sem("eye_loaded"), 16)
            for g in range(2):
                dve.wait_ge(sem("diag_done"), g + 1)
                for d in range(2):
                    ins = dve.tensor_tensor(att[d][:, g * 512:(g + 1) * 512].rearrange("p (a j) -> p a j", j=P),
                                            PS[4 + g][:, :].rearrange("p (a j) -> p a j", j=P),
                                            eye[:, :][:, None, :].to_broadcast([P, 4, P]), ALU.mult)
                    ins.then_inc(sem("diag_used"), 1)
            dve.wait_ge(sem("diag_used"), 4)
            dve.wait_ge(sem("tables_loaded"), 64)
            NL = len(LEVELS)
            for n in range(2 * NL + 1):
                if n < 2 * NL:
                    d, x = n // NL, LEVELS[n % NL]
                    qh, kh, ref = (1, 0, x - 1) if d == 0 else (0, 1, x)

                    def half(t, w):
                        return t.rearrange("p (b c x) -> p b c x", c=2, x=x)[:, :, w, :]
                    cum = blk(cumx, 4 * d, 4)
                    rv = cum.rearrange("p (b x) -> p b x", x=2 * x)[:, :, ref:ref + 1].to_broadcast([P, 2 * T // x, x])
                    if n >= 2:
                        dve.wait_ge(sem("lvl_ops"), n - 1)
                    dve.tensor_tensor(half(dec[n % 2][:, :], qh), half(cum, qh), rv, ALU.subtract)
                    dve.tensor_tensor(half(dec[n % 2][:, :], kh), rv, half(cum, kh), ALU.subtract).then_inc(sem("lvl_arg"), 1)
                if n >= 1 and (n - 1) % NL:
                    m = n - 1
                    d1, l1 = m // NL, m % NL
                    dve.wait_ge(sem("lvl_scores"), m + 1)
                    mask = lvl[:, (7 * d1 + l1 - 1) * P:(7 * d1 + l1) * P][:, None, :].to_broadcast([P, 4, P])
                    for g in range(2):
                        ins = dve.copy_predicated(att[d1][:, g * 512:(g + 1) * 512].rearrange("p (a j) -> p a j", j=P), mask,
                                                  PS[4 + 2 * (m % 2) + g][:, :].rearrange("p (a j) -> p a j", j=P))
                        ins.then_inc(sem("lvl_merged"), 1)
                    dve.wait_ge(sem("lvl_merged"), 2 * (m - m // NL))
                if n < 2 * NL:
                    dve.wait_ge(sem("lvl_exp"), n + 1)
                    if n >= 2:
                        dve.wait_ge(sem("lvl_scores"), n - 1)
                    dve.tensor_tensor(half(qk[n % 2][:, :], qh), half(dec[n % 2][:, :], qh), half(qg, qh), ALU.mult)
                    dve.tensor_tensor(half(qk[n % 2][:, :], kh), half(dec[n % 2][:, :], kh), half(kg, kh),
                                      ALU.mult).then_inc(sem("lvl_ops"), 1)
            for g in range(2):
                dve.wait_ge(sem("gla_root"), g + 1)
                own.done(dve.reciprocal(rgrp[:, g * 512:(g + 1) * 512], rgrp[:, g * 512:(g + 1) * 512]))
                own.wait()
                for b in range(4 * g, 4 * g + 4):
                    own.done(dve.scalar_tensor_tensor(blk(yf, b), PS[b // 2][:, (b % 2) * T:(b % 2 + 1) * T],
                                                      v("gla_g", b % 2), blk(rgrp, b // 2), ALU.mult, ALU.mult))
                own.wait()
                dve.tensor_tensor(blk(yf, 4 * g, 4), blk(yf, 4 * g, 4), blk(gates, 4 * g, 4), ALU.mult).then_inc(sem("operand_made"), 1)

            dve.wait_ge(sem("if_rows"), 1)
            own.done(dve.tensor_scalar(ri[:, :], PS[5][0:64, :], v("gate_b", 0)[0:64, :], None, ALU.add))
            own.done(dve.tensor_scalar(rf[:, :], PS[6][0:64, :], v("gate_b", 1)[0:64, :], None, ALU.add))
            own.wait()
            dve.scalar_tensor_tensor(rl[:, :], rf[:, :], -1.0, rf[:, :], ALU.mult, ALU.max).then_inc(sem("f_abs"), 1)
            dve.wait_ge(sem("f_ln"), 1)
            own.done(dve.scalar_tensor_tensor(rf[:, :], rf[:, :], 0.0, rl[:, :], ALU.min, ALU.subtract))
            own.wait()

            def scan(dst, src, op):
                for row, st in ((0, 1), (32, -1)):
                    a = src[row:row + 32, T:2 * T][:, ::st]
                    own.done(dve.tensor_tensor_scan(dst[row:row + 32, T:2 * T][:, ::st], a, a, 0.0, op, ALU.bypass))
                own.wait()
                for row, st, last in ((0, 1, 2 * T - 1), (32, -1, T)):
                    a = src[row:row + 32, 0:T][:, ::st]
                    own.done(dve.tensor_tensor_scan(dst[row:row + 32, 0:T][:, ::st], a, a,
                                                    dst[row:row + 32, last:last + 1], op, ALU.bypass))
                own.wait()
            scan(rl, rf, ALU.add)
            own.done(dve.tensor_tensor(rg[:, :], ri[:, :], rl[:, :], ALU.subtract))
            own.wait()
            scan(rm, rg, ALU.max)
            own.done(dve.tensor_scalar(ri[:, 0:T], rm[:, 0:T], -1.0, None, ALU.mult))
            own.wait()
            dve.tensor_tensor(rm[:, 0:T], rm[:, 0:T], rl[:, 0:T], ALU.add).then_inc(sem("m_rows"), 1)
            dve.wait_ge(sem("maskn_loaded"), 16)
            dve.wait_ge(sem("gtok_ready"), 1)
            for n in range(9):
                if n < 8:
                    h, d = n // 2, n % 2
                    W = wgt[n % 2]
                    if n >= 2:
                        dve.wait_ge(sem("ml_done"), n - 1)
                    for t in range(2):
                        c = t * 64 + 32 * d + h
                        ins = dve.scalar_tensor_tensor(W[:, t * T:(t + 1) * T], blk(neg_g, 4 * d + h), gtok[:, c:c + 1],
                                                       blk(maskn, 2 * d + t), ALU.add, ALU.add)
                    ins.then_inc(sem("w_arg"), 1)
                    dve.wait_ge(sem("w_x"), n + 1)
                    dve.wait_ge(sem("ml_scores"), h + 1)
                    for g in range(2):
                        ins = dve.tensor_tensor(W[:, g * 512:(g + 1) * 512], W[:, g * 512:(g + 1) * 512],
                                                PS[2 * (h % 2) + g][:, :], ALU.mult)
                    ins.then_inc(sem("ml_w"), 1)
                if n >= 1:
                    m = n - 1
                    h, d = m // 2, m % 2
                    dve.wait_ge(sem("ml_done"), m + 1)
                    den = PS[6][:, 0:T]
                    own.done(dve.tensor_tensor(rden[d][:, :], den, blk(em, 4 * d + h), ALU.max))
                    own.wait()
                    own.done(dve.scalar_tensor_tensor(rden[d][:, :], den, -1.0, rden[d][:, :], ALU.mult, ALU.max))
                    own.wait()
                    own.done(dve.reciprocal(rden[d][:, :], rden[d][:, :]))
                    own.wait()
                    o2 = blk(omix, 2 * h, 2).rearrange("p (a t) -> p a t", t=T)
                    t2 = tmpo[:, :].rearrange("p (a t) -> p a t", t=T)
                    n2 = PS[4 + d][:, :].rearrange("p (a t) -> p a t", t=T)
                    rb = rden[d][:, :][:, None, :].to_broadcast([P, 2, T])
                    if d == 0:
                        dve.tensor_tensor(o2, n2, rb, ALU.mult).then_inc(sem("ml_taken"), 1)
                        continue
                    dve.tensor_tensor(t2, n2, rb, ALU.mult).then_inc(sem("ml_taken"), 1)
                    dve.wait_ge(sem("ml_taken"), m + 1)
                    dve.tensor_tensor(o2, o2, t2, ALU.add).then_inc(sem("ml_h"), 1)
                    dve.wait_ge(sem("ml_root"), h + 1)
                    own.done(dve.reciprocal(rden[h % 2][:, :], rden[h % 2][:, :]))
                    own.wait()
                    for a in range(2):
                        own.done(dve.scalar_tensor_tensor(blk(yf, 8 + 2 * h + a), blk(omix, 2 * h + a), v("ml_g", a),
                                                          rden[h % 2][:, :], ALU.mult, ALU.mult))
                    own.wait()
                    ins = dve.tensor_tensor(blk(yf, 8 + 2 * h, 2), blk(yf, 8 + 2 * h, 2), blk(gates, 8 + 2 * h, 2), ALU.mult)
                    if h % 2:
                        ins.then_inc(sem("operand_made"), 1)
                    else:
                        own.done(ins)
            for q in range(4):
                rest("y", q, yh, yl, yf)

            clear_ssq()
            dve.wait_ge(sem("R_loaded"), 16)
            for i, r in turns(dve, 16):
                split("mix_out", i, r)
                u = 4 * i + r
                dve.wait_ge(slot_used, where("mix_out", i, r) + 1)
                dve.scalar_tensor_tensor(blk(R, u), PS[r % 2][:, 0:T], mods[:, bass.ds(64 + 2 * u, 1)], blk(R, u),
                                         ALU.mult, ALU.add).then_inc(evacuated, 1)
                dve.wait_ge(evacuated, EVAC["mix_out"] + u + 1)
                accumulate(Steps(dve, sem("square_steps"), reached("steps", "n2") + 2 * u), blk(R, u), tmpx)
            recip("n2", rs[:, :])
            normed("n2", R, lambda b: amod[:, 2 * KD + b:2 * KD + b + 1], tn, x2h, x2l,
                   shift=lambda b: mview[:, 48 + b, 0:1])
            own.done(dve.memset(pad[0][:, :], 0.0))
            dve.memset(pad[1][:, :], 0.0).then_inc(sem("pads_zeroed"), 1)

            for i, r in turns(dve, 2 * KF):
                split("up", i, r)
                j, b = 2 * i + r // 2, (r // 2) % 2
                if r % 2 == 0:
                    st = Steps(dve, sem("conv"), 9 * j)
                    dve.wait_ge(evacuated, EVAC["up"] + 2 * j + 1)
                    pv = pad[b][:, :].rearrange("p (y x) -> p y x", x=66)
                    a3 = acc[b][:, :].rearrange("p (y x) -> p y x", x=GRID_W)
                    for t in range(9):
                        window = pv[:, t // 3:t // 3 + GRID_H, t % 3:t % 3 + GRID_W]
                        tap = vec[:, bass.ds(9 * j + (VEC["conv_w"] + t), 1)]
                        if t == 0:
                            st.done(dve.tensor_scalar(a3, window, tap, None, ALU.mult))
                        else:
                            st.wait()
                            st.done(dve.scalar_tensor_tensor(a3, window, tap, a3, ALU.mult, ALU.add))
                else:
                    dve.wait_ge(slot_used, where("up", i, r) + 1)
                    dve.wait_ge(sem("ff_silu"), j + 1)
                    dve.wait_ge(sem("ff_x"), j)
                    dve.tensor_tensor(ht[b][:, :], sil[b][:, :], PS[r % 2][:, 0:T], ALU.mult).then_inc(evacuated, 1)
                    dve.wait_ge(sem("ff_hi"), j + 1)
                    dve.tensor_tensor(blk(hl, j), ht[b][:, :], blk(hh, j).bitcast(F32), ALU.subtract).then_inc(sem("ff_x"), 1)
            for i, r in turns(dve, KF):
                split("down", i, r)
            dve.wait_ge(slot_used, BASE["down"] + KF)
            for b in range(KD):
                ins = dve.scalar_tensor_tensor(blk(R, b), PS[b // 2][:, (b % 2) * T:(b % 2 + 1) * T],
                                               mods[:, 160 + 2 * b:161 + 2 * b], blk(R, b), ALU.mult, ALU.add)
                if b % 4 == 3:
                    ins.then_inc(sem("part_ready"), 1)
            add_squares("nf", tn)
            recip("nf", rs[:, :])
            for b in range(KD):
                ins = dve.scalar_tensor_tensor(blk(R, b), blk(R, b), v("gfin", b), rs[:, :], ALU.mult, ALU.mult)
                if b % 4 == 3:
                    ins.then_inc(sem("part_ready"), 1)
            add_squares("np", tn)
            recip("np", rs[:, :])
            dve.wait_ge(sem("part_ready"), reached("part", "np", 4))
            normed("np", R, lambda b: v("pre0", b), pnt, xph, xpl)
            for t in (up[0], up[1], ws[0]):
                own.done(dve.memset(t[:, :], 0.0))
            dve.memset(ws[1][:, :], 0.0).then_inc(sem("ups_zeroed"), 1)
            dve.wait_ge(sem("ups_zeroed"), 1)

            for g in range(4):
                with dve.Fori(2 * g, 2 * g + 2) as i:
                    for r in range(4):
                        split("pool_in", i, r)
                        u = 4 * i + r
                        st = Steps(dve, sem("window_steps"), 8 * sum(range(2, g + 2)) + (g + 2) * (u - 8 * g))
                        dve.wait_ge(evacuated, EVAC["pool_in"] + u + 1)
                        dve.wait_ge(sem("pool_x"), u)
                        src = up[r % 2]
                        for l in range(g + 1):
                            dst, lag = ws[l % 2], 1 << l
                            st.done(dve.tensor_tensor(dst[:, 16:UPW], src[:, 16:UPW], src[:, 16 - lag:UPW - lag], ALU.add))
                            st.wait()
                            src = dst
                        st.done(dve.tensor_tensor(src[:, 16:32], src[:, 16:32], v("corr", 16 * g, 16), ALU.mult))
                        st.wait()
                        dve.scalar_tensor_tensor(pf[:, :], src[:, 16:UPW], 1.0 / WINDOWS[g], up[r % 2][:, 16:UPW],
                                                 ALU.mult, ALU.subtract).then_inc(sem("pool_made"), 1)
                        dve.wait_ge(sem("pool_hi"), u + 1)
                        dve.tensor_tensor(blk(pl, u), pf[:, :], blk(ph, u).bitcast(F32), ALU.subtract).then_inc(sem("pool_x"), 1)
            with dve.Fori(8, 16) as i:
                for r in range(4):
                    split("pool_in", i, r)
            dve.wait_ge(evacuated, EVAC["group"])
            for i, r in turns(dve, 16):
                split("group", i, r)
                s = 4 * i + r
                dve.wait_ge(slot_used, where("group", i, r) + 1)
                dve.wait_ge(sem("y2_x"), s)
                for a in range(2):
                    ins = dve.scalar_tensor_tensor(gt[r % 2][:, a * T:(a + 1) * T], PS[r % 2][:, a * T:(a + 1) * T],
                                                   vec[:, bass.ds(2 * s + (VEC["pscale"] + a), 1)], blk(sg, 2 * s + a),
                                                   ALU.mult, ALU.mult)
                ins.then_inc(evacuated, 1)
                dve.wait_ge(sem("y2_hi"), s + 1)
                dve.tensor_tensor(blk(y2l, 2 * s, 2), gt[r % 2][:, :], blk(y2h, 2 * s, 2).bitcast(F32),
                                  ALU.subtract).then_inc(sem("y2_x"), 1)
            for i, r in turns(dve, 32):
                split("pool_out", i, r)
            dve.wait_ge(slot_used, BASE["pool_out"] + 32)
            for b in range(8):
                dve.tensor_copy(blk(O, 2 * b, 2), PS[b][:, :]).then_inc(sem("O_copied"), 1)
            add_squares("post0", ot, 8)

            def p_rest(tag, ptr, pth, ptl):
                dve.wait_ge(sem(f"p{tag}_hi"), 1)
                dve.tensor_tensor(ptl[:, :], ptr[:, :], pth[:, :].bitcast(F32), ALU.subtract).then_inc(sem(f"p{tag}_x"), 1)

            def after_block(tag, o_t, xh_, xl_):
                recip(f"post{tag}", rs[:, :])
                for q in range(4):
                    for b in range(4 * q, 4 * q + 4):
                        own.done(dve.scalar_tensor_tensor(blk(O, b), blk(O, b), v(f"post{tag}", b), rs[:, :], ALU.mult, ALU.mult))
                    own.wait()
                    dve.tensor_tensor(blk(R, 4 * q, 4), blk(R, 4 * q, 4), blk(O, 4 * q, 4), ALU.add).then_inc(sem("part_ready"), 1)
                add_squares(f"ple{tag}", o_t)
                recip(f"ple{tag}", rs[:, :])
                normed(f"ple{tag}", R, lambda b: v(f"ple{tag}", b), o_t, xh_, xl_)

            def gated(tag, pj, per, tail=0):
                dve.memset(ssq[:, :], 0.0).then_inc(sem(f"gate{tag}_used"), 1)
                dve.wait_ge(sem(f"gate{tag}_used"), 1)
                for i, r in turns(dve, 16, tail):
                    split(f"plegate{tag}", i, r)
                    u = 4 * i + r
                    dve.wait_ge(evacuated, EVAC[f"plegate{tag}"] + u + 1)
                    dve.tensor_tensor(sgt[r % 2][:, :], sgt[r % 2][:, :], blk(pj, u), ALU.mult).then_inc(sem(f"gate{tag}_mult"), 1)
                    dve.wait_ge(sem(f"gate{tag}_mult"), u + 1)
                    dve.tensor_tensor(blk(R, u), blk(R, u), sgt[r % 2][:, :], ALU.add).then_inc(sem(f"gate{tag}_used"), 1)
                    if per:
                        dve.wait_ge(sem(f"gate{tag}_used"), u + 2)
                        accumulate(Steps(dve, sem("square_steps"), reached("steps", "m") + 2 * u), blk(R, u), tmpg)

            p_rest(0, ptr0, pth0, ptl0)
            for s in range(2):
                split("proj0", 0, s)
            after_block(0, ot, gxh, gxl)
            gated(0, pj0, 2)

            dve.wait_ge(sem("pos_loaded"), 16)
            own.done(dve.tensor_copy(ang[2][:, :], post[:, :]))
            own.wait()
            own.done(dve.tensor_scalar(ang[0][:, :], ang[2][:, :], v("invf"), None, ALU.mult))
            own.wait()
            own.done(dve.tensor_scalar(ang[3][:, :], ang[0][:, :], float(1 / (2 * np.pi)), None, ALU.mult))
            own.wait()
            own.done(dve.tensor_scalar(ang[3][:, :], ang[3][:, :], 12582912.0, None, ALU.add))
            own.wait()
            own.done(dve.tensor_scalar(ang[3][:, :], ang[3][:, :], -12582912.0, None, ALU.add))
            own.wait()
            for part in TWO_PI:
                own.done(dve.scalar_tensor_tensor(ang[0][:, :], ang[3][:, :], -part, ang[0][:, :], ALU.mult, ALU.add))
                own.wait()
            own.done(dve.tensor_scalar(ang[0][:, :], ang[0][:, :], 3.1415925, -3.1415925, ALU.min, ALU.max))
            own.wait()
            dve.scalar_tensor_tensor(ang[1][:, :], ang[0][:, :], -1.0, ang[0][:, :], ALU.mult, ALU.max).then_inc(sem("ang_ready"), 1)
            recip("m", rs[:, :])
            normed("m", R, lambda b: v("pre1", b), mnt, xmh, xml)
            own.done(dve.memset(ssqk[:, :], 0.0))
            clear_ssq()

            def rotate(d1, d2, x1, x2, signal=None):
                cos, sin = cs[:, 0:T], cs[:, T:2 * T]
                own.wait()
                for n, (a, c) in enumerate(((x1, cos), (x2, sin), (x2, cos), (x1, sin))):
                    own.done(dve.tensor_tensor(rt[n][:, :], a, c, ALU.mult))
                own.wait()
                own.done(dve.tensor_tensor(d1, rt[0][:, :], rt[1][:, :], ALU.subtract))
                ins = dve.tensor_tensor(d2, rt[2][:, :], rt[3][:, :], ALU.add)
                ins.then_inc(sem(signal), 1) if signal else own.done(ins)

            for j in range(26):
                split("mla_in", j // 4, j % 4)
                if j < 10:
                    dve.wait_ge(evacuated, EVAC["mla_in"] + j + 1)
                if j < 8:
                    accumulate(Steps(dve, sem("square_steps"), reached("steps", "q") + 2 * j), blk(ql, j), rt[3], ssq if j < 4 else ssqk)
                if j == 9:
                    dve.wait_ge(sem("rope_cs"), 2)
                    dve.wait_ge(sem("square_steps"), reached("steps", "kv", 8))
                    rotate(kp[:, 0:T], kp[:, T:2 * T], kpr[:, 0:T], kpr[:, T:2 * T])
            recip("q", rs[:, :])
            recip("kv", rsk[:, :])
            normed("lat", ql, lambda b: v("q_norm", b) if b < 4 else v("kv_norm", b - 4), ql, lath, latl,
                   inv=lambda b: rs if b < 4 else rsk, quads=2)
            dve.wait_ge(sem("operand_rest"), reached("x", "lat", 2))
            for s in range(6):
                split("uq", s // 4, s % 4)
                if s >= 4:
                    dve.wait_ge(evacuated, EVAC["uq"] + s + 1)
                    for a in range(2):
                        m = 2 * (s - 4) + a
                        rotate(blk(qp, m), blk(qp, 4 + m), blk(qraw, 2 * a), blk(qraw, 2 * a + 1), a and "q_rot")
            for name in ("uk", "uv"):
                for s in range(4):
                    split(name, 0, s)
            dve.wait_ge(sem("maska_loaded"), 16)
            for n in range(NH + 3):
                if n < NH:
                    b = n % 2
                    c = 8 * n
                    dve.wait_ge(sem("scores_done"), n + 1)
                    if n >= 2:
                        dve.wait_ge(sem("p_exp"), 2 * (n - 1))
                    dve.tensor_tensor(s_[b][:, :], PS[b][:, 0:3 * P], maska[:, :], ALU.add).then_inc(sem("s_masked"), 1)
                    dve.wait_ge(sem("s_masked"), n + 1)
                    own.done(dve.reduce_max(stat[:, c + 4:c + 5], s_[b][:, 0:P], AX))
                    own.done(dve.reduce_max(stat[:, c + 5:c + 6], s_[b][:, P:3 * P], AX))
                    own.wait()
                    dve.tensor_scalar(stat[:, c:c + 2], stat[:, c + 4:c + 6], -SM_SCALE, None, ALU.mult).then_inc(sem("s_max"), 1)
                if 1 <= n <= NH:
                    h = n - 1
                    c, b = 8 * h, h % 2
                    dve.wait_ge(sem("p_exp"), 2 * h + 2)
                    own.done(dve.reciprocal(stat[:, c + 6:c + 8], stat[:, c + 2:c + 4]))
                    own.wait()
                    dve.tensor_scalar(p_[b][:, 0:P], p_[b][:, 0:P], stat[:, c + 6:c + 7], None, ALU.mult)
                    dve.tensor_scalar(p_[b][:, P:3 * P], p_[b][:, P:3 * P], stat[:, c + 7:c + 8], None,
                                      ALU.mult).then_inc(sem("p_norm"), 1)
                if 2 <= n <= NH + 1:
                    h = n - 2
                    dve.wait_ge(sem("pv_done"), h + 1)
                    if h >= 2:
                        dve.wait_ge(sem("y3_x"), h - 1)
                    dve.tensor_tensor(yt[h % 2][:, :], PS[2 + h % 2][:, 0:T], blk(sg2, h), ALU.mult).then_inc(sem("o_made"), 1)
                if n >= 3:
                    h = n - 3
                    dve.wait_ge(sem("y3_hi"), h + 1)
                    dve.tensor_tensor(blk(y3l, h), yt[h % 2][:, :], blk(y3h, h).bitcast(F32), ALU.subtract).then_inc(sem("y3_x"), 1)
            clear_ssq()
            for i, r in turns(dve, 16):
                split("mla_out", i, r)
                u = 4 * i + r
                dve.wait_ge(evacuated, EVAC["mla_out"] + u + 1)
                accumulate(Steps(dve, sem("square_steps"), reached("steps", "post1") + 2 * u), blk(O, u), tmpq)
            p_rest(1, ptr1, pth1, ptl1)
            for s in range(2):
                split("proj1", 0, s)
            after_block(1, ot1, fxh, fxl)
            gated(1, pj1, 0, tail=4)

        @block.tensor
        def _(pe):
            def mm3(o, wh, wl, ah, al, start, stop, swap=False):
                kw = dict(skip_group_check=True)
                if swap:
                    pe.matmul(o, ah, wh, start=start, stop=False, **kw)
                    pe.matmul(o, ah, wl, start=False, stop=False, **kw)
                    return pe.matmul(o, al, wh, start=False, stop=stop, **kw)
                pe.matmul(o, wh, ah, start=start, stop=False, **kw)
                pe.matmul(o, wh, al, start=False, stop=False, **kw)
                return pe.matmul(o, wl, ah, start=False, stop=stop, **kw)

            def slot(phase, i, r, product, count=BLOCKS):
                s = where(phase, i, r)
                p = (BASE[phase] + r) % PAIR
                for n in range(count):
                    if n % (count // 2) == 0:
                        pe.wait_ge(lo_ready, 2 * s + n // (count // 2) + 1)
                    c = slice(n * SLOT // count, (n + 1) * SLOT // count)
                    ins = product(n, HI[p][:, c], LO[p][:, c])
                ins.then_inc(slot_used, 1)

            def out_major(phase, i, r, ah, al, bank=None):
                u = 4 * i + r
                if not isinstance(u, int) or EVAC[phase] + u - 1 > 0:
                    pe.wait_ge(evacuated, EVAC[phase] + u - 1)
                slot(phase, i, r, lambda n, h, l: mm3(PS[r % 2][:, 0:T], h, l, blk(ah, n), blk(al, n), n == 0, n == 15))

            def sum_squares(name, kind, o=None, src=None):
                done = dict(SHARED[kind])[name]
                pe.wait_ge(sem({"steps": "square_steps", "ssq": "ssq_ready"}[kind]), reached(kind, name, done))
                src = ssq[:, :] if src is None else src
                o = PS[2][:, 0:T] if o is None else o
                pe.matmul(o, ones[:, :], src, start=True, stop=True, skip_group_check=True).then_inc(sem("norm_sum"), 1)

            pe.wait_ge(sem("ssq_ready"), reached("ssq", "n1", 2))
            pe.wait_ge(sem("ones_ready"), 1)
            pe.matmul(PS[2][:, :], ones[:, :], ssqx[:, :], start=True, stop=True).then_inc(sem("norm_sum"), 1)
            pe.wait_ge(sem("c_lo"), 1)
            for i, r in turns(pe, 96):
                u = 4 * i + r
                slot("mod", i, r, lambda n, h, l: mm3(PS[0][:, bass.ds(2 * u, 2)], h, l, ch[:, 2 * n:2 * n + 2],
                                                      cl[:, 2 * n:2 * n + 2], n == 0, n == 15))

            pe.wait_ge(sem("operand_rest"), reached("x", "x1", 8))
            xhv = xh[:, :].rearrange("p (s k t) -> p s k t", s=2, k=KD)
            xlv = xl[:, :].rearrange("p (s k t) -> p s k t", s=2, k=KD)

            def both(phase, i, r, bank):
                o = PS[bank][:, :].rearrange("p (s t) -> p s t", s=2)
                slot(phase, i, r, lambda n, h, l: mm3(o, h, l, xhv[:, :, n, :], xlv[:, :, n, :], n == 0, n == 15))
            both("lr", 0, 0, 0)
            for b in range(8):
                pe.wait_ge(evacuated, max(EVAC["key"] + b - 1, 1))
                both("key", b // 4, b % 4, b % 2)
            pe.wait_ge(evacuated, EVAC["value"])
            with pe.Fori(0, 2) as i:
                for r in range(8):
                    g, q = r // 4, r % 4
                    if q == 0:
                        pe.wait_ge(evacuated, EVAC["value"] + 8 * i + (4 * g - 4))

                    def product(n, h, l):
                        for tt in range(4):
                            k, s = 4 * q + n, tt // 2
                            c = slice((s * KD + k) * T + (tt % 2) * P, (s * KD + k) * T + (tt % 2 + 1) * P)
                            ins = mm3(PS[4 * g + tt][:, :], h, l, xh[:, c], xl[:, c], k == 0, k == 15, swap=True)
                        return ins
                    slot("value", 2 * i, r, product, count=4)
            pe.wait_ge(evacuated, EVAC["query"])
            for b in range(8):
                out_major("query", b // 4, b % 4, xh, xl)
            for i, r in turns(pe, 16):
                out_major("gate", i, r, xh, xl)

            pe.wait_ge(evacuated, EVAC["mix_out"])
            pe.wait_ge(sem("tables_loaded"), 64)
            for n in range(8):
                pe.matmul(PS[n][:, :], w_lr[:, n * P:(n + 1) * P], zlr[0:16, :], start=True, stop=True).then_inc(sem("dec_z"), 1)
            pe.wait_ge(sem("dec_abs"), 1)
            for g in range(2):
                for a in range(4):
                    h, t = 2 * g + a // 2, a % 2
                    c = slice(h * T + t * P, h * T + (t + 1) * P)
                    ins = pe.matmul(PS[4 + g][:, a * P:(a + 1) * P], K[:, c], Q[:, c], start=True, stop=True)
                ins.then_inc(sem("diag_done"), 1)
            pe.wait_ge(sem("eye_loaded"), 16)
            for d in range(2):
                pe.wait_ge(sem("kend_ready"), d + 1)
                for t in range(2):
                    if d:
                        pe.wait_ge(sem("kend_t_ready"), 2)
                    for h in range(HEADS):
                        ins = pe.transpose(PS[t][:, h * P:(h + 1) * P], kend[:, h * T + t * P:h * T + (t + 1) * P], eye[:, :])
                    ins.then_inc(sem("kend_turned"), 1)
                pe.wait_ge(sem("kend_t_ready"), 2 * d + 2)
                for g in range(2):
                    if d:
                        pe.wait_ge(sem("state_ready"), 2)
                    for h in (2 * g, 2 * g + 1):
                        for t in range(2):
                            ins = pe.matmul(PS[2 + g][:, (h % 2) * DV:(h % 2 + 1) * DV], kend_t[:, t * 512 + h * P:t * 512 + (h + 1) * P],
                                            V[:, (2 + t) * 2048 + h * DV:(2 + t) * 2048 + (h + 1) * DV], start=t == 0, stop=t == 1,
                                            skip_group_check=True)
                    ins.then_inc(sem("state_done"), 1)
            NL = len(LEVELS)
            pe.wait_ge(sem("diag_used"), 4)
            for n in range(2 * NL):
                d, l = n // NL, n % NL
                pe.wait_ge(sem("lvl_ops"), n + 1)
                if n >= 2:
                    m = n - 2
                    if m // NL or m % NL:
                        pe.wait_ge(sem("lvl_merged"), 2 * (m - m // NL))
                    pe.wait_ge(sem("cross_ready"), m // NL + 1)
                for a in range(4 if l == 0 else 8):
                    if l == 0:
                        kt, qt = (0, 1) if d == 0 else (1, 0)
                        ck, cq, o = a * T + kt * P, a * T + qt * P, PS[4][:, a * P:(a + 1) * P]
                    else:
                        ck = cq = a * P
                        o = PS[4 + 2 * (n % 2) + a // 4][:, (a % 4) * P:(a % 4 + 1) * P]
                    ins = pe.matmul(o, qk[n % 2][:, ck:ck + P], qk[n % 2][:, cq:cq + P], start=True, stop=True,
                                    skip_group_check=True)
                ins.then_inc(sem("lvl_scores"), 1)
            pe.wait_ge(sem("lvl_merged"), 4 * (NL - 1))
            pe.wait_ge(sem("cross_ready"), 2)
            pe.wait_ge(sem("state_ready"), 4)
            for h in range(HEADS):
                for a in range(2):
                    o = PS[h][:, a * T:(a + 1) * T]
                    vc = h * DV + a * P
                    kw = dict(skip_group_check=True)
                    for d in range(2):
                        pe.matmul(o, state[d][:, vc:vc + P], qb[d][:, h * T:(h + 1) * T], start=d == 0, stop=False, **kw)
                    for d in range(2):
                        for t in range(2):
                            pe.matmul(o[:, t * P:(t + 1) * P], V[:, t * 2048 + vc:t * 2048 + vc + P],
                                      att[d][:, (2 * h + t) * P:(2 * h + t + 1) * P], start=False, stop=False, **kw)
                        kt, qt = (0, 1) if d == 0 else (1, 0)
                        ins = pe.matmul(o[:, qt * P:(qt + 1) * P], V[:, kt * 2048 + vc:kt * 2048 + vc + P],
                                        cross[d][:, h * P:(h + 1) * P], start=False, stop=d == 1, **kw)
                ins.then_inc(sem("gla_out"), 1)
            for g in range(2):
                for h in (2 * g, 2 * g + 1):
                    pe.wait_ge(sem("gla_sq"), h + 1)
                    for a in range(2):
                        ins = pe.matmul(PS[4 + g][:, (h % 2) * T:(h % 2 + 1) * T], ones[:, :], blk(osq, 2 * h + a),
                                        start=a == 0, stop=a == 1, skip_group_check=True)
                ins.then_inc(sem("gla_sum"), 1)

            pe.wait_ge(sem("gla_root"), 2)
            for n in range(2):
                ins = pe.matmul(PS[5 + n][0:64, :], sel_if[:, n * 64:(n + 1) * 64], zlr[0:32, :], start=True, stop=True)
            ins.then_inc(sem("if_rows"), 1)
            pe.wait_ge(sem("m_rows"), 1)
            for src, ready, done, first in ((ri, "m_rows", "neg_g_rep", 0), (rm, "em_rows", "em_rep", 4)):
                pe.wait_ge(sem(ready), 1)
                for n in range(8):
                    ins = pe.matmul(PS[first + n // 2][:, (n % 2) * T:(n % 2 + 1) * T], rep_sel[:, n * P:(n + 1) * P],
                                    src[:, 0:T], start=True, stop=True, skip_group_check=True)
                    if n % 2:
                        ins.then_inc(sem(done), 1)
            pe.wait_ge(sem("neg_g_ready"), 4)
            for t in range(4):
                ins = pe.transpose(PS[0][:, t * 64:(t + 1) * 64], rg[:, t * P:(t + 1) * P], eye[0:64, 0:64])
            ins.then_inc(sem("g_turned"), 1)
            pe.wait_ge(sem("gtok_ready"), 1)
            pe.wait_ge(sem("em_ready"), 4)

            def ml_scores(h):
                if h >= 2:
                    pe.wait_ge(sem("ml_w"), 2 * h - 2)
                for s in range(2):
                    for t in range(2):
                        c = (8 * s + 4 + h) * T + t * P
                        ins = pe.matmul(PS[2 * (h % 2) + s][:, t * T:(t + 1) * T], K[:, c:c + P], blk(Q, 4 + h),
                                        start=True, stop=True, skip_group_check=True)
                ins.then_inc(sem("ml_scores"), 1)
            ml_scores(0)
            for n in range(9):
                h, d = n // 2, n % 2
                if n < 8:
                    if d == 0 and h + 1 < HEADS:
                        ml_scores(h + 1)
                    W = wgt[n % 2]
                    pe.wait_ge(sem("ml_w"), n + 1)
                    if n >= 2:
                        pe.wait_ge(sem("ml_taken"), n - 1)
                    for a in range(3):
                        if a == 2 and n:
                            pe.wait_ge(sem("ml_taken"), n)
                        for t in range(4):
                            vc = t * 2048 + 1024 + h * DV + a * P
                            w = V[:, vc:vc + P] if a < 2 else ones[:, :]
                            o = PS[4 + d][:, a * T:(a + 1) * T] if a < 2 else PS[6][:, 0:T]
                            ins = pe.matmul(o, w, W[:, t * T:(t + 1) * T], start=t == 0, stop=t == 3, skip_group_check=True)
                    ins.then_inc(sem("ml_done"), 1)
                if n >= 2 and d == 0:
                    pe.wait_ge(sem("ml_sq"), h)
                    if h >= 2:
                        pe.wait_ge(sem("ml_root"), h - 1)
                    for a in range(2):
                        ins = pe.matmul(PS[7][:, 0:T], ones[:, :], tmpo[:, a * T:(a + 1) * T], start=a == 0, stop=a == 1)
                    ins.then_inc(sem("ml_sum"), 1)

            pe.wait_ge(sem("operand_rest"), reached("x", "y", 4))
            for i, r in turns(pe, 16):
                out_major("mix_out", i, r, yh, yl)
            sum_squares("n2", "steps")
            pe.wait_ge(sem("operand_rest"), reached("x", "n2", 4))
            for i, r in turns(pe, 2 * KF):
                out_major("up", i, r, x2h, x2l)
            pe.wait_ge(sem("ff_x"), KF)
            pe.wait_ge(sem("norm_root"), reached("root", "n2", 1))

            def k_major(phase, ah, al):
                def one(i, r, u, first=False):
                    return slot(phase, i, r, lambda n, h, l: mm3(
                        PS[n // 2][:, (n % 2) * T:(n % 2 + 1) * T], h, l, blk(ah, u), blk(al, u), first and n % 2 == 0, False))
                for r in range(4):
                    one(0, r, r, first=r == 0)
                n = COUNT[phase] // 4
                with pe.Fori(1, n) as i:
                    for r in range(4):
                        one(i, r, 4 * i + r)
                for u in range(4 * n, COUNT[phase]):
                    one(n, u % 4, u)
            k_major("down", hh, hl)
            sum_squares("nf", "ssq")
            sum_squares("np", "ssq")

            pe.wait_ge(sem("operand_rest"), reached("x", "np", 4))
            for i, r in turns(pe, 64):
                out_major("pool_in", i, r, xph, xpl)
            pe.wait_ge(sem("pool_x"), 32)
            for i, r in turns(pe, 16):
                u = 4 * i + r
                pe.wait_ge(evacuated, EVAC["group"] + u - 1)
                slot("group", i, r, lambda n, h, l: mm3(
                    PS[r % 2][:, (n // 8) * T:(n // 8 + 1) * T], h, l, blk(ph, 8 * i + n % 8), blk(pl, 8 * i + n % 8),
                    n % 8 == 0, n % 8 == 7))
            pe.wait_ge(sem("y2_x"), 16)
            k_major("pool_out", y2h, y2l)

            def proj(tag, pth, ptl):
                pe.wait_ge(sem(f"p{tag}_x"), 1)
                for s in range(2):
                    if s:
                        pe.wait_ge(evacuated, EVAC[f"proj{tag}"] + 1)
                    slot(f"proj{tag}", 0, s, lambda n, h, l: mm3(
                        PS[4 + n // 4][:, (n // 2 % 2) * T:(n // 2 % 2 + 1) * T], h, l, blk(pth, n % 2), blk(ptl, n % 2),
                        n % 2 == 0, n % 2 == 1))
            pe.wait_ge(sem("O_copied"), 8)
            pe.wait_ge(sem("squares_ready"), reached("squares", "post0", 8))
            proj(0, pth0, ptl0)
            sum_squares("post0", "ssq")
            sum_squares("ple0", "ssq")
            pe.wait_ge(sem("operand_rest"), reached("x", "ple0", 4))
            for i, r in turns(pe, 16):
                out_major("plegate0", i, r, gxh, gxl)

            sum_squares("m", "steps")
            pe.wait_ge(sem("operand_rest"), reached("x", "m", 4))
            for j in range(26):
                out_major("mla_in", j // 4, j % 4, xmh, xml)
            sum_squares("q", "steps")
            sum_squares("kv", "steps", PS[3][:, 0:T], ssqk[:, :])
            pe.wait_ge(sem("operand_rest"), reached("x", "lat", 2))
            pe.wait_ge(evacuated, EVAC["uq"])
            for name, n_slots, first in (("uq", 6, 0), ("uk", 4, 4)):
                for s in range(n_slots):
                    e = EVAC[name] + (s - 1)
                    pe.wait_ge(evacuated, e)
                    slot(name, s // 4, s % 4, lambda n, h, l: mm3(
                        PS[2 * (s % 2) + n // 8][:, (n // 4 % 2) * T:(n // 4 % 2 + 1) * T], h, l,
                        blk(lath, first + n % 4), blk(latl, first + n % 4), n % 4 == 0, n % 4 == 3))
            for s in range(4):
                pe.wait_ge(evacuated, EVAC["uv"] + s - 1)

                def product(n, h, l):
                    for t in range(2):
                        c = slice((4 + n) * T + t * P, (4 + n) * T + (t + 1) * P)
                        ins = mm3(PS[2 * (s % 2) + t][:, :], h, l, lath[:, c], latl[:, c], n == 0, n == 3, swap=True)
                    return ins
                slot("uv", 0, s, product, count=4)
            pe.wait_ge(evacuated, EVAC["mla_out"])
            pe.wait_ge(sem("q_rot"), 2)
            for n in range(NH + 2):
                if n < NH:
                    m, row = n // 4, 32 * (n % 4)
                    if n >= 2:
                        pe.wait_ge(sem("s_masked"), n - 1)
                    for t in range(2):
                        o = PS[n % 2][:, P * t:P * t + P * (t + 1)]
                        pe.matmul(o, qn[:, n * T + t * P:n * T + (t + 1) * P], kn[:, n * T:n * T + (t + 1) * P],
                                  start=True, stop=False, skip_group_check=True)
                        for a in range(2):
                            ins = pe.matmul(o, qp[row:row + 32, (4 * a + m) * T + t * P:(4 * a + m) * T + (t + 1) * P],
                                            kp[row:row + 32, a * T:a * T + (t + 1) * P], start=False, stop=a == 1,
                                            skip_group_check=True)
                    ins.then_inc(sem("scores_done"), 1)
                if 1 <= n <= NH:
                    h = n - 1
                    pe.wait_ge(sem("p_norm"), h + 1)
                    if h >= 2:
                        pe.wait_ge(sem("pt_ready"), h - 1)
                    for t in range(3):
                        ins = pe.transpose(PS[4 + h % 2][:, t * P:(t + 1) * P], p_[h % 2][:, t * P:(t + 1) * P], eye[:, :])
                    ins.then_inc(sem("p_turned"), 1)
                if n >= 2:
                    h = n - 2
                    pe.wait_ge(sem("pt_ready"), h + 1)
                    if h >= 2:
                        pe.wait_ge(sem("o_made"), h - 1)
                    va, vb, w = v2[:, h * P:(h + 1) * P], v2[:, 2048 + h * P:2048 + (h + 1) * P], pt[h % 2]
                    o = PS[2 + h % 2]
                    pe.matmul(o[:, 0:P], va, w[:, 0:P], start=True, stop=True, skip_group_check=True)
                    pe.matmul(o[:, P:T], va, w[:, P:2 * P], start=True, stop=False, skip_group_check=True)
                    pe.matmul(o[:, P:T], vb, w[:, 2 * P:3 * P], start=False, stop=True,
                              skip_group_check=True).then_inc(sem("pv_done"), 1)
            pe.wait_ge(sem("y3_x"), 16)
            for i, r in turns(pe, 16):
                out_major("mla_out", i, r, y3h, y3l)
            proj(1, pth1, ptl1)
            sum_squares("post1", "steps")
            sum_squares("ple1", "ssq")
            pe.wait_ge(sem("operand_rest"), reached("x", "ple1", 4))
            for i, r in turns(pe, 16, tail=4):
                out_major("plegate1", i, r, fxh, fxl)


def blocks(w, outs=None):
    k, n = w.shape
    return w.reshape(k // P, P, n // P, P).transpose(2, 1, 0, 3)


def slots(w):
    b = blocks(w)
    n, _, kb, _ = b.shape
    per = BLOCKS // kb
    return b.reshape(n // per, per, P, kb, P).transpose(0, 2, 1, 3, 4).reshape(n // per, P, SLOT)


def k_slots(w):
    return w.reshape(-1, P, SLOT)


def wide_slots(w):
    k, n = w.shape
    return w.reshape(k // 512, 4, P, n // 512, 512).transpose(3, 0, 2, 1, 4).reshape(-1, P, SLOT)


def rows(a):
    return a.reshape(-1, P).T


def tokens(a):
    t, f = a.shape
    return a.reshape(t, f // P, P).transpose(2, 1, 0).reshape(P, -1)


def lay_out(x):
    A = {}
    w_in = x["w_in"][0]
    gq, gk, gv, gg, glr, mq, mk, mv, mo, mg = np.split(w_in, np.cumsum(
        [512, 512, 1024, 1024, 16, 512, 512, 1024, 1024]), axis=1)
    up_w = x["w_up"][0]
    gate_up = blocks(up_w).reshape(2, KF, P, SLOT).transpose(1, 0, 2, 3).reshape(2 * KF, P, SLOT)
    mi = x["mla_w_in_2"][0]
    k1, k2 = mi[:, 1024:1056], mi[:, 1056:1088]
    uq = x["mla_w_uq_2"][0].reshape(512, NH, 192)
    pe1 = uq[:, :, 128:160].reshape(512, 4, 1, P)
    pe2 = uq[:, :, 160:192].reshape(512, 4, 1, P)
    ukv = x["mla_w_ukv_2"][0].reshape(512, NH, 256)
    grp = x["pool_w_group_2"][0]
    parts = [slots(x["w_mod"][0]),
             slots(np.concatenate([glr, mg, np.zeros((D, P - 32), np.float32)], 1)),
             slots(gk), slots(mk), wide_slots(np.concatenate([gv, mv], 1)), slots(gq), slots(mq), slots(gg), slots(mo),
             slots(x["w_out"][0]), gate_up, k_slots(x["w_down"][0]), slots(x["pool_w_in_2"][0])]
    parts += [slots(g) for g in grp]
    parts += [k_slots(x["pool_w_out_2"][0]), slots(x["ple_w_proj_2"][0]), slots(x["ple_w_gate_2"][0]),
              slots(np.concatenate([mi[:, :1024]] + [k1] * 4 + [k2] * 4 + [mi[:, 1088:]], 1)),
              slots(uq[:, :, :128].reshape(512, 2048)),
              slots(np.concatenate([pe1, pe2], 2).reshape(512, 1024)),
              slots(ukv[:, :, :128].reshape(512, 2048)), wide_slots(ukv[:, :, 128:].reshape(512, 2048)),
              slots(x["mla_w_out_2"][0]), slots(x["ple_w_proj_2"][1]), slots(x["ple_w_gate_2"][1])]
    A["weights"] = np.concatenate(parts)
    assert A["weights"].shape[0] == SLOTS

    c2 = np.stack([rows(x["c"][0]), rows(x["c_ctx"])], 2).reshape(P, 2 * KD)
    gate_b = np.zeros((P, 2), np.float32)
    for d in range(2):
        gate_b[32 * d:32 * d + HEADS] = x["mlstm_b_gate"][0, d].T
    one = np.ones((P, 1), np.float32)
    invf = (np.float32(10000.0) ** (-np.arange(0, 64, 2, dtype=np.float32) / np.float32(64))).astype(np.float32)
    corr = np.concatenate([w / np.minimum(np.arange(16) + 1, w) for w in WINDOWS]).astype(np.float32)
    cols = {"c2": c2, "b_mod": rows(x["b_mod"][0]), "g1": rows(x["g_norm1"][0]), "g2": rows(x["g_norm2"][0]),
            "gfin": rows(x["g_final"]), "conv_w": x["conv_w"][0].reshape(9, KF, P).transpose(2, 1, 0).reshape(P, -1),
            "conv_b": rows(x["conv_b"][0]), "lr_b": rows(x["gla_b_lr"][0].reshape(-1)), "gla_g": rows(x["gla_g_norm"][0]),
            "ml_g": rows(x["mlstm_g_norm"][0]), "pre0": rows(x["pre_norm_2"][0]), "pre1": rows(x["pre_norm_2"][1]),
            "post0": rows(x["post_norm_2"][0]), "post1": rows(x["post_norm_2"][1]), "pscale": rows(x["pool_scale_2"][0]),
            "ple0": rows(x["ple_norm_2"][0]), "ple1": rows(x["ple_norm_2"][1]), "q_norm": rows(x["mla_q_norm_2"][0]),
            "kv_norm": rows(x["mla_kv_norm_2"][0]), "gate_b": gate_b, "eps": one * np.float32(EPS),
            "invf": np.tile(invf, 4)[:, None], "halfpi": one * np.float32(np.pi / 2), "corr": one * corr[None]}
    A["vec"] = np.concatenate([cols[n] for n in VEC], 1).astype(np.float32, copy=False)
    A["eye"] = np.eye(P, dtype=np.float32)
    A["xt"] = np.concatenate([tokens(x["x"][0]), tokens(x["ctx"][0])], 1)
    A["pt"] = np.concatenate([tokens(x["p_2"][0, 0]), tokens(x["p_2"][1, 0])], 1)
    A["pos"] = np.broadcast_to(x["positions_2"].astype(np.int32, copy=False), (P, T))
    A["w_lr"] = x["gla_w_lr"][0].transpose(1, 0, 2).reshape(16, 8 * P)
    i, j = np.arange(P)[:, None], np.arange(P)[None, :]
    lv = []
    for d in range(2):
        for h in LEVELS[1:]:
            m = (i // (2 * h) == j // (2 * h)) & (i // h % 2 == 0) & (j // h % 2 == 1)
            lv.append(m if d == 0 else m.T)
    A["lvl"] = np.concatenate(lv, 1).astype(np.int8).view(np.int32)
    rep = np.zeros((64, 8, P), np.float32)
    for n in range(8):
        rep[32 * (n // 4) + n % 4, n] = 1.0
    A["rep_sel"] = rep.reshape(64, -1)
    sel = np.zeros((32, 2, 64), np.float32)
    for f in range(2):
        for d in range(2):
            for h in range(HEADS):
                sel[16 + 8 * d + 4 * f + h, f, 32 * d + h] = 1.0
    A["sel_if"] = sel.reshape(32, -1)
    jj = np.arange(T)[None, :]
    mn = [np.where((t * P + i <= jj) if d == 0 else (t * P + i >= jj), 0.0, NEG) for d in range(2) for t in range(2)]
    A["maskn"] = np.concatenate(mn, 1).astype(np.float32)
    causal = np.where(j <= i, 0.0, NEG)
    A["maska"] = np.concatenate([causal, np.zeros((P, P)), causal], 1).astype(np.float32)
    return {k: np.ascontiguousarray(a) for k, a in A.items()}


def kernel(**inputs):
    import concourse.bacc as _bacc
    from concourse.bass_utils import run_bass_kernel_spmd as _run

    x = {k: np.asarray(a) for k, a in inputs.items()}
    arrays = lay_out(x)
    nc = _bacc.Bacc("TRN2", target_bir_lowering=False, num_devices=1, dynamic_dma_scratch_size=1024)
    aps = {k: nc.dram_tensor(f"in_{k}", a.shape, mybir.dt.from_np(a.dtype), kind="ExternalInput").ap()
           for k, a in arrays.items()}
    out = nc.dram_tensor("out_0", (P, KD * T), F32, kind="ExternalOutput").ap()
    build(nc, aps, out)
    r = _run(nc, [{f"in_{k}": a for k, a in arrays.items()}], core_ids=[0])
    got = r.results[0]["out_0"]
    return np.ascontiguousarray(got.reshape(P, KD, T).transpose(2, 1, 0).reshape(1, T, D))
```

```python
from contextlib import ExitStack

import numpy as np
import concourse.bass as bass
from concourse import mybir

F32 = mybir.dt.float32
F32R = mybir.dt.float32r
I32 = mybir.dt.int32
I8 = mybir.dt.int8
ALU = mybir.AluOpType
ACT = mybir.ActivationFunctionType
AX = mybir.AxisListType.X

P = 128
D = 2048
KD = D // P
T = 256
HEADS = 4
DK, DV = 128, 256
FF = 5504
KF = FF // P
EPS = 1e-6
NEG = -1e30
GRID_W = 64
GRID_H = T // GRID_W
WINDOWS = (2, 4, 8, 16)
POOL = 4096
NH = 16
SM_SCALE = (128 + 64) ** -0.5
LEVELS = (128, 64, 32, 16, 8, 4, 2, 1)
BLOCKS = 16
SLOT = BLOCKS * P
RING, PAIR = 4, 2

ROUND = 32
MGROUPS = 8
PHASES = [("lr", 1, 1), ("key", 8, 8), ("value", 16, 16), ("query", 8, 8),
          ("gate", 16, 16), ("mix_out", 16, 16), ("up", 2 * KF, 0), ("down", KF, 0),
          ("pool_in", 64, 64), ("group", 16, 16), ("pool_out", 32, 0), ("proj0", 2, 2),
          ("plegate0", 16, 16), ("mla_in", 26, 26), ("uq", 6, 6), ("uk", 4, 4), ("uv", 4, 4),
          ("mla_out", 16, 16), ("proj1", 2, 2), ("plegate1", 16, 16)]
BASE, COUNT, EVAC = {}, {}, {}
_s = _e = 0
for _n, _c, _v in PHASES:
    BASE[_n], COUNT[_n], EVAC[_n] = _s, _c, _e
    _s, _e = _s + _c, _e + _v
SLOTS = _s
MOD_AT = BASE["mix_out"] + 2


def loads_before(s):
    return ROUND if s < MOD_AT else 3 * ROUND

VEC, _w = {}, 0
for _n, _c in [("c2", 2 * KD), ("b_mod", 96), ("g1", 16), ("g2", 16), ("gfin", 16), ("conv_w", 9 * KF),
               ("conv_b", KF), ("lr_b", 8), ("gla_g", 2), ("ml_g", 2), ("pre0", 16), ("pre1", 16),
               ("post0", 16), ("post1", 16), ("pscale", 32), ("ple0", 16), ("ple1", 16),
               ("q_norm", 4), ("kv_norm", 4), ("gate_b", 2), ("eps", 1), ("invf", 1), ("halfpi", 1),
               ("corr", 64)]:
    VEC[_n] = _w
    _w += _c
NVEC = _w

KB = 1024

FILL = (16, 8, 4, 6, 6, 8, 48)

TWO_PI = (6.28125, 0.00193500518798828125, float(2 * np.pi - 6.28125 - 0.00193500518798828125))


SHARED = {
    "sum": [(n, 1) for n in ("n1", "n2", "nf", "np", "post0", "ple0", "m", "q", "kv", "post1", "ple1")],
    "root": [(n, 1) for n in ("n1", "n2", "nf", "np", "post0", "ple0", "m", "q", "kv", "post1", "ple1")],
    "ssq": [("n1", 2)] + [(n, 1) for n in ("nf", "np", "post0", "ple0", "ple1")],
    "part": [(n, 4) for n in ("nf", "np", "ple0", "ple1")],
    "squares": [("n1", 2), ("nf", 4), ("np", 4), ("post0", 8), ("ple0", 4), ("ple1", 4)],
    "steps": [("n2", 32), ("m", 32), ("q", 8), ("kv", 8), ("post1", 32)],
}
for _k in ("made", "hi", "x"):
    SHARED[_k] = [("x1", 8), ("y", 4), ("n2", 4), ("np", 4), ("ple0", 4), ("m", 4), ("lat", 2), ("ple1", 4)]


def reached(kind, name, n=0):
    names = [a for a, _ in SHARED[kind]]
    return sum(c for _, c in SHARED[kind][:names.index(name)]) + n


class Steps:

    def __init__(self, eng, sem, base=0):
        self.eng, self.sem, self.base, self.n = eng, sem, base, 0

    def start(self):
        self.eng.wait_ge(self.sem, self.base)

    def done(self, ins):
        ins.then_inc(self.sem, 1)
        self.n += 1

    def wait(self):
        if self.n:
            self.eng.wait_ge(self.sem, self.base + self.n)


def turns(eng, n, tail=0, lead=0):
    q = max((n - tail) // RING, 0)
    if q > lead + 1:
        for j in range(RING * lead):
            yield j // RING, j % RING
        with eng.Fori(lead, q) as i:
            for r in range(RING):
                yield i, r
    else:
        q = 0
    for j in range(RING * q, n):
        yield j // RING, j % RING


def build(nc, A, out):
    with ExitStack() as ctx:
        sems = {}

        def sem(name):
            if name not in sems:
                sems[name] = ctx.enter_context(nc.semaphore(name))
            return sems[name]

        arena0 = (nc.sbuf_base + 63) // 64 * 64
        ctx.enter_context(nc.sbuf_tensor("arena", [P, (nc.sbuf_usable_end - arena0 - 64) // 4], F32))

        def at(name, cols, kb, dt=F32, rows=P):
            return nc.alloc_sbuf_tensor_at(name, [rows, cols], dt, offset=arena0 + int(kb * KB))

        RAW = [at(f"raw{i}", SLOT, 8 * i) for i in range(RING)]
        HI = [at(f"hi{i}", SLOT, 32 + 8 * i, F32R) for i in range(PAIR)]
        LO = [at(f"lo{i}", SLOT, 48 + 8 * i, F32R) for i in range(PAIR)]
        vec = at("vec", NVEC, 64)
        mods = at("mods", 192, 67.5)
        eye = at("eye", P, 68.25)
        ones = at("ones", P, 68.75)
        ssq = at("ssq", T, 69.25)
        rs = at("rs", T, 70.25)
        amod = at("amod", 3 * KD, 71.25)
        csil = at("csil", 2 * KD, 71.75)
        W0 = 72
        wk = lambda name, cols, kb, dt=F32, rows=P: at(name, cols, W0 + kb, dt, rows)
        xh, xl = wk("xh", 2 * KD * T, 0, F32R), wk("xl", 2 * KD * T, 32, F32R)
        xf = wk("xf", 2 * KD * T, 64)
        sq = [wk("sq0", KD * T, 96), wk("sq1", KD * T, 112)]
        rsx = wk("rsx", 2 * T, 128)
        ssqx = wk("ssqx", 2 * T, 130)
        K = wk("K", 2 * 8 * T, 64)
        V = wk("V", 4 * 2048, 80)
        zlr = wk("zlr", 2 * T, 112)
        Q = wk("Q", 8 * T, 114)
        gates = wk("gates", 16 * T, 16)
        loga = wk("loga", 8 * 2 * T, 122)
        softp = wk("softp", 8 * 2 * T, 32)
        cumx = wk("cumx", 8 * T, 0)
        cumc = wk("cumc", 8 * T, 8)
        dec = [wk("dec0", 4 * T, 32), wk("dec1", 4 * T, 36)]
        qk = [wk("qk0", 4 * T, 40), wk("qk1", 4 * T, 44)]
        w_lr = wk("w_lr", 8 * P, 138, rows=16)
        att = [wk("att0", 8 * P, 48), wk("att1", 8 * P, 52)]
        cross = [wk("cross0", 4 * P, 56), wk("cross1", 4 * P, 58)]
        kend = wk("kend", 4 * T, 60)
        kend_t = wk("kend_t", 2 * 4 * P, 122)
        state = [wk("state0", 4 * DV, 126), wk("state1", 4 * DV, 130)]
        qb = [wk("qb0", 4 * T, 134), wk("qb1", 4 * T, 138)]
        rep_sel = wk("rep_sel", 8 * P, 142, rows=64)
        lvl_words = wk("lvl_words", 2 * 7 * P // 4, 146, I32)
        lvl = lvl_words[:, :].bitcast(I8)
        sel_if = wk("sel_if", P, 148, rows=32)
        MW = 4 * MGROUPS - 2
        cwin = wk("cwin", KD * MW, 148.5)
        mrows = [wk("mrows0", 512, 134, rows=16), wk("mrows1", 512, 60, rows=16), wk("mrows2", 512, 62, rows=16)]
        osq = wk("osq", 8 * T, 32)
        rgrp = wk("rgrp", 4 * T, 40)
        yf = wk("yf", 16 * T, 48)
        neg_g = wk("neg_g", 8 * T, 0)
        em = wk("em", 8 * T, 8)
        maskn = wk("maskn", 4 * T, 32)
        wgt = [wk("wgt0", 4 * T, 36), wk("wgt1", 4 * T, 40)]
        ri = wk("ri", 2 * T, 122, rows=64)
        rf = wk("rf", 2 * T, 124, rows=64)
        rl = wk("rl", 2 * T, 126, rows=64)
        rg = wk("rg", 2 * T, 128, rows=64)
        rm = wk("rm", 2 * T, 130, rows=64)
        gtok = wk("gtok", 4 * 64, 132)
        rden = [wk("rden0", T, 44), wk("rden1", T, 45)]
        tmpo = wk("tmpo", 2 * T, 46)
        omix = wk("omix", 8 * T, 122)
        yh, yl = wk("yh", 16 * T, 64, F32R), wk("yl", 16 * T, 80, F32R)
        R = wk("R", KD * T, 134)
        tmpx = wk("tmpx", T, 118)
        tn = wk("tn", KD * T, 118)
        x2h, x2l = wk("x2h", KD * T, 86, F32R), wk("x2l", KD * T, 102, F32R)
        hh, hl = wk("hh", KF * T, 0, F32R), wk("hl", KF * T, 43, F32R)
        pad = [wk("pad0", 6 * 66, 118), wk("pad1", 6 * 66, 120)]
        acc = [wk("acc0", T, 122), wk("acc1", T, 123)]
        accb = [wk("accb0", T, 128), wk("accb1", T, 129)]
        sil = [wk("sil0", T, 124), wk("sil1", T, 125)]
        ht = [wk("ht0", T, 126), wk("ht1", T, 127)]
        UPW = 16 + T
        pnt = wk("pnt", KD * T, 64)
        xph, xpl = wk("xph", KD * T, 96, F32R), wk("xpl", KD * T, 112, F32R)
        ph, pl = wk("ph", 32 * T, 0, F32R), wk("pl", 32 * T, 32, F32R)
        sg = wk("sg", 32 * T, 64)
        y2h, y2l = wk("y2h", 32 * T, 64, F32R), wk("y2l", 32 * T, 96, F32R)
        up = [wk("up0", UPW, 128), wk("up1", UPW, 129.0625)]
        ws = [wk("ws0", UPW, 130.125), wk("ws1", UPW, 131.1875)]
        pf = wk("pf", T, 132.25)
        gt = [wk("gt0", 2 * T, 128), wk("gt1", 2 * T, 130)]
        O = wk("O", KD * T, 0)
        ot = wk("ot", KD * T, 16)
        pj0 = wk("pj0", KD * T, 32)
        pth0, ptl0, ptr0 = wk("pth0", 2 * T, 48, F32R), wk("ptl0", 2 * T, 50, F32R), wk("ptr0", 2 * T, 52)
        gxh, gxl = wk("gxh", KD * T, 64, F32R), wk("gxl", KD * T, 80, F32R)
        sgt = [wk("sgt0", T, 54), wk("sgt1", T, 55)]
        mnt = wk("mnt", KD * T, 0)
        xmh, xml = wk("xmh", KD * T, 96, F32R), wk("xml", KD * T, 112, F32R)
        ql = wk("ql", 8 * T, 16)
        kpr = wk("kpr", 2 * T, 24)
        kp = wk("kp", 2 * T, 26)
        cs = wk("cs", 2 * T, 28)
        sg2 = wk("sg2", 16 * T, 32)
        lath, latl = wk("lath", 8 * T, 48, F32R), wk("latl", 8 * T, 56, F32R)
        ssqk = wk("ssqk", T, 30)
        rsk = wk("rsk", T, 31)
        qn = wk("qn", 16 * T, 64)
        qp = wk("qp", 8 * T, 16)
        rt = [wk(f"rt{i}", T, 128 + i) for i in range(4)]
        qraw = wk("qraw", 4 * T, 0)
        kn = wk("kn", 16 * T, 96)
        v2 = wk("v2", 2 * 2048, 112)
        tmpq = wk("tmpq", T, 30)
        tmpg = wk("tmpg", T, 53)
        s_ = [wk("s0", 384, 0), wk("s1", 384, 1.5)]
        p_ = [wk("p0", 384, 3), wk("p1", 384, 4.5)]
        pt = [wk("pt0", 384, 6), wk("pt1", 384, 7.5)]
        maska = wk("maska", 384, 9)
        yt = [wk("yt0", T, 11), wk("yt1", T, 12)]
        stat = wk("stat", 16 * 8, 13)
        y3h, y3l = wk("y3h", 16 * T, 48, F32R), wk("y3l", 16 * T, 80, F32R)
        pj1 = wk("pj1", KD * T, 16)
        ot1 = wk("ot1", KD * T, 32)
        fxh, fxl = wk("fxh", KD * T, 96, F32R), wk("fxl", KD * T, 112, F32R)
        pth1, ptl1, ptr1 = wk("pth1", 2 * T, 128, F32R), wk("ptl1", 2 * T, 130, F32R), wk("ptr1", 2 * T, 132)
        post = wk("post", T, 86, I32)
        ang = [wk(f"ang{i}", T, 87 + i) for i in range(4)]

        PS = [ctx.enter_context(nc.psum_tensor(f"ps{i}", [P, 512], F32)) for i in range(8)]

        raw_loaded = [sem(f"raw_loaded{i}") for i in range(RING)]
        hi_ready, lo_ready = sem("hi_ready"), sem("lo_ready")
        mod_used = sem("mod_used")
        slot_used = sem("slot_used")
        evacuated = sem("evacuated")

        def v(name, j=0, n=1):
            return vec[:, bass.ds(VEC[name] + j, n)] if not isinstance(j, int) else \
                vec[:, VEC[name] + j:VEC[name] + j + n]

        def blk(t, j, n=1):
            return t[:, bass.ds(j * T, n * T)] if not isinstance(j, int) else t[:, j * T:(j + n) * T]

        level_banks = ((4, 5), (6, 3))

        def x_quad(n):
            return 4 * (n % 2) + n // 2

        def where(phase, i, r):
            return BASE[phase] + RING * i + r

        block = ctx.enter_context(nc.Block())

        @block.sync
        def _(sp):
            def load(q, r):
                sp.dma_start(RAW[r][:, :], A["weights"][bass.ds(q, 1)].rearrange("a p n -> (a p) n")
                             if not isinstance(q, int) else A["weights"][q]).then_inc(raw_loaded[r], 16)

            def after_mod(q, u):
                sp.wait_ge(mod_used, u + 1)
                load(q, q % RING)

            def after_split(q, s, r=None):
                sp.wait_ge(lo_ready, 2 * s + 2)
                load(q, q % RING if r is None else r)

            for q in range(RING):
                load(q, q)
            for q in range(RING, ROUND + RING):
                after_mod(q, q - RING)
            first = ROUND + RING
            n = (MOD_AT - RING) // RING
            with sp.Fori(0, n) as i:
                for r in range(RING):
                    after_split(i * RING + (first + r), i * RING + r, r)
            for s in range(n * RING, MOD_AT):
                after_split(first + s, s)
            for u in range(ROUND, 3 * ROUND):
                after_mod(MOD_AT + RING + u, u)
            first = 3 * ROUND + RING
            n = (SLOTS - RING - MOD_AT) // RING
            with sp.Fori(0, n) as i:
                for r in range(RING):
                    after_split(i * RING + (first + MOD_AT + r), i * RING + (MOD_AT + r), (MOD_AT + r) % RING)
            for s in range(MOD_AT + n * RING, SLOTS - RING):
                after_split(first + s, s)
            sp.wait_ge(sem("gate1_used"), 1 + KD)
            sp.dma_start(out, R[:, :]).then_inc(sem("stored"), 16)
            sp.wait_ge(sem("stored"), 16)

        @block.scalar
        def _(act):
            def split(phase, i, r, ahead=2):
                t = where(phase, i, r) + ahead
                if isinstance(t, int) and t >= SLOTS:
                    return
                p = BASE[phase] + r + ahead
                if isinstance(i, int):
                    p += RING * i
                    i = 0
                act.wait_ge(raw_loaded[p % RING], 16 * (i + p // RING + 1 + loads_before(p) // RING))
                if not isinstance(t, int) or t >= 2:
                    act.wait_ge(slot_used, t - 1)
                for h in range(2):
                    c = slice(h * SLOT // 2, (h + 1) * SLOT // 2)
                    act.activation(HI[p % PAIR][:, c], RAW[p % RING][:, c], ACT.Copy).then_inc(hi_ready, 1)

            def round_hi(name, dst, src, quads=4, order=lambda q: q):
                for n in range(quads):
                    act.wait_ge(sem("operand_made"), reached("made", name, n + 1))
                    q = order(n)
                    act.activation(blk(dst, 4 * q, 4), blk(src, 4 * q, 4), ACT.Copy).then_inc(sem("operand_hi"), 1)

            def root(name, dst, src, n):
                act.wait_ge(sem("norm_sum"), reached("sum", name, 1))
                act.activation(dst, src, ACT.Sqrt, bias=v("eps"), scale=1.0 / n).then_inc(sem("norm_root"), 1)

            def square(name, dst, src, quads=4):
                for q in range(quads):
                    act.wait_ge(sem("part_ready"), reached("part", name, q + 1))
                    act.activation(blk(dst, 4 * q, 4), blk(src, 4 * q, 4), ACT.Square).then_inc(sem("squares_ready"), 1)

            def mod_rows(n):
                act.wait_ge(mod_used, ROUND * (n + 1))
                act.activation(mrows[n][:, :], PS[7][0:16, :], ACT.Copy).then_inc(sem("mod_rows"), 1)

            act.dma_start(vec[:, :], A["vec"]).then_inc(sem("vec_loaded"), 16)
            act.dma_start(eye[:, :], A["eye"]).then_inc(sem("eye_loaded"), 16)
            act.dma_start(xf[:, :], A["xt"]).then_inc(sem("x_loaded"), 16)
            for dst, name in ((lvl_words, "lvl"), (rep_sel, "rep_sel"), (sel_if, "sel_if"), (w_lr, "w_lr")):
                act.dma_start(dst[:, :], A[name]).then_inc(sem("tables_loaded"), 16)
            act.wait_ge(sem("vec_loaded"), 16)
            act.activation(csil[:, :], v("c2", 0, 2 * KD), ACT.Silu).then_inc(sem("c_act"), 1)
            act.wait_ge(sem("x_loaded"), 16)
            for s in range(2):
                act.activation(sq[s][:, :], blk(xf, KD * s, KD), ACT.Square).then_inc(sem("squares_ready"), 1)
            root("n1", rsx[:, :], PS[2][:, :], D)
            mod_rows(0)
            split("lr", 0, 0, 0)
            split("lr", 0, 1, 0)
            round_hi("x1", xh, xf, 8, x_quad)

            split("lr", 0, 0)
            act.wait_ge(slot_used, BASE["lr"] + 1)
            act.activation(zlr[:, :], PS[0][:, :], ACT.Copy).then_inc(evacuated, 1)
            kview = K[:, :].rearrange("p (s b t) -> p s b t", s=2, b=8)
            for half, scale in ((0, 1.0), (1, DK ** -0.5)):
                for r in range(4):
                    b = 4 * half + r
                    split("key", half, r)
                    act.wait_ge(slot_used, BASE["key"] + b + 1)
                    act.activation(kview[:, :, b, :], PS[b % 2][:, :].rearrange("p (s t) -> p s t", s=2),
                                   ACT.Copy, scale=scale).then_inc(evacuated, 1)
            with act.Fori(0, 2) as i:
                for r in range(8):
                    split("value", 2 * i, r)
                    if r % 4 == 3:
                        act.wait_ge(slot_used, BASE["value"] + 8 * i + r + 1)
                        for tt in range(4):
                            act.activation(V[:, bass.ds(i * 1024 + (tt * 2048 + (r // 4) * 512), 512)],
                                           PS[4 * (r // 4) + tt][:, :], ACT.Copy).then_inc(evacuated, 1)
            for half, scale in ((0, DK ** -0.5), (1, 1.0)):
                for r in range(4):
                    b = 4 * half + r
                    split("query", half, r)
                    act.wait_ge(slot_used, BASE["query"] + b + 1)
                    act.activation(blk(Q, b), PS[b % 2][:, 0:T], ACT.Copy, scale=scale).then_inc(evacuated, 1)
            for half, func in ((0, ACT.Silu), (1, ACT.Sigmoid)):
                with act.Fori(2 * half, 2 * half + 2) as i:
                    for r in range(4):
                        split("gate", i, r)
                        act.wait_ge(slot_used, where("gate", i, r) + 1)
                        act.activation(blk(gates, 4 * i + r), PS[r % 2][:, 0:T], func).then_inc(evacuated, 1)

            act.wait_ge(sem("dec_abs"), 1)
            act.activation(softp[:, :], softp[:, :], ACT.Exp, scale=-1.0).then_inc(sem("dec_exp"), 1)
            act.wait_ge(sem("dec_exp"), 1)
            act.activation(softp[:, :], softp[:, :], ACT.Ln, bias=1.0).then_inc(sem("dec_ln"), 1)
            for d in range(2):
                act.wait_ge(sem("kend_arg"), d + 1)
                act.activation(dec[0][:, :], dec[0][:, :], ACT.Exp, scale=1 / 16.0).then_inc(sem("kend_exp"), 1)
                if d:
                    act.wait_ge(sem("qb_ready"), d)
                act.activation(dec[1][:, :], blk(cumx, 4 * d, 4), ACT.Exp, scale=1 / 16.0).then_inc(sem("qb_exp"), 1)
                for t in range(2):
                    act.wait_ge(sem("kend_turned"), 2 * d + t + 1)
                    act.activation(kend_t[:, t * 512:(t + 1) * 512], PS[t][:, :], ACT.Copy).then_inc(sem("kend_t_ready"), 1)
                for g in range(2):
                    act.wait_ge(sem("state_done"), 2 * d + g + 1)
                    act.activation(state[d][:, g * 512:(g + 1) * 512], PS[2 + g][:, :], ACT.Copy).then_inc(sem("state_ready"), 1)
            NL = len(LEVELS)
            for n in range(2 * NL):
                act.wait_ge(sem("lvl_arg"), n + 1)
                act.activation(dec[n % 2][:, :], dec[n % 2][:, :], ACT.Exp, scale=1 / 16.0).then_inc(sem("lvl_exp"), 1)
                if n % NL == 0:
                    act.wait_ge(sem("lvl_scores"), n + 1)
                    act.activation(cross[n // NL][:, :], PS[4][:, :], ACT.Copy).then_inc(sem("cross_ready"), 1)
            mod_rows(1)
            for h in range(HEADS):
                act.wait_ge(sem("gla_out"), h + 1)
                act.activation(blk(osq, 2 * h, 2), PS[h][:, :], ACT.Square).then_inc(sem("gla_sq"), 1)
            for g in range(2):
                act.wait_ge(sem("gla_sum"), g + 1)
                act.activation(rgrp[:, g * 512:(g + 1) * 512], PS[4 + g][:, :], ACT.Sqrt, bias=v("eps"),
                               scale=1.0 / DV).then_inc(sem("gla_root"), 1)

            act.wait_ge(sem("operand_made"), reached("made", "y", 2))
            act.dma_start(maskn[:, :], A["maskn"]).then_inc(sem("maskn_loaded"), 16)
            act.wait_ge(sem("f_abs"), 1)
            act.activation(rl[:, :], rl[:, :], ACT.Exp, scale=-1.0).then_inc(sem("f_exp"), 1)
            act.wait_ge(sem("f_exp"), 1)
            act.activation(rl[:, :], rl[:, :], ACT.Ln, bias=1.0).then_inc(sem("f_ln"), 1)
            act.wait_ge(sem("m_rows"), 1)
            act.activation(rm[:, 0:T], rm[:, 0:T], ACT.Exp, scale=-1.0).then_inc(sem("em_rows"), 1)
            for n in range(4):
                act.wait_ge(sem("neg_g_rep"), n + 1)
                act.activation(neg_g[:, n * 512:(n + 1) * 512], PS[n][:, :], ACT.Copy).then_inc(sem("neg_g_ready"), 1)
            for n in range(4):
                act.wait_ge(sem("em_rep"), n + 1)
                act.activation(em[:, n * 512:(n + 1) * 512], PS[(4, 5, 6, 3)[n]][:, :], ACT.Copy).then_inc(sem("em_ready"), 1)
            act.wait_ge(sem("g_turned"), 1)
            act.activation(gtok[:, :], PS[0][:, 0:256], ACT.Copy).then_inc(sem("gtok_ready"), 1)
            act.wait_ge(sem("gtok_ready"), 1)
            mod_rows(2)
            act.dma_start(R[:, :], A["xt"][:, 0:KD * T]).then_inc(sem("R_loaded"), 16)
            for n in range(9):
                h, d = n // 2, n % 2
                if n < 8:
                    W = wgt[n % 2]
                    if n >= 2:
                        act.wait_ge(sem("ml_done"), n - 1)
                    for t in range(2, 4):
                        c = t * 64 + 32 * d + h
                        act.activation(W[:, t * T:(t + 1) * T], blk(neg_g, 4 * d + h), ACT.Exp,
                                       bias=gtok[:, c:c + 1]).then_inc(sem("w_ctx"), 1)
                    act.wait_ge(sem("w_arg"), n + 1)
                    act.activation(W[:, 0:2 * T], W[:, 0:2 * T], ACT.Exp).then_inc(sem("w_x"), 1)
                if n >= 2 and d == 0:
                    act.wait_ge(sem("ml_h"), h)
                    act.activation(tmpo[:, :], blk(omix, 2 * h - 2, 2), ACT.Square).then_inc(sem("ml_sq"), 1)
                    act.wait_ge(sem("ml_sum"), h)
                    act.activation(rden[(h - 1) % 2][:, :], PS[7][:, 0:T], ACT.Sqrt, bias=v("eps"),
                                   scale=1.0 / DV).then_inc(sem("ml_root"), 1)
            act.wait_ge(sem("ml_done"), 8)
            round_hi("y", yh, yf)

            for i, r in turns(act, 16):
                split("mix_out", i, r)
            root("n2", rs[:, :], PS[2][:, 0:T], D)
            round_hi("n2", x2h, tn)
            def ff_silu(j, b):
                act.wait_ge(sem("conv"), 9 * j + 9)
                act.activation(sil[b][:, :], acc[b][:, :], ACT.Silu, bias=v("conv_b", j)).then_inc(sem("ff_silu"), 1)

            def ff_hi(j, b):
                act.wait_ge(sem("ff_made"), j + 1)
                act.activation(blk(hh, j), ht[b][:, :], ACT.Copy).then_inc(sem("ff_hi"), 1)

            for i, r in turns(act, 2 * KF, lead=1):
                split("up", i, r)
                j, b = 2 * i + r // 2, r // 2
                first = isinstance(i, int) and i == 0 and r < 2
                if r % 2 == 0:
                    if first:
                        act.wait_ge(sem("pads_zeroed"), 1)
                    else:
                        ff_silu(j - 1, 1 - b)
                    act.wait_ge(slot_used, where("up", i, r) + 1)
                    if not isinstance(i, int) or i:
                        act.wait_ge(sem("ff_silu"), j - 1)
                    act.activation(pad[b][:, :].rearrange("p (y x) -> p y x", x=66)[:, 1:1 + GRID_H, 1:1 + GRID_W],
                                   PS[r][:, 0:T].rearrange("p (y x) -> p y x", x=GRID_W), ACT.Copy).then_inc(sem("pad_ready"), 1)
                    act.activation(acc[b][:, :], PS[r][:, 0:T], ACT.Copy, scale=v("conv_w", 9 * j + 4)).then_inc(sem("gate_used"), 1)
                elif not first:
                    ff_hi(j - 1, 1 - b)
            ff_silu(KF - 1, 0)
            ff_hi(KF - 1, 0)
            for i, r in turns(act, KF):
                split("down", i, r)
            square("nf", tn, R)
            root("nf", rs[:, :], PS[2][:, 0:T], D)
            square("np", tn, R)
            root("np", rs[:, :], PS[2][:, 0:T], D)
            round_hi("np", xph, pnt)

            for g in range(4):
                with act.Fori(2 * g, 2 * g + 2) as i:
                    for r in range(4):
                        split("pool_in", i, r)
                        u = 4 * i + r
                        act.wait_ge(slot_used, where("pool_in", i, r) + 1)
                        if g == 0 and r == 0:
                            act.wait_ge(sem("ups_zeroed"), 1)
                        act.activation(up[r % 2][:, 16:UPW], PS[r % 2][:, 0:T], ACT.Copy).then_inc(evacuated, 1)
                        act.wait_ge(sem("pool_made"), u + 1)
                        act.activation(blk(ph, u), pf[:, :], ACT.Copy).then_inc(sem("pool_hi"), 1)
            with act.Fori(8, 16) as i:
                for r in range(4):
                    split("pool_in", i, r)
                    act.wait_ge(slot_used, where("pool_in", i, r) + 1)
                    act.activation(blk(sg, 4 * i + (r - 32)), PS[r % 2][:, 0:T], ACT.Silu).then_inc(evacuated, 1)
            for i, r in turns(act, 16):
                split("group", i, r)
                s = 4 * i + r
                act.wait_ge(evacuated, EVAC["group"] + s + 1)
                act.activation(blk(y2h, 2 * s, 2), gt[r % 2][:, :], ACT.Copy).then_inc(sem("y2_hi"), 1)
            for i, r in turns(act, 32):
                split("pool_out", i, r)
            for b in range(8):
                act.wait_ge(sem("O_copied"), b + 1)
                act.activation(blk(ot, 2 * b, 2), blk(O, 2 * b, 2), ACT.Square).then_inc(sem("squares_ready"), 1)

            def p_operand(tag, ptr, pth):
                act.dma_start(ptr[:, :], A["pt"][:, tag * 2 * T:(tag + 1) * 2 * T]).then_inc(sem(f"p{tag}_loaded"), 16)
                act.wait_ge(sem(f"p{tag}_loaded"), 16)
                act.activation(pth[:, :], ptr[:, :], ACT.Copy).then_inc(sem(f"p{tag}_hi"), 1)

            def proj(tag, pj):
                for s in range(2):
                    split(f"proj{tag}", 0, s)
                    act.wait_ge(slot_used, BASE[f"proj{tag}"] + s + 1)
                    for b in range(4):
                        ins = act.activation(blk(pj, 8 * s + 2 * b, 2), PS[4 + b][:, :], ACT.Copy)
                    ins.then_inc(evacuated, 1)

            def gate(tag, tail=0):
                name = f"plegate{tag}"
                for i, r in turns(act, 16, tail):
                    split(name, i, r)
                    act.wait_ge(slot_used, where(name, i, r) + 1)
                    act.wait_ge(sem(f"gate{tag}_used"), 4 * i + r)
                    act.activation(sgt[r % 2][:, :], PS[r % 2][:, 0:T], ACT.Sigmoid).then_inc(evacuated, 1)

            p_operand(0, ptr0, pth0)
            proj(0, pj0)
            root("post0", rs[:, :], PS[2][:, 0:T], D)
            square("ple0", ot, R)
            root("ple0", rs[:, :], PS[2][:, 0:T], D)
            round_hi("ple0", gxh, ot)
            gate(0)

            act.dma_start(post[:, :], A["pos"]).then_inc(sem("pos_loaded"), 16)
            root("m", rs[:, :], PS[2][:, 0:T], D)
            round_hi("m", xmh, mnt)
            act.wait_ge(sem("ang_ready"), 1)
            act.activation(cs[:, T:2 * T], ang[0][:, :], ACT.Sin).then_inc(sem("rope_cs"), 1)
            act.activation(cs[:, 0:T], ang[1][:, :], ACT.Sin, bias=v("halfpi"), scale=-1.0).then_inc(sem("rope_cs"), 1)
            for j in range(10):
                split("mla_in", j // 4, j % 4)
                act.wait_ge(slot_used, BASE["mla_in"] + j + 1)
                act.activation(blk(ql, j) if j < 8 else blk(kpr, j - 8), PS[j % 2][:, 0:T], ACT.Copy).then_inc(evacuated, 1)
            for j in range(10, 26):
                split("mla_in", j // 4, j % 4)
                act.wait_ge(slot_used, BASE["mla_in"] + j + 1)
                act.activation(blk(sg2, j - 10), PS[j % 2][:, 0:T], ACT.Silu).then_inc(evacuated, 1)
            root("q", rs[:, :], PS[2][:, 0:T], 512)
            root("kv", rsk[:, :], PS[3][:, 0:T], 512)
            round_hi("lat", lath, ql, 2)
            for s in range(6):
                split("uq", s // 4, s % 4)
                act.wait_ge(slot_used, BASE["uq"] + s + 1)
                if s == 5:
                    act.wait_ge(sem("q_rot"), 1)
                for b in range(2):
                    dst = blk(qn, 4 * s + 2 * b, 2) if s < 4 else blk(qraw, 2 * b, 2)
                    ins = act.activation(dst, PS[2 * (s % 2) + b][:, :], ACT.Copy)
                ins.then_inc(evacuated, 1)
            for s in range(4):
                split("uk", 0, s)
                act.wait_ge(slot_used, BASE["uk"] + s + 1)
                for b in range(2):
                    ins = act.activation(blk(kn, 4 * s + 2 * b, 2), PS[2 * (s % 2) + b][:, :], ACT.Copy)
                ins.then_inc(evacuated, 1)
            for s in range(4):
                split("uv", 0, s)
                act.wait_ge(slot_used, BASE["uv"] + s + 1)
                for t in range(2):
                    ins = act.activation(v2[:, t * 2048 + s * 512:t * 2048 + (s + 1) * 512], PS[2 * (s % 2) + t][:, :], ACT.Copy)
                ins.then_inc(evacuated, 1)
            act.dma_start(maska[:, :], A["maska"]).then_inc(sem("maska_loaded"), 16)
            for n in range(NH + 2):
                if n < NH:
                    b = n % 2
                    act.wait_ge(sem("s_max"), n + 1)
                    if n >= 2:
                        act.wait_ge(sem("p_turned"), n - 1)
                    for t, c in ((0, slice(0, P)), (1, slice(P, 3 * P))):
                        act.activation(p_[b][:, c], s_[b][:, c], ACT.Exp, bias=stat[:, 8 * n + t:8 * n + t + 1],
                                       scale=SM_SCALE, accum_out=stat[:, 8 * n + 2 + t:8 * n + 3 + t]).then_inc(sem("p_exp"), 1)
                if 1 <= n <= NH:
                    h = n - 1
                    act.wait_ge(sem("p_turned"), h + 1)
                    if h >= 2:
                        act.wait_ge(sem("pv_done"), h - 1)
                    act.activation(pt[h % 2][:, :], PS[4 + h % 2][:, 0:3 * P], ACT.Copy).then_inc(sem("pt_ready"), 1)
                if n >= 2:
                    h = n - 2
                    act.wait_ge(sem("o_made"), h + 1)
                    act.activation(blk(y3h, h), yt[h % 2][:, :], ACT.Copy).then_inc(sem("y3_hi"), 1)
            for i, r in turns(act, 16):
                split("mla_out", i, r)
                act.wait_ge(slot_used, where("mla_out", i, r) + 1)
                act.activation(blk(O, 4 * i + r), PS[r % 2][:, 0:T], ACT.Copy).then_inc(evacuated, 1)
            p_operand(1, ptr1, pth1)
            proj(1, pj1)
            root("post1", rs[:, :], PS[2][:, 0:T], D)
            square("ple1", ot1, R)
            root("ple1", rs[:, :], PS[2][:, 0:T], D)
            round_hi("ple1", fxh, ot1)
            gate(1, tail=4)

        @block.vector
        def _(dve):
            own = Steps(dve, sem("vector_steps"))

            def split(phase, i, r, ahead=2):
                t = where(phase, i, r) + ahead
                if isinstance(t, int) and t >= SLOTS:
                    return
                p = BASE[phase] + r + ahead
                for h in range(2):
                    c = slice(h * SLOT // 2, (h + 1) * SLOT // 2)
                    dve.wait_ge(hi_ready, 2 * t + h + 1)
                    dve.tensor_tensor(LO[p % PAIR][:, c], RAW[p % RING][:, c], HI[p % PAIR][:, c].bitcast(F32),
                                      ALU.subtract).then_inc(lo_ready, 1)

            def recip(name, dst):
                dve.wait_ge(sem("norm_root"), reached("root", name, 1))
                own.done(dve.reciprocal(dst, dst))
                own.wait()

            def rest(name, q, hi, lo, src, at=None):
                dve.wait_ge(sem("operand_hi"), reached("hi", name, q + 1))
                q = q if at is None else at
                dve.tensor_tensor(blk(lo, 4 * q, 4), blk(src, 4 * q, 4), blk(hi, 4 * q, 4).bitcast(F32),
                                  ALU.subtract).then_inc(sem("operand_rest"), 1)

            def normed(name, src, gain, dst, hi, lo, inv=None, shift=None, quads=4):
                for q in range(quads + 1):
                    if q < quads:
                        for b in range(4 * q, 4 * q + 4):
                            ins = dve.scalar_tensor_tensor(blk(dst, b), blk(src, b), gain(b),
                                                           (inv(b) if inv else rs)[:, :], ALU.mult, ALU.mult)
                            if shift:
                                own.done(ins)
                        if shift:
                            own.wait()
                            for b in range(4 * q, 4 * q + 4):
                                ins = dve.tensor_scalar(blk(dst, b), blk(dst, b), shift(b), None, ALU.add)
                        ins.then_inc(sem("operand_made"), 1)
                    if q:
                        rest(name, q - 1, hi, lo, dst)

            def accumulate(st, src, tmp, total=ssq):
                st.start()
                st.done(dve.tensor_tensor(tmp[:, :], src, src, ALU.mult))
                st.wait()
                st.done(dve.tensor_tensor(total[:, :], total[:, :], tmp[:, :], ALU.add))

            def add_squares(name, src, count=4):
                dve.wait_ge(sem("squares_ready"), reached("squares", name, count))
                dve.tensor_reduce(ssq[:, :], src[:, 0:KD * T].rearrange("p (k t) -> p t k", t=T), AX,
                                  ALU.add).then_inc(sem("ssq_ready"), 1)

            def clear_ssq():
                own.done(dve.memset(ssq[:, :], 0.0))
                own.wait()

            dve.memset(ones[:, :], 1.0).then_inc(sem("ones_ready"), 1)
            own.done(dve.memset(cwin[:, :], 0.0))
            own.wait()
            dve.wait_ge(sem("c_act"), 1)
            mid = 2 * MGROUPS - 2
            dve.tensor_copy(cwin[:, :].rearrange("p (k w) -> p k w", w=MW)[:, :, mid:mid + 2],
                            csil[:, :].rearrange("p (k s) -> p k s", s=2)).then_inc(sem("c_ready"), 1)
            for s in range(2):
                dve.wait_ge(sem("squares_ready"), reached("squares", "n1", s + 1))
                dve.tensor_reduce(ssqx[:, s * T:(s + 1) * T], sq[s][:, :].rearrange("p (k t) -> p t k", t=T), AX,
                                  ALU.add).then_inc(sem("ssq_ready"), 1)
            recip("n1", rsx[:, :])
            for s in range(2):
                xs = blk(xf, KD * s, KD).rearrange("p (k t) -> p k t", t=T)
                own.done(dve.tensor_tensor(xs, xs, rsx[:, s * T:(s + 1) * T][:, None, :].to_broadcast([P, KD, T]), ALU.mult))
            mview = mods[:, :].rearrange("p (j s) -> p j s", s=2)

            def modulation(n):
                dve.wait_ge(sem("mod_turned"), n + 1)
                own.wait()
                w = 4 * MGROUPS
                dve.tensor_tensor(mview[:, w * n:w * (n + 1), :].rearrange("p (g q) s -> p g q s", q=4),
                                  PS[7 if n == 2 else 6][:, 0:2 * w].rearrange("p (q g s) -> p g q s", q=4, s=2),
                                  v("b_mod", w * n, w).rearrange("p (g q) -> p g q", q=4)[:, :, :, None].to_broadcast([P, MGROUPS, 4, 2]),
                                  ALU.add).then_inc(sem("mods_ready"), 1)
                dve.wait_ge(sem("mods_ready"), n + 1)

            def gains(n, j, s, g):
                own.done(dve.scalar_tensor_tensor(amod[:, n * KD:(n + 1) * KD], mview[:, j:j + KD, s], 1.0,
                                                  v(g, 0, KD), ALU.add, ALU.mult))
            modulation(0)
            gains(0, 16, 0, "g1")
            gains(1, 16, 1, "g1")
            own.wait()
            for n in range(9):
                if n < 8:
                    for b in range(4 * (n // 2), 4 * (n // 2) + 4):
                        f, k = (n % 2) * KD + b, b
                        ins = dve.tensor_scalar(blk(xf, f), blk(xf, f), amod[:, f:f + 1], mview[:, k, n % 2:n % 2 + 1],
                                                ALU.mult, ALU.add)
                    ins.then_inc(sem("operand_made"), 1)
                if n:
                    rest("x1", n - 1, xh, xl, xf, x_quad(n - 1))
                if n == 1:
                    split("lr", 0, 0, 0)
                    split("lr", 0, 1, 0)
            for name in ("lr", "key", "value", "query", "gate"):
                for i, r in turns(dve, COUNT[name]):
                    split(name, i, r)

            for n in range(8):
                dve.wait_ge(sem("dec_z"), n + 1)
                own.done(dve.tensor_scalar(loga[:, n * 512:(n + 1) * 512], PS[n][:, :], v("lr_b", n), None, ALU.add))
            own.wait()
            dve.scalar_tensor_tensor(softp[:, :], loga[:, :], -1.0, loga[:, :], ALU.mult, ALU.max).then_inc(sem("dec_abs"), 1)
            dve.wait_ge(sem("dec_ln"), 1)
            own.done(dve.scalar_tensor_tensor(loga[:, :], loga[:, :], 0.0, softp[:, :], ALU.min, ALU.subtract))
            own.wait()
            for n in range(8):
                step = 1 if n < 4 else -1
                for s, dst in ((0, cumx), (1, cumc)):
                    src = loga[:, n * 512 + s * T:n * 512 + (s + 1) * T][:, ::step]
                    own.done(dve.tensor_tensor_scan(blk(dst, n)[:, ::step], src, src, 0.0, ALU.add, ALU.bypass))
            own.wait()
            qg, kg = Q[:, 0:4 * T], K[:, 0:4 * T]
            for d in range(2):
                end = T - 1 if d == 0 else 0
                if d:
                    dve.wait_ge(sem("kend_ready"), d)
                cc = blk(cumc, 4 * d, 4).rearrange("p (h t) -> p h t", t=T)
                dve.tensor_tensor(dec[0][:, :].rearrange("p (h t) -> p h t", t=T),
                                  cc[:, :, end:end + 1].to_broadcast([P, 4, T]), cc, ALU.subtract).then_inc(sem("kend_arg"), 1)
                dve.wait_ge(sem("kend_exp"), d + 1)
                if d:
                    dve.wait_ge(sem("kend_turned"), 2 * d)
                dve.tensor_tensor(kend[:, :], dec[0][:, :], K[:, 8 * T:12 * T], ALU.mult).then_inc(sem("kend_ready"), 1)
                dve.wait_ge(sem("qb_exp"), d + 1)
                dve.tensor_tensor(qb[d][:, :], dec[1][:, :], qg, ALU.mult).then_inc(sem("qb_ready"), 1)
            dve.wait_ge(sem("qb_ready"), 2)
            dve.wait_ge(sem("eye_loaded"), 16)
            for g in range(2):
                dve.wait_ge(sem("diag_done"), g + 1)
                for d in range(2):
                    ins = dve.tensor_tensor(att[d][:, g * 512:(g + 1) * 512].rearrange("p (a j) -> p a j", j=P),
                                            PS[4 + g][:, :].rearrange("p (a j) -> p a j", j=P),
                                            eye[:, :][:, None, :].to_broadcast([P, 4, P]), ALU.mult)
                    ins.then_inc(sem("diag_used"), 1)
            dve.wait_ge(sem("diag_used"), 4)
            dve.wait_ge(sem("tables_loaded"), 64)
            NL = len(LEVELS)
            for n in range(2 * NL + 1):
                if n < 2 * NL:
                    d, x = n // NL, LEVELS[n % NL]
                    qh, kh, ref = (1, 0, x - 1) if d == 0 else (0, 1, x)

                    def half(t, w):
                        return t.rearrange("p (b c x) -> p b c x", c=2, x=x)[:, :, w, :]
                    cum = blk(cumx, 4 * d, 4)
                    rv = cum.rearrange("p (b x) -> p b x", x=2 * x)[:, :, ref:ref + 1].to_broadcast([P, 2 * T // x, x])
                    if n >= 2:
                        dve.wait_ge(sem("lvl_ops"), n - 1)
                    dve.tensor_tensor(half(dec[n % 2][:, :], qh), half(cum, qh), rv, ALU.subtract)
                    dve.tensor_tensor(half(dec[n % 2][:, :], kh), rv, half(cum, kh), ALU.subtract).then_inc(sem("lvl_arg"), 1)
                if n >= 1 and (n - 1) % NL:
                    m = n - 1
                    d1, l1 = m // NL, m % NL
                    dve.wait_ge(sem("lvl_scores"), m + 1)
                    mask = lvl[:, (7 * d1 + l1 - 1) * P:(7 * d1 + l1) * P][:, None, :].to_broadcast([P, 4, P])
                    for g in range(2):
                        ins = dve.copy_predicated(att[d1][:, g * 512:(g + 1) * 512].rearrange("p (a j) -> p a j", j=P), mask,
                                                  PS[level_banks[m % 2][g]][:, :].rearrange("p (a j) -> p a j", j=P))
                        ins.then_inc(sem("lvl_merged"), 1)
                    dve.wait_ge(sem("lvl_merged"), 2 * (m - m // NL))
                if n < 2 * NL:
                    dve.wait_ge(sem("lvl_exp"), n + 1)
                    if n >= 2:
                        dve.wait_ge(sem("lvl_scores"), n - 1)
                    dve.tensor_tensor(half(qk[n % 2][:, :], qh), half(dec[n % 2][:, :], qh), half(qg, qh), ALU.mult)
                    dve.tensor_tensor(half(qk[n % 2][:, :], kh), half(dec[n % 2][:, :], kh), half(kg, kh),
                                      ALU.mult).then_inc(sem("lvl_ops"), 1)
            modulation(1)
            for g in range(2):
                dve.wait_ge(sem("gla_root"), g + 1)
                own.done(dve.reciprocal(rgrp[:, g * 512:(g + 1) * 512], rgrp[:, g * 512:(g + 1) * 512]))
                own.wait()
                for b in range(4 * g, 4 * g + 4):
                    own.done(dve.scalar_tensor_tensor(blk(yf, b), PS[b // 2][:, (b % 2) * T:(b % 2 + 1) * T],
                                                      v("gla_g", b % 2), blk(rgrp, b // 2), ALU.mult, ALU.mult))
                own.wait()
                dve.tensor_tensor(blk(yf, 4 * g, 4), blk(yf, 4 * g, 4), blk(gates, 4 * g, 4), ALU.mult).then_inc(sem("operand_made"), 1)

            dve.wait_ge(sem("if_rows"), 1)
            own.done(dve.tensor_scalar(ri[:, :], PS[5][0:64, :], v("gate_b", 0)[0:64, :], None, ALU.add))
            own.done(dve.tensor_scalar(rf[:, :], PS[6][0:64, :], v("gate_b", 1)[0:64, :], None, ALU.add))
            own.wait()
            dve.scalar_tensor_tensor(rl[:, :], rf[:, :], -1.0, rf[:, :], ALU.mult, ALU.max).then_inc(sem("f_abs"), 1)
            dve.wait_ge(sem("f_ln"), 1)
            own.done(dve.scalar_tensor_tensor(rf[:, :], rf[:, :], 0.0, rl[:, :], ALU.min, ALU.subtract))
            own.wait()

            def scan(dst, src, op):
                for row, st in ((0, 1), (32, -1)):
                    a = src[row:row + 32, T:2 * T][:, ::st]
                    own.done(dve.tensor_tensor_scan(dst[row:row + 32, T:2 * T][:, ::st], a, a, 0.0, op, ALU.bypass))
                own.wait()
                for row, st, last in ((0, 1, 2 * T - 1), (32, -1, T)):
                    a = src[row:row + 32, 0:T][:, ::st]
                    own.done(dve.tensor_tensor_scan(dst[row:row + 32, 0:T][:, ::st], a, a,
                                                    dst[row:row + 32, last:last + 1], op, ALU.bypass))
                own.wait()
            scan(rl, rf, ALU.add)
            own.done(dve.tensor_tensor(rg[:, :], ri[:, :], rl[:, :], ALU.subtract))
            own.wait()
            scan(rm, rg, ALU.max)
            own.done(dve.tensor_scalar(ri[:, 0:T], rm[:, 0:T], -1.0, None, ALU.mult))
            own.wait()
            dve.tensor_tensor(rm[:, 0:T], rm[:, 0:T], rl[:, 0:T], ALU.add).then_inc(sem("m_rows"), 1)
            dve.wait_ge(sem("maskn_loaded"), 16)
            dve.wait_ge(sem("gtok_ready"), 1)
            modulation(2)
            gains(2, 64, 0, "g2")
            for n in range(9):
                if n < 8:
                    h, d = n // 2, n % 2
                    W = wgt[n % 2]
                    if n >= 2:
                        dve.wait_ge(sem("ml_done"), n - 1)
                    for t in range(2):
                        c = t * 64 + 32 * d + h
                        ins = dve.scalar_tensor_tensor(W[:, t * T:(t + 1) * T], blk(neg_g, 4 * d + h), gtok[:, c:c + 1],
                                                       blk(maskn, 2 * d + t), ALU.add, ALU.add)
                    ins.then_inc(sem("w_arg"), 1)
                    dve.wait_ge(sem("w_x"), n + 1)
                    dve.wait_ge(sem("ml_scores"), h + 1)
                    for g in range(2):
                        ins = dve.tensor_tensor(W[:, g * 512:(g + 1) * 512], W[:, g * 512:(g + 1) * 512],
                                                PS[2 * (h % 2) + g][:, :], ALU.mult)
                    ins.then_inc(sem("ml_w"), 1)
                if n >= 1:
                    m = n - 1
                    h, d = m // 2, m % 2
                    dve.wait_ge(sem("ml_done"), m + 1)
                    den = PS[6][:, 0:T]
                    own.done(dve.tensor_tensor(rden[d][:, :], den, blk(em, 4 * d + h), ALU.max))
                    own.wait()
                    own.done(dve.scalar_tensor_tensor(rden[d][:, :], den, -1.0, rden[d][:, :], ALU.mult, ALU.max))
                    own.wait()
                    own.done(dve.reciprocal(rden[d][:, :], rden[d][:, :]))
                    own.wait()
                    o2 = blk(omix, 2 * h, 2).rearrange("p (a t) -> p a t", t=T)
                    t2 = tmpo[:, :].rearrange("p (a t) -> p a t", t=T)
                    n2 = PS[4 + d][:, :].rearrange("p (a t) -> p a t", t=T)
                    rb = rden[d][:, :][:, None, :].to_broadcast([P, 2, T])
                    if d == 0:
                        dve.tensor_tensor(o2, n2, rb, ALU.mult).then_inc(sem("ml_taken"), 1)
                        continue
                    dve.tensor_tensor(t2, n2, rb, ALU.mult).then_inc(sem("ml_taken"), 1)
                    dve.wait_ge(sem("ml_taken"), m + 1)
                    dve.tensor_tensor(o2, o2, t2, ALU.add).then_inc(sem("ml_h"), 1)
                    dve.wait_ge(sem("ml_root"), h + 1)
                    own.done(dve.reciprocal(rden[h % 2][:, :], rden[h % 2][:, :]))
                    own.wait()
                    for a in range(2):
                        own.done(dve.scalar_tensor_tensor(blk(yf, 8 + 2 * h + a), blk(omix, 2 * h + a), v("ml_g", a),
                                                          rden[h % 2][:, :], ALU.mult, ALU.mult))
                    own.wait()
                    ins = dve.tensor_tensor(blk(yf, 8 + 2 * h, 2), blk(yf, 8 + 2 * h, 2), blk(gates, 8 + 2 * h, 2), ALU.mult)
                    if h % 2:
                        ins.then_inc(sem("operand_made"), 1)
                    else:
                        own.done(ins)
            for q in range(4):
                rest("y", q, yh, yl, yf)

            clear_ssq()
            dve.wait_ge(sem("R_loaded"), 16)
            for i, r in turns(dve, 16):
                split("mix_out", i, r)
                u = 4 * i + r
                dve.wait_ge(slot_used, where("mix_out", i, r) + 1)
                dve.scalar_tensor_tensor(blk(R, u), PS[r % 2][:, 0:T], mods[:, bass.ds(64 + 2 * u, 1)], blk(R, u),
                                         ALU.mult, ALU.add).then_inc(evacuated, 1)
                dve.wait_ge(evacuated, EVAC["mix_out"] + u + 1)
                accumulate(Steps(dve, sem("square_steps"), reached("steps", "n2") + 2 * u), blk(R, u), tmpx)
            recip("n2", rs[:, :])
            normed("n2", R, lambda b: amod[:, 2 * KD + b:2 * KD + b + 1], tn, x2h, x2l,
                   shift=lambda b: mview[:, 48 + b, 0:1])
            own.done(dve.memset(pad[0][:, :], 0.0))
            dve.memset(pad[1][:, :], 0.0).then_inc(sem("pads_zeroed"), 1)

            def ff_product(j, b):
                dve.wait_ge(sem("ff_silu"), j + 1)
                dve.wait_ge(slot_used, BASE["up"] + 2 * j + 2)
                if not isinstance(j, int) or j >= 2:
                    dve.wait_ge(sem("ff_x"), j - 1)
                dve.tensor_tensor(ht[b][:, :], sil[b][:, :], PS[2 * b + 1][:, 0:T], ALU.mult).then_inc(sem("ff_made"), 1)

            def ff_rest(j, b):
                dve.wait_ge(sem("ff_hi"), j + 1)
                dve.tensor_tensor(blk(hl, j), ht[b][:, :], blk(hh, j).bitcast(F32), ALU.subtract).then_inc(sem("ff_x"), 1)

            TAPS = ((accb, 0), (acc, 1), (accb, 2), (acc, 3), (accb, 6), (acc, 5), (accb, 8), (acc, 7))

            def conv(j, b, steps):
                pv = pad[b][:, :].rearrange("p (y x) -> p y x", x=66)
                for n in steps:
                    if n >= 2:
                        dve.wait_ge(sem("conv"), 9 * j + (n if n == 8 else n - 1))
                    if n == 8:
                        dve.tensor_tensor(acc[b][:, :], acc[b][:, :], accb[b][:, :], ALU.add).then_inc(sem("conv"), 1)
                        continue
                    total, t = TAPS[n]
                    a3 = total[b][:, :].rearrange("p (y x) -> p y x", x=GRID_W)
                    window = pv[:, t // 3:t // 3 + GRID_H, t % 3:t % 3 + GRID_W]
                    tap = v("conv_w", 9 * j + t)
                    ins = dve.tensor_scalar(a3, window, tap, None, ALU.mult) if n == 0 else \
                        dve.scalar_tensor_tensor(a3, window, tap, a3, ALU.mult, ALU.add)
                    ins.then_inc(sem("conv"), 1)

            for i, r in turns(dve, 2 * KF, lead=1):
                split("up", i, r)
                j, b = 2 * i + r // 2, r // 2
                first = isinstance(i, int) and i == 0 and r < 2
                if r % 2 == 0:
                    if not first:
                        ff_product(j - 1, 1 - b)
                    dve.wait_ge(sem("gate_used"), j + 1)
                    if not isinstance(j, int) or j >= 2:
                        dve.wait_ge(sem("conv"), 9 * j - 9)
                    conv(j, b, range(5))
                else:
                    conv(j, b, range(5, 9))
                    if not first:
                        ff_rest(j - 1, 1 - b)
            ff_product(KF - 1, 0)
            ff_rest(KF - 1, 0)
            for i, r in turns(dve, KF):
                split("down", i, r)
            dve.wait_ge(slot_used, BASE["down"] + KF)
            for b in range(KD):
                ins = dve.scalar_tensor_tensor(blk(R, b), PS[b // 2][:, (b % 2) * T:(b % 2 + 1) * T],
                                               mods[:, 160 + 2 * b:161 + 2 * b], blk(R, b), ALU.mult, ALU.add)
                if b % 4 == 3:
                    ins.then_inc(sem("part_ready"), 1)
            add_squares("nf", tn)
            recip("nf", rs[:, :])
            for b in range(KD):
                ins = dve.scalar_tensor_tensor(blk(R, b), blk(R, b), v("gfin", b), rs[:, :], ALU.mult, ALU.mult)
                if b % 4 == 3:
                    ins.then_inc(sem("part_ready"), 1)
            add_squares("np", tn)
            recip("np", rs[:, :])
            dve.wait_ge(sem("part_ready"), reached("part", "np", 4))
            normed("np", R, lambda b: v("pre0", b), pnt, xph, xpl)
            for t in (up[0], up[1], ws[0]):
                own.done(dve.memset(t[:, :], 0.0))
            dve.memset(ws[1][:, :], 0.0).then_inc(sem("ups_zeroed"), 1)
            dve.wait_ge(sem("ups_zeroed"), 1)

            for g in range(4):
                with dve.Fori(2 * g, 2 * g + 2) as i:
                    for r in range(4):
                        split("pool_in", i, r)
                        u = 4 * i + r
                        st = Steps(dve, sem("window_steps"), 8 * sum(range(2, g + 2)) + (g + 2) * (u - 8 * g))
                        dve.wait_ge(evacuated, EVAC["pool_in"] + u + 1)
                        dve.wait_ge(sem("pool_x"), u)
                        src = up[r % 2]
                        for l in range(g + 1):
                            dst, lag = ws[l % 2], 1 << l
                            st.done(dve.tensor_tensor(dst[:, 16:UPW], src[:, 16:UPW], src[:, 16 - lag:UPW - lag], ALU.add))
                            st.wait()
                            src = dst
                        st.done(dve.tensor_tensor(src[:, 16:32], src[:, 16:32], v("corr", 16 * g, 16), ALU.mult))
                        st.wait()
                        dve.scalar_tensor_tensor(pf[:, :], src[:, 16:UPW], 1.0 / WINDOWS[g], up[r % 2][:, 16:UPW],
                                                 ALU.mult, ALU.subtract).then_inc(sem("pool_made"), 1)
                        dve.wait_ge(sem("pool_hi"), u + 1)
                        dve.tensor_tensor(blk(pl, u), pf[:, :], blk(ph, u).bitcast(F32), ALU.subtract).then_inc(sem("pool_x"), 1)
            with dve.Fori(8, 16) as i:
                for r in range(4):
                    split("pool_in", i, r)
            dve.wait_ge(evacuated, EVAC["group"])
            for i, r in turns(dve, 16):
                split("group", i, r)
                s = 4 * i + r
                dve.wait_ge(slot_used, where("group", i, r) + 1)
                dve.wait_ge(sem("y2_x"), s)
                for a in range(2):
                    ins = dve.scalar_tensor_tensor(gt[r % 2][:, a * T:(a + 1) * T], PS[r % 2][:, a * T:(a + 1) * T],
                                                   vec[:, bass.ds(2 * s + (VEC["pscale"] + a), 1)], blk(sg, 2 * s + a),
                                                   ALU.mult, ALU.mult)
                ins.then_inc(evacuated, 1)
                dve.wait_ge(sem("y2_hi"), s + 1)
                dve.tensor_tensor(blk(y2l, 2 * s, 2), gt[r % 2][:, :], blk(y2h, 2 * s, 2).bitcast(F32),
                                  ALU.subtract).then_inc(sem("y2_x"), 1)
            for i, r in turns(dve, 32):
                split("pool_out", i, r)
            dve.wait_ge(slot_used, BASE["pool_out"] + 32)
            for b in range(8):
                dve.tensor_copy(blk(O, 2 * b, 2), PS[b][:, :]).then_inc(sem("O_copied"), 1)
            add_squares("post0", ot, 8)

            def p_rest(tag, ptr, pth, ptl):
                dve.wait_ge(sem(f"p{tag}_hi"), 1)
                dve.tensor_tensor(ptl[:, :], ptr[:, :], pth[:, :].bitcast(F32), ALU.subtract).then_inc(sem(f"p{tag}_x"), 1)

            def after_block(tag, o_t, xh_, xl_):
                recip(f"post{tag}", rs[:, :])
                for q in range(4):
                    for b in range(4 * q, 4 * q + 4):
                        own.done(dve.scalar_tensor_tensor(blk(O, b), blk(O, b), v(f"post{tag}", b), rs[:, :], ALU.mult, ALU.mult))
                    own.wait()
                    dve.tensor_tensor(blk(R, 4 * q, 4), blk(R, 4 * q, 4), blk(O, 4 * q, 4), ALU.add).then_inc(sem("part_ready"), 1)
                add_squares(f"ple{tag}", o_t)
                recip(f"ple{tag}", rs[:, :])
                normed(f"ple{tag}", R, lambda b: v(f"ple{tag}", b), o_t, xh_, xl_)

            def gated(tag, pj, per, tail=0):
                dve.memset(ssq[:, :], 0.0).then_inc(sem(f"gate{tag}_used"), 1)
                dve.wait_ge(sem(f"gate{tag}_used"), 1)
                for i, r in turns(dve, 16, tail):
                    split(f"plegate{tag}", i, r)
                    u = 4 * i + r
                    dve.wait_ge(evacuated, EVAC[f"plegate{tag}"] + u + 1)
                    dve.tensor_tensor(sgt[r % 2][:, :], sgt[r % 2][:, :], blk(pj, u), ALU.mult).then_inc(sem(f"gate{tag}_mult"), 1)
                    dve.wait_ge(sem(f"gate{tag}_mult"), u + 1)
                    dve.tensor_tensor(blk(R, u), blk(R, u), sgt[r % 2][:, :], ALU.add).then_inc(sem(f"gate{tag}_used"), 1)
                    if per:
                        dve.wait_ge(sem(f"gate{tag}_used"), u + 2)
                        accumulate(Steps(dve, sem("square_steps"), reached("steps", "m") + 2 * u), blk(R, u), tmpg)

            p_rest(0, ptr0, pth0, ptl0)
            for s in range(2):
                split("proj0", 0, s)
            after_block(0, ot, gxh, gxl)
            gated(0, pj0, 2)

            dve.wait_ge(sem("pos_loaded"), 16)
            own.done(dve.tensor_copy(ang[2][:, :], post[:, :]))
            own.wait()
            own.done(dve.tensor_scalar(ang[0][:, :], ang[2][:, :], v("invf"), None, ALU.mult))
            own.wait()
            own.done(dve.tensor_scalar(ang[3][:, :], ang[0][:, :], float(1 / (2 * np.pi)), None, ALU.mult))
            own.wait()
            own.done(dve.tensor_scalar(ang[3][:, :], ang[3][:, :], 12582912.0, None, ALU.add))
            own.wait()
            own.done(dve.tensor_scalar(ang[3][:, :], ang[3][:, :], -12582912.0, None, ALU.add))
            own.wait()
            for part in TWO_PI:
                own.done(dve.scalar_tensor_tensor(ang[0][:, :], ang[3][:, :], -part, ang[0][:, :], ALU.mult, ALU.add))
                own.wait()
            own.done(dve.tensor_scalar(ang[0][:, :], ang[0][:, :], 3.1415925, -3.1415925, ALU.min, ALU.max))
            own.wait()
            dve.scalar_tensor_tensor(ang[1][:, :], ang[0][:, :], -1.0, ang[0][:, :], ALU.mult, ALU.max).then_inc(sem("ang_ready"), 1)
            recip("m", rs[:, :])
            normed("m", R, lambda b: v("pre1", b), mnt, xmh, xml)
            own.done(dve.memset(ssqk[:, :], 0.0))
            clear_ssq()

            def rotate(d1, d2, x1, x2, signal=None):
                cos, sin = cs[:, 0:T], cs[:, T:2 * T]
                own.wait()
                for n, (a, c) in enumerate(((x1, cos), (x2, sin), (x2, cos), (x1, sin))):
                    own.done(dve.tensor_tensor(rt[n][:, :], a, c, ALU.mult))
                own.wait()
                own.done(dve.tensor_tensor(d1, rt[0][:, :], rt[1][:, :], ALU.subtract))
                ins = dve.tensor_tensor(d2, rt[2][:, :], rt[3][:, :], ALU.add)
                ins.then_inc(sem(signal), 1) if signal else own.done(ins)

            for j in range(26):
                split("mla_in", j // 4, j % 4)
                if j < 10:
                    dve.wait_ge(evacuated, EVAC["mla_in"] + j + 1)
                if j < 8:
                    accumulate(Steps(dve, sem("square_steps"), reached("steps", "q") + 2 * j), blk(ql, j), rt[3], ssq if j < 4 else ssqk)
                if j == 9:
                    dve.wait_ge(sem("rope_cs"), 2)
                    dve.wait_ge(sem("square_steps"), reached("steps", "kv", 8))
                    rotate(kp[:, 0:T], kp[:, T:2 * T], kpr[:, 0:T], kpr[:, T:2 * T])
            recip("q", rs[:, :])
            recip("kv", rsk[:, :])
            normed("lat", ql, lambda b: v("q_norm", b) if b < 4 else v("kv_norm", b - 4), ql, lath, latl,
                   inv=lambda b: rs if b < 4 else rsk, quads=2)
            dve.wait_ge(sem("operand_rest"), reached("x", "lat", 2))
            for s in range(6):
                split("uq", s // 4, s % 4)
                if s >= 4:
                    dve.wait_ge(evacuated, EVAC["uq"] + s + 1)
                    for a in range(2):
                        m = 2 * (s - 4) + a
                        rotate(blk(qp, m), blk(qp, 4 + m), blk(qraw, 2 * a), blk(qraw, 2 * a + 1), a and "q_rot")
            for name in ("uk", "uv"):
                for s in range(4):
                    split(name, 0, s)
            dve.wait_ge(sem("maska_loaded"), 16)
            for n in range(NH + 3):
                if n < NH:
                    b = n % 2
                    c = 8 * n
                    dve.wait_ge(sem("scores_done"), n + 1)
                    if n >= 2:
                        dve.wait_ge(sem("p_exp"), 2 * (n - 1))
                    dve.tensor_tensor(s_[b][:, :], PS[b][:, 0:3 * P], maska[:, :], ALU.add).then_inc(sem("s_masked"), 1)
                    dve.wait_ge(sem("s_masked"), n + 1)
                    own.done(dve.reduce_max(stat[:, c + 4:c + 5], s_[b][:, 0:P], AX))
                    own.done(dve.reduce_max(stat[:, c + 5:c + 6], s_[b][:, P:3 * P], AX))
                    own.wait()
                    dve.tensor_scalar(stat[:, c:c + 2], stat[:, c + 4:c + 6], -SM_SCALE, None, ALU.mult).then_inc(sem("s_max"), 1)
                if 1 <= n <= NH:
                    h = n - 1
                    c, b = 8 * h, h % 2
                    dve.wait_ge(sem("p_exp"), 2 * h + 2)
                    own.done(dve.reciprocal(stat[:, c + 6:c + 8], stat[:, c + 2:c + 4]))
                    own.wait()
                    dve.tensor_scalar(p_[b][:, 0:P], p_[b][:, 0:P], stat[:, c + 6:c + 7], None, ALU.mult)
                    dve.tensor_scalar(p_[b][:, P:3 * P], p_[b][:, P:3 * P], stat[:, c + 7:c + 8], None,
                                      ALU.mult).then_inc(sem("p_norm"), 1)
                if 2 <= n <= NH + 1:
                    h = n - 2
                    dve.wait_ge(sem("pv_done"), h + 1)
                    if h >= 2:
                        dve.wait_ge(sem("y3_x"), h - 1)
                    dve.tensor_tensor(yt[h % 2][:, :], PS[2 + h % 2][:, 0:T], blk(sg2, h), ALU.mult).then_inc(sem("o_made"), 1)
                if n >= 3:
                    h = n - 3
                    dve.wait_ge(sem("y3_hi"), h + 1)
                    dve.tensor_tensor(blk(y3l, h), yt[h % 2][:, :], blk(y3h, h).bitcast(F32), ALU.subtract).then_inc(sem("y3_x"), 1)
            clear_ssq()
            for i, r in turns(dve, 16):
                split("mla_out", i, r)
                u = 4 * i + r
                dve.wait_ge(evacuated, EVAC["mla_out"] + u + 1)
                accumulate(Steps(dve, sem("square_steps"), reached("steps", "post1") + 2 * u), blk(O, u), tmpq)
            p_rest(1, ptr1, pth1, ptl1)
            for s in range(2):
                split("proj1", 0, s)
            after_block(1, ot1, fxh, fxl)
            gated(1, pj1, 0, tail=4)

        @block.tensor
        def _(pe):
            def mm3(o, wh, wl, ah, al, start, stop, swap=False):
                kw = dict(skip_group_check=True)
                if swap:
                    pe.matmul(o, ah, wh, start=start, stop=False, **kw)
                    pe.matmul(o, ah, wl, start=False, stop=False, **kw)
                    return pe.matmul(o, al, wh, start=False, stop=stop, **kw)
                pe.matmul(o, wh, ah, start=start, stop=False, **kw)
                pe.matmul(o, wh, al, start=False, stop=False, **kw)
                return pe.matmul(o, wl, ah, start=False, stop=stop, **kw)

            def slot(phase, i, r, product, count=BLOCKS):
                s = where(phase, i, r)
                p = (BASE[phase] + r) % PAIR
                for n in range(count):
                    if n % (count // 2) == 0:
                        pe.wait_ge(lo_ready, 2 * s + n // (count // 2) + 1)
                    c = slice(n * SLOT // count, (n + 1) * SLOT // count)
                    ins = product(n, HI[p][:, c], LO[p][:, c])
                ins.then_inc(slot_used, 1)

            def out_block(phase, i, r, ah, al, bank, operand=None):
                def product(n, h, l):
                    if operand and n % 4 == 0 and isinstance(i, int) and i + r == 0:
                        pe.wait_ge(sem("operand_rest"), reached("x", operand, n // 4 + 1))
                    return mm3(PS[bank][:, 0:T], h, l, blk(ah, n), blk(al, n), n == 0, n == 15)
                slot(phase, i, r, product)

            def out_major(phase, i, r, ah, al, operand=None):
                u = 4 * i + r
                if not isinstance(u, int) or EVAC[phase] + u - 1 > 0:
                    pe.wait_ge(evacuated, EVAC[phase] + u - 1)
                out_block(phase, i, r, ah, al, r % 2, operand)

            def sum_squares(name, kind, o=None, src=None):
                done = dict(SHARED[kind])[name]
                pe.wait_ge(sem({"steps": "square_steps", "ssq": "ssq_ready"}[kind]), reached(kind, name, done))
                src = ssq[:, :] if src is None else src
                o = PS[2][:, 0:T] if o is None else o
                pe.matmul(o, ones[:, :], src, start=True, stop=True, skip_group_check=True).then_inc(sem("norm_sum"), 1)

            def mod_block(u, n, place, g, start=False, stop=False):
                k = 4 * (u % 4) + n
                lo = k * MW + 2 * (MGROUPS - 1 - g)
                ins = pe.matmul(PS[7][0:16, :], cwin[:, lo:lo + 16], RAW[place][:, n * 512:(n + 1) * 512], start=start, stop=stop,
                                skip_group_check=True)
                if n == 3:
                    ins.then_inc(mod_used, 1)

            def turn_rows(n):
                pe.wait_ge(sem("mod_rows"), n + 1)
                for q in range(4):
                    ins = pe.transpose(PS[7 if n == 2 else 6][:, q * 16:(q + 1) * 16], mrows[n][:, q * P:(q + 1) * P], eye[0:16, 0:16])
                ins.then_inc(sem("mod_turned"), 1)

            filled = [0]

            def fill(count):
                for _ in range(count):
                    c = filled[0]
                    filled[0] += 1
                    u, n = c // 4, c % 4
                    q = u if u < ROUND else MOD_AT + u
                    if n == 0:
                        pe.wait_ge(raw_loaded[q % RING], 16 * (q // RING + 1))
                    mod_block(u, n, q % RING, u // 4 % MGROUPS, u % ROUND + n == 0, u % ROUND == ROUND - 1 and n == 3)

            pe.wait_ge(sem("c_ready"), 1)
            fill(4 * ROUND // 2)
            pe.wait_ge(sem("ssq_ready"), reached("ssq", "n1", 2))
            pe.wait_ge(sem("ones_ready"), 1)
            pe.matmul(PS[2][:, :], ones[:, :], ssqx[:, :], start=True, stop=True).then_inc(sem("norm_sum"), 1)
            fill(4 * ROUND // 2)
            pe.wait_ge(sem("eye_loaded"), 16)
            turn_rows(0)

            xhv = xh[:, :].rearrange("p (s k t) -> p s k t", s=2, k=KD)
            xlv = xl[:, :].rearrange("p (s k t) -> p s k t", s=2, k=KD)

            def both(phase, i, r, bank):
                o = PS[bank][:, :].rearrange("p (s t) -> p s t", s=2)

                def product(n, h, l):
                    if phase == "lr" and n % 4 == 0:
                        pe.wait_ge(sem("operand_rest"), reached("x", "x1", n // 2 + 2))
                    return mm3(o, h, l, xhv[:, :, n, :], xlv[:, :, n, :], n == 0, n == 15)
                slot(phase, i, r, product)
            both("lr", 0, 0, 0)
            for b in range(8):
                pe.wait_ge(evacuated, max(EVAC["key"] + b - 1, 1))
                both("key", b // 4, b % 4, b % 2)
            pe.wait_ge(evacuated, EVAC["value"])
            with pe.Fori(0, 2) as i:
                for r in range(8):
                    g, q = r // 4, r % 4
                    if q == 0:
                        pe.wait_ge(evacuated, EVAC["value"] + 8 * i + (4 * g - 4))

                    def product(n, h, l):
                        for tt in range(4):
                            k, s = 4 * q + n, tt // 2
                            c = slice((s * KD + k) * T + (tt % 2) * P, (s * KD + k) * T + (tt % 2 + 1) * P)
                            ins = mm3(PS[4 * g + tt][:, :], h, l, xh[:, c], xl[:, c], k == 0, k == 15, swap=True)
                        return ins
                    slot("value", 2 * i, r, product, count=4)
            pe.wait_ge(evacuated, EVAC["query"])
            for b in range(8):
                out_major("query", b // 4, b % 4, xh, xl)
            for i, r in turns(pe, 16):
                out_major("gate", i, r, xh, xl)

            pe.wait_ge(evacuated, EVAC["mix_out"])
            pe.wait_ge(sem("tables_loaded"), 64)
            for n in range(8):
                pe.matmul(PS[n][:, :], w_lr[:, n * P:(n + 1) * P], zlr[0:16, :], start=True, stop=True).then_inc(sem("dec_z"), 1)
            pe.wait_ge(sem("dec_abs"), 1)
            fill(FILL[0])
            for g in range(2):
                for a in range(4):
                    h, t = 2 * g + a // 2, a % 2
                    c = slice(h * T + t * P, h * T + (t + 1) * P)
                    ins = pe.matmul(PS[4 + g][:, a * P:(a + 1) * P], K[:, c], Q[:, c], start=True, stop=True)
                ins.then_inc(sem("diag_done"), 1)
            for d in range(2):
                fill(FILL[1])
                pe.wait_ge(sem("kend_ready"), d + 1)
                for t in range(2):
                    if d:
                        pe.wait_ge(sem("kend_t_ready"), 2)
                    for h in range(HEADS):
                        ins = pe.transpose(PS[t][:, h * P:(h + 1) * P], kend[:, h * T + t * P:h * T + (t + 1) * P], eye[:, :])
                    ins.then_inc(sem("kend_turned"), 1)
                fill(FILL[2])
                pe.wait_ge(sem("kend_t_ready"), 2 * d + 2)
                for g in range(2):
                    if d:
                        pe.wait_ge(sem("state_ready"), 2)
                    for h in (2 * g, 2 * g + 1):
                        for t in range(2):
                            ins = pe.matmul(PS[2 + g][:, (h % 2) * DV:(h % 2 + 1) * DV], kend_t[:, t * 512 + h * P:t * 512 + (h + 1) * P],
                                            V[:, (2 + t) * 2048 + h * DV:(2 + t) * 2048 + (h + 1) * DV], start=t == 0, stop=t == 1,
                                            skip_group_check=True)
                    ins.then_inc(sem("state_done"), 1)
            NL = len(LEVELS)
            pe.wait_ge(sem("diag_used"), 4)
            for n in range(2 * NL):
                d, l = n // NL, n % NL
                fill(min(FILL[3], 8 * ROUND - filled[0]) if n < 2 * NL - 1 else 8 * ROUND - filled[0])
                pe.wait_ge(sem("lvl_ops"), n + 1)
                if n == 1:
                    pe.wait_ge(sem("state_ready"), 4)
                if n >= 2:
                    m = n - 2
                    if m // NL or m % NL:
                        pe.wait_ge(sem("lvl_merged"), 2 * (m - m // NL))
                    pe.wait_ge(sem("cross_ready"), m // NL + 1)
                for a in range(4 if l == 0 else 8):
                    if l == 0:
                        kt, qt = (0, 1) if d == 0 else (1, 0)
                        ck, cq, o = a * T + kt * P, a * T + qt * P, PS[4][:, a * P:(a + 1) * P]
                    else:
                        ck = cq = a * P
                        o = PS[level_banks[n % 2][a // 4]][:, (a % 4) * P:(a % 4 + 1) * P]
                    ins = pe.matmul(o, qk[n % 2][:, ck:ck + P], qk[n % 2][:, cq:cq + P], start=True, stop=True,
                                    skip_group_check=True)
                ins.then_inc(sem("lvl_scores"), 1)
            pe.wait_ge(sem("lvl_merged"), 4 * (NL - 1))
            pe.wait_ge(sem("cross_ready"), 2)
            pe.wait_ge(sem("state_ready"), 4)
            for h in range(HEADS):
                for a in range(2):
                    o = PS[h][:, a * T:(a + 1) * T]
                    vc = h * DV + a * P
                    kw = dict(skip_group_check=True)
                    for d in range(2):
                        pe.matmul(o, state[d][:, vc:vc + P], qb[d][:, h * T:(h + 1) * T], start=d == 0, stop=False, **kw)
                    for d in range(2):
                        for t in range(2):
                            pe.matmul(o[:, t * P:(t + 1) * P], V[:, t * 2048 + vc:t * 2048 + vc + P],
                                      att[d][:, (2 * h + t) * P:(2 * h + t + 1) * P], start=False, stop=False, **kw)
                        kt, qt = (0, 1) if d == 0 else (1, 0)
                        ins = pe.matmul(o[:, qt * P:(qt + 1) * P], V[:, kt * 2048 + vc:kt * 2048 + vc + P],
                                        cross[d][:, h * P:(h + 1) * P], start=False, stop=d == 1, **kw)
                ins.then_inc(sem("gla_out"), 1)
                if h == 0:
                    turn_rows(1)
                fill(FILL[4])
            for g in range(2):
                for h in (2 * g, 2 * g + 1):
                    pe.wait_ge(sem("gla_sq"), h + 1)
                    for a in range(2):
                        ins = pe.matmul(PS[4 + g][:, (h % 2) * T:(h % 2 + 1) * T], ones[:, :], blk(osq, 2 * h + a),
                                        start=a == 0, stop=a == 1, skip_group_check=True)
                ins.then_inc(sem("gla_sum"), 1)
                fill(FILL[5])

            pe.wait_ge(sem("gla_root"), 2)
            pe.wait_ge(sem("mods_ready"), 2)
            for n in range(2):
                ins = pe.matmul(PS[5 + n][0:64, :], sel_if[:, n * 64:(n + 1) * 64], zlr[0:32, :], start=True, stop=True)
            ins.then_inc(sem("if_rows"), 1)
            fill(FILL[6])
            pe.wait_ge(sem("m_rows"), 1)
            for src, ready, done, banks in ((ri, "m_rows", "neg_g_rep", (0, 1, 2, 3)), (rm, "em_rows", "em_rep", (4, 5, 6, 3))):
                pe.wait_ge(sem(ready), 1)
                for n in range(8):
                    if n == 6 and src is rm:
                        pe.wait_ge(sem("neg_g_ready"), 4)
                    ins = pe.matmul(PS[banks[n // 2]][:, (n % 2) * T:(n % 2 + 1) * T], rep_sel[:, n * P:(n + 1) * P],
                                    src[:, 0:T], start=True, stop=True, skip_group_check=True)
                    if n % 2:
                        ins.then_inc(sem(done), 1)
            pe.wait_ge(sem("neg_g_ready"), 4)
            for t in range(4):
                ins = pe.transpose(PS[0][:, t * 64:(t + 1) * 64], rg[:, t * P:(t + 1) * P], eye[0:64, 0:64])
            ins.then_inc(sem("g_turned"), 1)
            fill(12 * ROUND - filled[0])
            turn_rows(2)
            pe.wait_ge(sem("gtok_ready"), 1)
            pe.wait_ge(sem("em_ready"), 4)

            def ml_scores(h):
                if h >= 2:
                    pe.wait_ge(sem("ml_w"), 2 * h - 2)
                for s in range(2):
                    for t in range(2):
                        c = (8 * s + 4 + h) * T + t * P
                        ins = pe.matmul(PS[2 * (h % 2) + s][:, t * T:(t + 1) * T], K[:, c:c + P], blk(Q, 4 + h),
                                        start=True, stop=True, skip_group_check=True)
                ins.then_inc(sem("ml_scores"), 1)
            ml_scores(0)
            for n in range(9):
                h, d = n // 2, n % 2
                if n < 8:
                    if d == 0 and h + 1 < HEADS:
                        ml_scores(h + 1)
                    W = wgt[n % 2]
                    pe.wait_ge(sem("ml_w"), n + 1)
                    if n >= 2:
                        pe.wait_ge(sem("ml_taken"), n - 1)
                    for a in range(3):
                        if a == 2 and n:
                            pe.wait_ge(sem("ml_taken"), n)
                        for t in range(4):
                            vc = t * 2048 + 1024 + h * DV + a * P
                            w = V[:, vc:vc + P] if a < 2 else ones[:, :]
                            o = PS[4 + d][:, a * T:(a + 1) * T] if a < 2 else PS[6][:, 0:T]
                            ins = pe.matmul(o, w, W[:, t * T:(t + 1) * T], start=t == 0, stop=t == 3, skip_group_check=True)
                    ins.then_inc(sem("ml_done"), 1)
                if n >= 2 and d == 0:
                    pe.wait_ge(sem("ml_sq"), h)
                    if h == 1:
                        pe.wait_ge(sem("mods_ready"), 3)
                    if h >= 2:
                        pe.wait_ge(sem("ml_root"), h - 1)
                    for a in range(2):
                        ins = pe.matmul(PS[7][:, 0:T], ones[:, :], tmpo[:, a * T:(a + 1) * T], start=a == 0, stop=a == 1)
                    ins.then_inc(sem("ml_sum"), 1)

            for i, r in turns(pe, 16, lead=1):
                out_major("mix_out", i, r, yh, yl, "y")
            sum_squares("n2", "steps")
            for i, r in turns(pe, 2 * KF, lead=1):
                if not isinstance(i, int) or i:
                    pe.wait_ge(sem("ff_made" if r % 2 else "gate_used"), 2 * i + (r // 2 - 1))
                out_block("up", i, r, x2h, x2l, r, "n2")
            pe.wait_ge(sem("gate_used"), KF)
            pe.wait_ge(sem("ff_made"), KF)
            pe.wait_ge(sem("ff_x"), KF)
            pe.wait_ge(sem("norm_root"), reached("root", "n2", 1))

            def k_major(phase, ah, al):
                def one(i, r, u, first=False):
                    return slot(phase, i, r, lambda n, h, l: mm3(
                        PS[n // 2][:, (n % 2) * T:(n % 2 + 1) * T], h, l, blk(ah, u), blk(al, u), first and n % 2 == 0, False))
                for r in range(4):
                    one(0, r, r, first=r == 0)
                n = COUNT[phase] // 4
                with pe.Fori(1, n) as i:
                    for r in range(4):
                        one(i, r, 4 * i + r)
                for u in range(4 * n, COUNT[phase]):
                    one(n, u % 4, u)
            k_major("down", hh, hl)
            sum_squares("nf", "ssq")
            sum_squares("np", "ssq")

            for i, r in turns(pe, 64, lead=1):
                out_major("pool_in", i, r, xph, xpl, "np")
            pe.wait_ge(sem("pool_x"), 32)
            for i, r in turns(pe, 16):
                u = 4 * i + r
                pe.wait_ge(evacuated, EVAC["group"] + u - 1)
                slot("group", i, r, lambda n, h, l: mm3(
                    PS[r % 2][:, (n // 8) * T:(n // 8 + 1) * T], h, l, blk(ph, 8 * i + n % 8), blk(pl, 8 * i + n % 8),
                    n % 8 == 0, n % 8 == 7))
            pe.wait_ge(sem("y2_x"), 16)
            k_major("pool_out", y2h, y2l)

            def proj(tag, pth, ptl):
                pe.wait_ge(sem(f"p{tag}_x"), 1)
                for s in range(2):
                    if s:
                        pe.wait_ge(evacuated, EVAC[f"proj{tag}"] + 1)
                    slot(f"proj{tag}", 0, s, lambda n, h, l: mm3(
                        PS[4 + n // 4][:, (n // 2 % 2) * T:(n // 2 % 2 + 1) * T], h, l, blk(pth, n % 2), blk(ptl, n % 2),
                        n % 2 == 0, n % 2 == 1))
            pe.wait_ge(sem("O_copied"), 8)
            pe.wait_ge(sem("squares_ready"), reached("squares", "post0", 8))
            proj(0, pth0, ptl0)
            sum_squares("post0", "ssq")
            sum_squares("ple0", "ssq")
            for i, r in turns(pe, 16, lead=1):
                out_major("plegate0", i, r, gxh, gxl, "ple0")

            sum_squares("m", "steps")
            for j in range(26):
                out_major("mla_in", j // 4, j % 4, xmh, xml, "m")
            sum_squares("q", "steps")
            sum_squares("kv", "steps", PS[3][:, 0:T], ssqk[:, :])
            pe.wait_ge(sem("operand_rest"), reached("x", "lat", 2))
            pe.wait_ge(evacuated, EVAC["uq"])
            for name, n_slots, first in (("uq", 6, 0), ("uk", 4, 4)):
                for s in range(n_slots):
                    e = EVAC[name] + (s - 1)
                    pe.wait_ge(evacuated, e)
                    slot(name, s // 4, s % 4, lambda n, h, l: mm3(
                        PS[2 * (s % 2) + n // 8][:, (n // 4 % 2) * T:(n // 4 % 2 + 1) * T], h, l,
                        blk(lath, first + n % 4), blk(latl, first + n % 4), n % 4 == 0, n % 4 == 3))
            for s in range(4):
                pe.wait_ge(evacuated, EVAC["uv"] + s - 1)

                def product(n, h, l):
                    for t in range(2):
                        c = slice((4 + n) * T + t * P, (4 + n) * T + (t + 1) * P)
                        ins = mm3(PS[2 * (s % 2) + t][:, :], h, l, lath[:, c], latl[:, c], n == 0, n == 3, swap=True)
                    return ins
                slot("uv", 0, s, product, count=4)
            pe.wait_ge(evacuated, EVAC["mla_out"])
            pe.wait_ge(sem("q_rot"), 2)
            for n in range(NH + 2):
                if n < NH:
                    m, row = n // 4, 32 * (n % 4)
                    if n >= 2:
                        pe.wait_ge(sem("s_masked"), n - 1)
                    for t in range(2):
                        o = PS[n % 2][:, P * t:P * t + P * (t + 1)]
                        pe.matmul(o, qn[:, n * T + t * P:n * T + (t + 1) * P], kn[:, n * T:n * T + (t + 1) * P],
                                  start=True, stop=False, skip_group_check=True)
                        for a in range(2):
                            ins = pe.matmul(o, qp[row:row + 32, (4 * a + m) * T + t * P:(4 * a + m) * T + (t + 1) * P],
                                            kp[row:row + 32, a * T:a * T + (t + 1) * P], start=False, stop=a == 1,
                                            skip_group_check=True)
                    ins.then_inc(sem("scores_done"), 1)
                if 1 <= n <= NH:
                    h = n - 1
                    pe.wait_ge(sem("p_norm"), h + 1)
                    if h >= 2:
                        pe.wait_ge(sem("pt_ready"), h - 1)
                    for t in range(3):
                        ins = pe.transpose(PS[4 + h % 2][:, t * P:(t + 1) * P], p_[h % 2][:, t * P:(t + 1) * P], eye[:, :])
                    ins.then_inc(sem("p_turned"), 1)
                if n >= 2:
                    h = n - 2
                    pe.wait_ge(sem("pt_ready"), h + 1)
                    if h >= 2:
                        pe.wait_ge(sem("o_made"), h - 1)
                    va, vb, w = v2[:, h * P:(h + 1) * P], v2[:, 2048 + h * P:2048 + (h + 1) * P], pt[h % 2]
                    o = PS[2 + h % 2]
                    pe.matmul(o[:, 0:P], va, w[:, 0:P], start=True, stop=True, skip_group_check=True)
                    pe.matmul(o[:, P:T], va, w[:, P:2 * P], start=True, stop=False, skip_group_check=True)
                    pe.matmul(o[:, P:T], vb, w[:, 2 * P:3 * P], start=False, stop=True,
                              skip_group_check=True).then_inc(sem("pv_done"), 1)
            pe.wait_ge(sem("y3_x"), 16)
            for i, r in turns(pe, 16):
                out_major("mla_out", i, r, y3h, y3l)
            proj(1, pth1, ptl1)
            sum_squares("post1", "steps")
            sum_squares("ple1", "ssq")
            for i, r in turns(pe, 16, tail=4, lead=1):
                out_major("plegate1", i, r, fxh, fxl, "ple1")


def blocks(w, outs=None):
    k, n = w.shape
    return w.reshape(k // P, P, n // P, P).transpose(2, 1, 0, 3)


def slots(w):
    b = blocks(w)
    n, _, kb, _ = b.shape
    per = BLOCKS // kb
    return b.reshape(n // per, per, P, kb, P).transpose(0, 2, 1, 3, 4).reshape(n // per, P, SLOT)


def k_slots(w):
    return w.reshape(-1, P, SLOT)


def wide_slots(w):
    k, n = w.shape
    return w.reshape(k // 512, 4, P, n // 512, 512).transpose(3, 0, 2, 1, 4).reshape(-1, P, SLOT)


def rows(a):
    return a.reshape(-1, P).T


def tokens(a):
    t, f = a.shape
    return a.reshape(t, f // P, P).transpose(2, 1, 0).reshape(P, -1)


def lay_out(x):
    A = {}
    w_in = x["w_in"][0]
    gq, gk, gv, gg, glr, mq, mk, mv, mo, mg = np.split(w_in, np.cumsum(
        [512, 512, 1024, 1024, 16, 512, 512, 1024, 1024]), axis=1)
    up_w = x["w_up"][0]
    gate_up = blocks(up_w).reshape(2, KF, P, SLOT).transpose(1, 0, 2, 3).reshape(2 * KF, P, SLOT)
    mi = x["mla_w_in_2"][0]
    k1, k2 = mi[:, 1024:1056], mi[:, 1056:1088]
    uq = x["mla_w_uq_2"][0].reshape(512, NH, 192)
    pe1 = uq[:, :, 128:160].reshape(512, 4, 1, P)
    pe2 = uq[:, :, 160:192].reshape(512, 4, 1, P)
    ukv = x["mla_w_ukv_2"][0].reshape(512, NH, 256)
    grp = x["pool_w_group_2"][0]
    mod = wide_slots(x["w_mod"][0])
    parts = [slots(np.concatenate([glr, mg, np.zeros((D, P - 32), np.float32)], 1)),
             slots(gk), slots(mk), wide_slots(np.concatenate([gv, mv], 1)), slots(gq), slots(mq), slots(gg), slots(mo),
             slots(x["w_out"][0]), gate_up, k_slots(x["w_down"][0]), slots(x["pool_w_in_2"][0])]
    parts += [slots(g) for g in grp]
    parts += [k_slots(x["pool_w_out_2"][0]), slots(x["ple_w_proj_2"][0]), slots(x["ple_w_gate_2"][0]),
              slots(np.concatenate([mi[:, :1024]] + [k1] * 4 + [k2] * 4 + [mi[:, 1088:]], 1)),
              slots(uq[:, :, :128].reshape(512, 2048)),
              slots(np.concatenate([pe1, pe2], 2).reshape(512, 1024)),
              slots(ukv[:, :, :128].reshape(512, 2048)), wide_slots(ukv[:, :, 128:].reshape(512, 2048)),
              slots(x["mla_w_out_2"][0]), slots(x["ple_w_proj_2"][1]), slots(x["ple_w_gate_2"][1])]
    w = np.concatenate(parts)
    A["weights"] = np.concatenate([mod[:ROUND], w[:MOD_AT], mod[ROUND:], w[MOD_AT:]])
    assert w.shape[0] == SLOTS and mod.shape[0] == 3 * ROUND

    c2 = np.stack([rows(x["c"][0]), rows(x["c_ctx"])], 2).reshape(P, 2 * KD)
    gate_b = np.zeros((P, 2), np.float32)
    for d in range(2):
        gate_b[32 * d:32 * d + HEADS] = x["mlstm_b_gate"][0, d].T
    one = np.ones((P, 1), np.float32)
    invf = (np.float32(10000.0) ** (-np.arange(0, 64, 2, dtype=np.float32) / np.float32(64))).astype(np.float32)
    corr = np.concatenate([w / np.minimum(np.arange(16) + 1, w) for w in WINDOWS]).astype(np.float32)
    cols = {"c2": c2, "b_mod": rows(x["b_mod"][0]), "g1": rows(x["g_norm1"][0]), "g2": rows(x["g_norm2"][0]),
            "gfin": rows(x["g_final"]), "conv_w": x["conv_w"][0].reshape(9, KF, P).transpose(2, 1, 0).reshape(P, -1),
            "conv_b": rows(x["conv_b"][0]), "lr_b": rows(x["gla_b_lr"][0].reshape(-1)), "gla_g": rows(x["gla_g_norm"][0]),
            "ml_g": rows(x["mlstm_g_norm"][0]), "pre0": rows(x["pre_norm_2"][0]), "pre1": rows(x["pre_norm_2"][1]),
            "post0": rows(x["post_norm_2"][0]), "post1": rows(x["post_norm_2"][1]), "pscale": rows(x["pool_scale_2"][0]),
            "ple0": rows(x["ple_norm_2"][0]), "ple1": rows(x["ple_norm_2"][1]), "q_norm": rows(x["mla_q_norm_2"][0]),
            "kv_norm": rows(x["mla_kv_norm_2"][0]), "gate_b": gate_b, "eps": one * np.float32(EPS),
            "invf": np.tile(invf, 4)[:, None], "halfpi": one * np.float32(np.pi / 2), "corr": one * corr[None]}
    A["vec"] = np.concatenate([cols[n] for n in VEC], 1).astype(np.float32, copy=False)
    A["eye"] = np.eye(P, dtype=np.float32)
    A["xt"] = np.concatenate([tokens(x["x"][0]), tokens(x["ctx"][0])], 1)
    A["pt"] = np.concatenate([tokens(x["p_2"][0, 0]), tokens(x["p_2"][1, 0])], 1)
    A["pos"] = np.broadcast_to(x["positions_2"].astype(np.int32, copy=False), (P, T))
    A["w_lr"] = x["gla_w_lr"][0].transpose(1, 0, 2).reshape(16, 8 * P)
    i, j = np.arange(P)[:, None], np.arange(P)[None, :]
    lv = []
    for d in range(2):
        for h in LEVELS[1:]:
            m = (i // (2 * h) == j // (2 * h)) & (i // h % 2 == 0) & (j // h % 2 == 1)
            lv.append(m if d == 0 else m.T)
    A["lvl"] = np.concatenate(lv, 1).astype(np.int8).view(np.int32)
    rep = np.zeros((64, 8, P), np.float32)
    for n in range(8):
        rep[32 * (n // 4) + n % 4, n] = 1.0
    A["rep_sel"] = rep.reshape(64, -1)
    sel = np.zeros((32, 2, 64), np.float32)
    for f in range(2):
        for d in range(2):
            for h in range(HEADS):
                sel[16 + 8 * d + 4 * f + h, f, 32 * d + h] = 1.0
    A["sel_if"] = sel.reshape(32, -1)
    jj = np.arange(T)[None, :]
    mn = [np.where((t * P + i <= jj) if d == 0 else (t * P + i >= jj), 0.0, NEG) for d in range(2) for t in range(2)]
    A["maskn"] = np.concatenate(mn, 1).astype(np.float32)
    causal = np.where(j <= i, 0.0, NEG)
    A["maska"] = np.concatenate([causal, np.zeros((P, P)), causal], 1).astype(np.float32)
    return {k: np.ascontiguousarray(a) for k, a in A.items()}


def kernel(**inputs):
    import concourse.bacc as _bacc
    from concourse.bass_utils import run_bass_kernel_spmd as _run

    x = {k: np.asarray(a) for k, a in inputs.items()}
    arrays = lay_out(x)
    nc = _bacc.Bacc("TRN2", target_bir_lowering=False, num_devices=1, dynamic_dma_scratch_size=1024)
    aps = {k: nc.dram_tensor(f"in_{k}", a.shape, mybir.dt.from_np(a.dtype), kind="ExternalInput").ap()
           for k, a in arrays.items()}
    out = nc.dram_tensor("out_0", (P, KD * T), F32, kind="ExternalOutput").ap()
    build(nc, aps, out)
    r = _run(nc, [{f"in_{k}": a for k, a in arrays.items()}], core_ids=[0])
    got = r.results[0]["out_0"]
    return np.ascontiguousarray(got.reshape(P, KD, T).transpose(2, 1, 0).reshape(1, T, D))
```

```python
from contextlib import ExitStack

import numpy as np
import concourse.bass as bass
from concourse import mybir

F32 = mybir.dt.float32
F32R = mybir.dt.float32r
I32 = mybir.dt.int32
I8 = mybir.dt.int8
ALU = mybir.AluOpType
ACT = mybir.ActivationFunctionType
AX = mybir.AxisListType.X

P = 128
D = 2048
KD = D // P
T = 256
HEADS = 4
DK, DV = 128, 256
FF = 5504
KF = FF // P
EPS = 1e-6
NEG = -1e30
GRID_W = 64
GRID_H = T // GRID_W
WINDOWS = (2, 4, 8, 16)
NH = 16
SM_SCALE = (128 + 64) ** -0.5
LEVELS = (128, 64, 32, 16, 8, 4, 2, 1)
BLOCKS = 16
SLOT = BLOCKS * P
RING, PAIR = 4, 2

ROUNDS = (8, 2, 7, 7)
MGROUPS = max(ROUNDS)
MSTART = [4 * sum(ROUNDS[:n]) for n in range(len(ROUNDS) + 1)]
EARLY, MSLOTS = MSTART[2], MSTART[-1]
PHASES = [("lr", 1, 1), ("key", 8, 8), ("value", 16, 16), ("query", 8, 8),
          ("gate", 16, 16), ("mix_out", 16, 16), ("up", 2 * KF, 0), ("down", KF, 0),
          ("pool_in", 64, 64), ("group", 16, 16), ("pool_out", 32, 0), ("proj0", 2, 2),
          ("plegate0", 16, 16), ("mla_in", 26, 26), ("uq", 6, 6), ("uk", 4, 4), ("uv", 4, 4),
          ("mla_out", 16, 16), ("proj1", 2, 2), ("plegate1", 16, 16)]
BASE, COUNT, EVAC = {}, {}, {}
_s = _e = 0
for _n, _c, _v in PHASES:
    BASE[_n], COUNT[_n], EVAC[_n] = _s, _c, _e
    _s, _e = _s + _c, _e + _v
SLOTS = _s
MOD_AT = BASE["mix_out"] + 2


def loads_before(s):
    return EARLY if s < MOD_AT else MSLOTS

VEC, _w = {}, 0
for _n, _c in [("c2", 2 * KD), ("b_mod", 96), ("g1", 16), ("g2", 16), ("gfin", 16), ("conv_w", 9 * KF),
               ("conv_b", KF), ("lr_b", 8), ("gla_g", 2), ("ml_g", 2), ("pre0", 16), ("pre1", 16),
               ("post0", 16), ("post1", 16), ("pscale", 32), ("ple0", 16), ("ple1", 16),
               ("q_norm", 4), ("kv_norm", 4), ("gate_b", 2), ("eps", 1), ("invf", 1), ("halfpi", 1),
               ("corr", 64)]:
    VEC[_n] = _w
    _w += _c
NVEC = _w

KB = 1024

FILL = (16, 4, 4, 4, 12, 12, 48)

TWO_PI = (6.28125, 0.00193500518798828125, float(2 * np.pi - 6.28125 - 0.00193500518798828125))


SHARED = {
    "sum": [(n, 1) for n in ("n1", "n2", "nf", "np", "post0", "ple0", "m", "q", "kv", "post1", "ple1")],
    "root": [(n, 1) for n in ("n1", "n2", "nf", "np", "post0", "ple0", "m", "q", "kv", "post1", "ple1")],
    "ssq": [("n1", 2)] + [(n, 1) for n in ("np", "ple0", "ple1")],
    "part": [(n, 4) for n in ("nf", "np", "ple0", "ple1")],
    "squares": [("n1", 2), ("nf", 4), ("np", 4), ("post0", 8), ("ple0", 4), ("ple1", 4)],
    "steps": [("n2", 32), ("m", 32), ("q", 8), ("kv", 8), ("post1", 32)],
}
SHARED["made"] = [("x1", 8), ("y", 4), ("n2", 4), ("lat", 2)]
for _k in ("hi", "x"):
    SHARED[_k] = [("x1", 8), ("y", 4), ("n2", 4), ("np", 4), ("ple0", 4), ("m", 16), ("lat", 2), ("ple1", 4)]


def reached(kind, name, n=0):
    names = [a for a, _ in SHARED[kind]]
    return sum(c for _, c in SHARED[kind][:names.index(name)]) + n


class Steps:

    def __init__(self, eng, sem, base=0):
        self.eng, self.sem, self.base, self.n = eng, sem, base, 0

    def start(self):
        self.eng.wait_ge(self.sem, self.base)

    def done(self, ins):
        ins.then_inc(self.sem, 1)
        self.n += 1

    def wait(self):
        if self.n:
            self.eng.wait_ge(self.sem, self.base + self.n)


def turns(eng, n, tail=0, lead=0):
    q = max((n - tail) // RING, 0)
    if q > lead + 1:
        for j in range(RING * lead):
            yield j // RING, j % RING
        with eng.Fori(lead, q) as i:
            for r in range(RING):
                yield i, r
    else:
        q = 0
    for j in range(RING * q, n):
        yield j // RING, j % RING


def build(nc, A, out):
    with ExitStack() as ctx:
        sems = {}

        def sem(name):
            if name not in sems:
                sems[name] = ctx.enter_context(nc.semaphore(name))
            return sems[name]

        arena0 = (nc.sbuf_base + 63) // 64 * 64
        ctx.enter_context(nc.sbuf_tensor("arena", [P, (nc.sbuf_usable_end - arena0 - 64) // 4], F32))

        def at(name, cols, kb, dt=F32, rows=P):
            return nc.alloc_sbuf_tensor_at(name, [rows, cols], dt, offset=arena0 + int(kb * KB))

        RAW = [at(f"raw{i}", SLOT, 8 * i) for i in range(RING)]
        HI = [at(f"hi{i}", SLOT, 32 + 8 * i, F32R) for i in range(PAIR)]
        LO = [at(f"lo{i}", SLOT, 48 + 8 * i, F32R) for i in range(PAIR)]
        vec = at("vec", NVEC, 64)
        mods = at("mods", 192, 67.5)
        eye = at("eye", P, 68.25)
        ones = at("ones", P, 68.75)
        ssq = at("ssq", T, 69.25)
        rs = at("rs", T, 70.25)
        amod = at("amod", 3 * KD, 71.25)
        csil = at("csil", 2 * KD, 71.75)
        W0 = 72
        wk = lambda name, cols, kb, dt=F32, rows=P: at(name, cols, W0 + kb, dt, rows)
        xh, xl = wk("xh", 2 * KD * T, 0, F32R), wk("xl", 2 * KD * T, 32, F32R)
        xf = wk("xf", 2 * KD * T, 64)
        sq = [wk("sq0", KD * T, 96), wk("sq1", KD * T, 112)]
        rsx = wk("rsx", 2 * T, 128)
        ssqx = wk("ssqx", 2 * T, 130)
        K = wk("K", 2 * 8 * T, 64)
        V = wk("V", 4 * 2048, 80)
        zlr = wk("zlr", 2 * T, 112)
        Q = wk("Q", 8 * T, 114)
        gates = wk("gates", 16 * T, 16)
        loga = wk("loga", 8 * 2 * T, 122)
        softp = wk("softp", 8 * 2 * T, 32)
        cumx = wk("cumx", 8 * T, 0)
        cumc = wk("cumc", 8 * T, 8)
        dec = [wk("dec0", 4 * T, 32), wk("dec1", 4 * T, 36)]
        qk = [wk("qk0", 4 * T, 40), wk("qk1", 4 * T, 44)]
        w_lr = wk("w_lr", 8 * P, 138, rows=16)
        att = [wk("att0", 8 * P, 48), wk("att1", 8 * P, 52)]
        cross = [wk("cross0", 4 * P, 56), wk("cross1", 4 * P, 58)]
        kend = wk("kend", 4 * T, 60)
        kend_t = wk("kend_t", 2 * 4 * P, 122)
        state = [wk("state0", 4 * DV, 126), wk("state1", 4 * DV, 130)]
        qb = [wk("qb0", 4 * T, 134), wk("qb1", 4 * T, 138)]
        rep_sel = wk("rep_sel", 8 * P, 142, rows=64)
        lvl_words = wk("lvl_words", 2 * 7 * P // 4, 146, I32)
        lvl = lvl_words[:, :].bitcast(I8)
        sel_if = wk("sel_if", P, 148, rows=32)
        MW = 4 * MGROUPS - 2
        cwin = wk("cwin", KD * MW, 148.5)
        mrows = [wk(f"mrows{n}", 512, kb, rows=16) for n, kb in enumerate((134, 136, 60, 62))]
        osq = wk("osq", 8 * T, 32)
        rgrp = wk("rgrp", 4 * T, 40)
        yf = wk("yf", 16 * T, 48)
        neg_g = wk("neg_g", 8 * T, 0)
        em = wk("em", 8 * T, 8)
        maskn = wk("maskn", 4 * T, 32)
        wgt = [wk("wgt0", 4 * T, 36), wk("wgt1", 4 * T, 40)]
        ri = wk("ri", 2 * T, 122, rows=64)
        rf = wk("rf", 2 * T, 124, rows=64)
        rl = wk("rl", 2 * T, 126, rows=64)
        rg = wk("rg", 2 * T, 128, rows=64)
        rm = wk("rm", 2 * T, 130, rows=64)
        gtok = wk("gtok", 4 * 64, 132)
        rden = [wk("rden0", T, 44), wk("rden1", T, 45)]
        tmpo = wk("tmpo", 2 * T, 46)
        omix = wk("omix", 8 * T, 122)
        yh, yl = wk("yh", 16 * T, 64, F32R), wk("yl", 16 * T, 80, F32R)
        R = wk("R", KD * T, 134)
        tmpx = wk("tmpx", T, 118)
        tn = wk("tn", KD * T, 118)
        x2h, x2l = wk("x2h", KD * T, 86, F32R), wk("x2l", KD * T, 102, F32R)
        hh, hl = wk("hh", KF * T, 0, F32R), wk("hl", KF * T, 43, F32R)
        pad = [wk("pad0", 6 * 66, 118), wk("pad1", 6 * 66, 120)]
        acc = [wk("acc0", T, 122), wk("acc1", T, 123)]
        accb = [wk("accb0", T, 128), wk("accb1", T, 129)]
        sil = [wk("sil0", T, 124), wk("sil1", T, 125)]
        ht = [wk("ht0", T, 126), wk("ht1", T, 127)]
        UPW = 16 + T
        xph, xpl = wk("xph", KD * T, 96, F32R), wk("xpl", KD * T, 112, F32R)
        ph, pl = wk("ph", 32 * T, 0, F32R), wk("pl", 32 * T, 32, F32R)
        sg = wk("sg", 32 * T, 64)
        y2h, y2l = wk("y2h", 32 * T, 64, F32R), wk("y2l", 32 * T, 96, F32R)
        up = [wk("up0", UPW, 128), wk("up1", UPW, 129.0625)]
        ws = [wk("ws0", UPW, 130.125), wk("ws1", UPW, 131.1875)]
        pf = wk("pf", T, 132.25)
        gt = [wk("gt0", 2 * T, 128), wk("gt1", 2 * T, 130)]
        O = wk("O", KD * T, 0)
        ot = wk("ot", KD * T, 16)
        pj0 = wk("pj0", KD * T, 32)
        pth0, ptl0, ptr0 = wk("pth0", 2 * T, 48, F32R), wk("ptl0", 2 * T, 50, F32R), wk("ptr0", 2 * T, 52)
        gxh, gxl = wk("gxh", KD * T, 64, F32R), wk("gxl", KD * T, 80, F32R)
        sgt = [wk("sgt0", T, 54), wk("sgt1", T, 55)]
        sqp = wk("sqp", KD * T, 64)
        rsq = wk("rsq", T, 14.5)
        xmh, xml = wk("xmh", KD * T, 96, F32R), wk("xml", KD * T, 112, F32R)
        ql = wk("ql", 8 * T, 16)
        kpr = wk("kpr", 2 * T, 24)
        kp = wk("kp", 2 * T, 26)
        cs = wk("cs", 2 * T, 28)
        sg2 = wk("sg2", 16 * T, 32)
        lath, latl = wk("lath", 8 * T, 48, F32R), wk("latl", 8 * T, 56, F32R)
        ssqk = wk("ssqk", T, 30)
        rsk = wk("rsk", T, 31)
        qn = wk("qn", 16 * T, 64)
        qp = wk("qp", 8 * T, 16)
        rt = [wk(f"rt{i}", T, 128 + i) for i in range(4)]
        qraw = wk("qraw", 4 * T, 0)
        kn = wk("kn", 16 * T, 96)
        v2 = wk("v2", 2 * 2048, 112)
        tmpq = wk("tmpq", T, 30)
        tmpg = wk("tmpg", T, 53)
        s_ = [wk("s0", 384, 0), wk("s1", 384, 1.5)]
        p_ = [wk("p0", 384, 3), wk("p1", 384, 4.5), wk("p2", 384, 128)]
        pt = [wk("pt0", 384, 6), wk("pt1", 384, 7.5)]
        maska = wk("maska", 384, 9)
        yt = [wk("yt0", T, 11), wk("yt1", T, 12)]
        stat = wk("stat", 16 * 8, 13)
        y3h, y3l = wk("y3h", 16 * T, 48, F32R), wk("y3l", 16 * T, 80, F32R)
        pj1 = wk("pj1", KD * T, 16)
        ot1 = wk("ot1", KD * T, 32)
        fxh, fxl = wk("fxh", KD * T, 96, F32R), wk("fxl", KD * T, 112, F32R)
        pth1, ptl1, ptr1 = wk("pth1", 2 * T, 128, F32R), wk("ptl1", 2 * T, 130, F32R), wk("ptr1", 2 * T, 132)
        post = wk("post", T, 86, I32)
        ang = [wk(f"ang{i}", T, 87 + i) for i in range(4)]

        PS = [ctx.enter_context(nc.psum_tensor(f"ps{i}", [P, 512], F32)) for i in range(8)]

        raw_loaded = [sem(f"raw_loaded{i}") for i in range(RING)]
        hi_ready, lo_ready = sem("hi_ready"), sem("lo_ready")
        mod_used = sem("mod_used")
        slot_used = sem("slot_used")
        evacuated = sem("evacuated")

        def v(name, j=0, n=1):
            return vec[:, bass.ds(VEC[name] + j, n)] if not isinstance(j, int) else \
                vec[:, VEC[name] + j:VEC[name] + j + n]

        def blk(t, j, n=1):
            return t[:, bass.ds(j * T, n * T)] if not isinstance(j, int) else t[:, j * T:(j + n) * T]

        level_banks = ((4, 5), (6, 3))

        def turned_bank(n):
            return 7 if n == len(ROUNDS) - 1 else 6

        def x_quad(n):
            return 4 * (n % 2) + n // 2

        def where(phase, i, r):
            return BASE[phase] + RING * i + r

        block = ctx.enter_context(nc.Block())

        @block.sync
        def _(sp):
            def load(q, r):
                sp.dma_start(RAW[r][:, :], A["weights"][bass.ds(q, 1)].rearrange("a p n -> (a p) n")
                             if not isinstance(q, int) else A["weights"][q]).then_inc(raw_loaded[r], 16)

            def after_mod(q, u):
                sp.wait_ge(mod_used, u + 1)
                load(q, q % RING)

            def after_split(q, s, r=None):
                sp.wait_ge(lo_ready, 2 * s + 2)
                load(q, q % RING if r is None else r)

            for q in range(RING):
                load(q, q)
            for q in range(RING, EARLY + RING):
                after_mod(q, q - RING)
            first = EARLY + RING
            n = (MOD_AT - RING) // RING
            with sp.Fori(0, n) as i:
                for r in range(RING):
                    after_split(i * RING + (first + r), i * RING + r, r)
            for s in range(n * RING, MOD_AT):
                after_split(first + s, s)
            for u in range(EARLY, MSLOTS):
                after_mod(MOD_AT + RING + u, u)
            first = MSLOTS + RING
            n = (SLOTS - RING - MOD_AT) // RING
            with sp.Fori(0, n) as i:
                for r in range(RING):
                    after_split(i * RING + (first + MOD_AT + r), i * RING + (MOD_AT + r), (MOD_AT + r) % RING)
            for s in range(MOD_AT + n * RING, SLOTS - RING):
                after_split(first + s, s)
            sp.wait_ge(sem("gate1_used"), 1 + KD)
            sp.dma_start(out, R[:, :]).then_inc(sem("stored"), 16)
            sp.wait_ge(sem("stored"), 16)

        @block.scalar
        def _(act):
            def split(phase, i, r, ahead=2):
                t = where(phase, i, r) + ahead
                if isinstance(t, int) and t >= SLOTS:
                    return
                p = BASE[phase] + r + ahead
                if isinstance(i, int):
                    p += RING * i
                    i = 0
                act.wait_ge(raw_loaded[p % RING], 16 * (i + p // RING + 1 + loads_before(p) // RING))
                if not isinstance(t, int) or t >= 2:
                    act.wait_ge(slot_used, t - 1)
                for h in range(2):
                    c = slice(h * SLOT // 2, (h + 1) * SLOT // 2)
                    act.activation(HI[p % PAIR][:, c], RAW[p % RING][:, c], ACT.Copy).then_inc(hi_ready, 1)

            def round_hi(name, dst, src, quads=4, order=lambda q: q):
                for n in range(quads):
                    act.wait_ge(sem("operand_made"), reached("made", name, n + 1))
                    q = order(n)
                    act.activation(blk(dst, 4 * q, 4), blk(src, 4 * q, 4), ACT.Copy).then_inc(sem("operand_hi"), 1)

            def root(name, dst, src, n):
                act.wait_ge(sem("norm_sum"), reached("sum", name, 1))
                act.activation(dst, src, ACT.Sqrt, bias=v("eps"), scale=1.0 / n).then_inc(sem("norm_root"), 1)

            def square(name, dst, src, gain=None, hi=None):
                for q in range(4):
                    act.wait_ge(sem("part_ready"), reached("part", name, q + 1))
                    if hi:
                        for b in range(4 * q, 4 * q + 4):
                            ins = act.activation(blk(hi, b), blk(src, b), ACT.Copy, scale=v(gain, b))
                        ins.then_inc(sem("operand_hi"), 1)
                    act.activation(blk(dst, 4 * q, 4), blk(src, 4 * q, 4), ACT.Square).then_inc(sem("squares_ready"), 1)

            def mod_rows(n):
                act.wait_ge(mod_used, MSTART[n + 1])
                act.activation(mrows[n][:, :], PS[7][0:16, :], ACT.Copy).then_inc(sem("mod_rows"), 1)

            act.dma_start(vec[:, :], A["vec"]).then_inc(sem("vec_loaded"), 16)
            act.dma_start(eye[:, :], A["eye"]).then_inc(sem("eye_loaded"), 16)
            act.dma_start(xf[:, :], A["xt"]).then_inc(sem("x_loaded"), 16)
            for dst, name in ((lvl_words, "lvl"), (rep_sel, "rep_sel"), (sel_if, "sel_if"), (w_lr, "w_lr")):
                act.dma_start(dst[:, :], A[name]).then_inc(sem("tables_loaded"), 16)
            act.wait_ge(sem("vec_loaded"), 16)
            act.activation(csil[:, :], v("c2", 0, 2 * KD), ACT.Silu).then_inc(sem("c_act"), 1)
            act.wait_ge(sem("x_loaded"), 16)
            for s in range(2):
                act.activation(sq[s][:, :], blk(xf, KD * s, KD), ACT.Square).then_inc(sem("squares_ready"), 1)
            root("n1", rsx[:, :], PS[2][:, :], D)
            mod_rows(0)
            round_hi("x1", xh, xf, 8, x_quad)
            split("lr", 0, 0, 0)
            split("lr", 0, 1, 0)
            mod_rows(1)

            split("lr", 0, 0)
            act.wait_ge(slot_used, BASE["lr"] + 1)
            act.activation(zlr[:, :], PS[0][:, :], ACT.Copy).then_inc(evacuated, 1)
            kview = K[:, :].rearrange("p (s b t) -> p s b t", s=2, b=8)
            for half, scale in ((0, 1.0), (1, DK ** -0.5)):
                for r in range(4):
                    b = 4 * half + r
                    split("key", half, r)
                    act.wait_ge(slot_used, BASE["key"] + b + 1)
                    act.activation(kview[:, :, b, :], PS[b % 2][:, :].rearrange("p (s t) -> p s t", s=2),
                                   ACT.Copy, scale=scale).then_inc(evacuated, 1)
            with act.Fori(0, 2) as i:
                for r in range(8):
                    split("value", 2 * i, r)
                    if r % 4 == 3:
                        act.wait_ge(slot_used, BASE["value"] + 8 * i + r + 1)
                        for tt in range(4):
                            act.activation(V[:, bass.ds(i * 1024 + (tt * 2048 + (r // 4) * 512), 512)],
                                           PS[4 * (r // 4) + tt][:, :], ACT.Copy).then_inc(evacuated, 1)
            for half, scale in ((0, DK ** -0.5), (1, 1.0)):
                for r in range(4):
                    b = 4 * half + r
                    split("query", half, r)
                    act.wait_ge(slot_used, BASE["query"] + b + 1)
                    act.activation(blk(Q, b), PS[b % 2][:, 0:T], ACT.Copy, scale=scale).then_inc(evacuated, 1)
            for half, func in ((0, ACT.Silu), (1, ACT.Sigmoid)):
                with act.Fori(2 * half, 2 * half + 2) as i:
                    for r in range(4):
                        split("gate", i, r)
                        act.wait_ge(slot_used, where("gate", i, r) + 1)
                        act.activation(blk(gates, 4 * i + r), PS[r % 2][:, 0:T], func).then_inc(evacuated, 1)

            act.wait_ge(sem("dec_abs"), 1)
            act.activation(softp[:, :], softp[:, :], ACT.Exp, scale=-1.0).then_inc(sem("dec_exp"), 1)
            act.wait_ge(sem("dec_exp"), 1)
            act.activation(softp[:, :], softp[:, :], ACT.Ln, bias=1.0).then_inc(sem("dec_ln"), 1)
            for d in range(2):
                act.wait_ge(sem("kend_arg"), d + 1)
                act.activation(dec[0][:, :], dec[0][:, :], ACT.Exp, scale=1 / 16.0).then_inc(sem("kend_exp"), 1)
                if d:
                    act.wait_ge(sem("qb_ready"), d)
                act.activation(dec[1][:, :], blk(cumx, 4 * d, 4), ACT.Exp, scale=1 / 16.0).then_inc(sem("qb_exp"), 1)
                for t in range(2):
                    act.wait_ge(sem("kend_turned"), 2 * d + t + 1)
                    act.activation(kend_t[:, t * 512:(t + 1) * 512], PS[t][:, :], ACT.Copy).then_inc(sem("kend_t_ready"), 1)
                for g in range(2):
                    act.wait_ge(sem("state_done"), 2 * d + g + 1)
                    act.activation(state[d][:, g * 512:(g + 1) * 512], PS[2 + g][:, :], ACT.Copy).then_inc(sem("state_ready"), 1)
            NL = len(LEVELS)
            for n in range(2 * NL):
                act.wait_ge(sem("lvl_arg"), n + 1)
                act.activation(dec[n % 2][:, :], dec[n % 2][:, :], ACT.Exp, scale=1 / 16.0).then_inc(sem("lvl_exp"), 1)
                if n % NL == 0:
                    act.wait_ge(sem("lvl_scores"), n + 1)
                    act.activation(cross[n // NL][:, :], PS[4][:, :], ACT.Copy).then_inc(sem("cross_ready"), 1)
            mod_rows(2)
            for h in range(HEADS):
                act.wait_ge(sem("gla_out"), h + 1)
                act.activation(blk(osq, 2 * h, 2), PS[h][:, :], ACT.Square).then_inc(sem("gla_sq"), 1)
            for g in range(2):
                act.wait_ge(sem("gla_sum"), g + 1)
                act.activation(rgrp[:, g * 512:(g + 1) * 512], PS[4 + g][:, :], ACT.Sqrt, bias=v("eps"),
                               scale=1.0 / DV).then_inc(sem("gla_root"), 1)

            act.wait_ge(sem("operand_made"), reached("made", "y", 2))
            act.dma_start(maskn[:, :], A["maskn"]).then_inc(sem("maskn_loaded"), 16)
            act.wait_ge(sem("f_abs"), 1)
            act.activation(rl[:, :], rl[:, :], ACT.Exp, scale=-1.0).then_inc(sem("f_exp"), 1)
            act.wait_ge(sem("f_exp"), 1)
            act.activation(rl[:, :], rl[:, :], ACT.Ln, bias=1.0).then_inc(sem("f_ln"), 1)
            act.wait_ge(sem("m_rows"), 1)
            act.activation(rm[:, 0:T], rm[:, 0:T], ACT.Exp, scale=-1.0).then_inc(sem("em_rows"), 1)
            for n in range(4):
                act.wait_ge(sem("neg_g_rep"), n + 1)
                act.activation(neg_g[:, n * 512:(n + 1) * 512], PS[n][:, :], ACT.Copy).then_inc(sem("neg_g_ready"), 1)
            for n in range(4):
                act.wait_ge(sem("em_rep"), n + 1)
                act.activation(em[:, n * 512:(n + 1) * 512], PS[(4, 5, 6, 3)[n]][:, :], ACT.Copy).then_inc(sem("em_ready"), 1)
            act.wait_ge(sem("g_turned"), 1)
            act.activation(gtok[:, :], PS[0][:, 0:256], ACT.Copy).then_inc(sem("gtok_ready"), 1)
            act.wait_ge(sem("gtok_ready"), 1)
            mod_rows(3)
            act.dma_start(R[:, :], A["xt"][:, 0:KD * T]).then_inc(sem("R_loaded"), 16)
            for n in range(9):
                h, d = n // 2, n % 2
                if n < 8:
                    W = wgt[n % 2]
                    if n >= 2:
                        act.wait_ge(sem("ml_done"), n - 1)
                    for t in range(2, 4):
                        c = t * 64 + 32 * d + h
                        act.activation(W[:, t * T:(t + 1) * T], blk(neg_g, 4 * d + h), ACT.Exp,
                                       bias=gtok[:, c:c + 1]).then_inc(sem("w_ctx"), 1)
                    act.wait_ge(sem("w_arg"), n + 1)
                    act.activation(W[:, 0:2 * T], W[:, 0:2 * T], ACT.Exp).then_inc(sem("w_x"), 1)
                if n >= 2 and d == 0:
                    act.wait_ge(sem("ml_h"), h)
                    act.activation(tmpo[:, :], blk(omix, 2 * h - 2, 2), ACT.Square).then_inc(sem("ml_sq"), 1)
                    act.wait_ge(sem("ml_sum"), h)
                    act.activation(rden[(h - 1) % 2][:, :], PS[7][:, 0:T], ACT.Sqrt, bias=v("eps"),
                                   scale=1.0 / DV).then_inc(sem("ml_root"), 1)
            act.wait_ge(sem("ml_done"), 8)
            round_hi("y", yh, yf)

            for i, r in turns(act, 16):
                split("mix_out", i, r)
            root("n2", rs[:, :], PS[2][:, 0:T], D)
            round_hi("n2", x2h, tn)
            def ff_silu(j, b):
                act.wait_ge(sem("conv"), 9 * j + 9)
                act.activation(sil[b][:, :], acc[b][:, :], ACT.Silu, bias=v("conv_b", j)).then_inc(sem("ff_silu"), 1)

            def ff_hi(j, b):
                act.wait_ge(sem("ff_made"), j + 1)
                act.activation(blk(hh, j), ht[b][:, :], ACT.Copy).then_inc(sem("ff_hi"), 1)

            for i, r in turns(act, 2 * KF, lead=1):
                split("up", i, r)
                j, b = 2 * i + r // 2, r // 2
                first = isinstance(i, int) and i == 0 and r < 2
                if r % 2 == 0:
                    if first:
                        act.wait_ge(sem("pads_zeroed"), 1)
                    else:
                        ff_silu(j - 1, 1 - b)
                    act.wait_ge(slot_used, where("up", i, r) + 1)
                    if not isinstance(i, int) or i:
                        act.wait_ge(sem("ff_silu"), j - 1)
                    act.activation(pad[b][:, :].rearrange("p (y x) -> p y x", x=66)[:, 1:1 + GRID_H, 1:1 + GRID_W],
                                   PS[r][:, 0:T].rearrange("p (y x) -> p y x", x=GRID_W), ACT.Copy).then_inc(sem("pad_ready"), 1)
                    act.activation(acc[b][:, :], PS[r][:, 0:T], ACT.Copy, scale=v("conv_w", 9 * j + 4)).then_inc(sem("gate_used"), 1)
                elif not first:
                    ff_hi(j - 1, 1 - b)
            ff_silu(KF - 1, 0)
            ff_hi(KF - 1, 0)
            for i, r in turns(act, KF):
                split("down", i, r)
            square("nf", tn, R)
            root("nf", rs[:, :], PS[0][:, 0:T], D)
            square("np", sqp, R, "pre0", xph)
            root("np", rs[:, :], PS[4][:, 0:T], D)

            with act.Fori(0, 16) as i:
                for r in range(4):
                    split("pool_in", i, r)
                    u = 2 * i + r // 2
                    if r % 2:
                        act.wait_ge(sem("pool_made"), u + 1)
                        act.activation(blk(ph, u), pf[:, :], ACT.Copy).then_inc(sem("pool_hi"), 1)
                        act.wait_ge(evacuated, EVAC["pool_in"] + (4 * i + (r + 1)))
                        act.activation(blk(sg, u), blk(sg, u), ACT.Silu).then_inc(sem("sg_ready"), 1)
            for i, r in turns(act, 16):
                split("group", i, r)
                s = 4 * i + r
                act.wait_ge(evacuated, EVAC["group"] + s + 1)
                act.activation(blk(y2h, 2 * s, 2), gt[r % 2][:, :], ACT.Copy).then_inc(sem("y2_hi"), 1)
            def p_operand(tag, ptr, pth):
                act.dma_start(ptr[:, :], A["pt"][:, tag * 2 * T:(tag + 1) * 2 * T]).then_inc(sem(f"p{tag}_loaded"), 16)
                act.wait_ge(sem(f"p{tag}_loaded"), 16)
                act.activation(pth[:, :], ptr[:, :], ACT.Copy).then_inc(sem(f"p{tag}_hi"), 1)

            def proj(tag, pj, s):
                split(f"proj{tag}", 0, s)
                act.wait_ge(slot_used, BASE[f"proj{tag}"] + s + 1)
                for b in range(4):
                    ins = act.activation(blk(pj, 8 * s + 2 * b, 2), PS[4 + b][:, :], ACT.Copy)
                ins.then_inc(evacuated, 1)

            def after_block(tag, pj, squares, hi):
                proj(tag, pj, 0)
                root(f"post{tag}", rs[:, :], PS[2][:, 0:T], D)
                proj(tag, pj, 1)
                square(f"ple{tag}", squares, R, f"ple{tag}", hi)
                root(f"ple{tag}", rs[:, :], PS[2][:, 0:T], D)

            def gate(tag, tail=0):
                name = f"plegate{tag}"
                for i, r in turns(act, 16, tail, lead=1):
                    u = 4 * i + r
                    split(name, i, r)
                    act.wait_ge(evacuated, EVAC[name] + u + 1)
                    act.activation(sgt[r % 2][:, :], sgt[r % 2][:, :], ACT.Sigmoid).then_inc(sem(f"gate{tag}_ready"), 1)
                    if tag == 0 and (not isinstance(u, int) or u):
                        gated_hi(u - 1)
                if tag == 0:
                    gated_hi(KD - 1)

            def gated_hi(u):
                act.wait_ge(sem("gate0_used"), u + 2)
                act.activation(blk(xmh, u), blk(R, u), ACT.Copy, scale=v("pre1", u)).then_inc(sem("operand_hi"), 1)

            act.wait_ge(slot_used, BASE["pool_out"])
            p_operand(0, ptr0, pth0)
            for i, r in turns(act, 32):
                split("pool_out", i, r)
            for b in range(8):
                act.wait_ge(sem("O_copied"), b + 1)
                c = 2 * ((b + 4) % 8)
                act.activation(blk(ot, c, 2), blk(O, c, 2), ACT.Square).then_inc(sem("squares_ready"), 1)
            after_block(0, pj0, ot, gxh)
            gate(0)

            act.dma_start(post[:, :], A["pos"]).then_inc(sem("pos_loaded"), 16)
            root("m", rs[:, :], PS[2][:, 0:T], D)
            act.wait_ge(sem("ang_ready"), 1)
            act.activation(cs[:, T:2 * T], ang[0][:, :], ACT.Sin).then_inc(sem("rope_cs"), 1)
            act.activation(cs[:, 0:T], ang[1][:, :], ACT.Sin, bias=v("halfpi"), scale=-1.0).then_inc(sem("rope_cs"), 1)
            for j in range(26):
                split("mla_in", j // 4, j % 4)
                if j >= 10:
                    act.wait_ge(evacuated, EVAC["mla_in"] + j + 1)
                    act.activation(blk(sg2, j - 10), blk(sg2, j - 10), ACT.Silu).then_inc(sem("sg2_ready"), 1)
                if j == 12:
                    root("q", rsq[:, :], PS[2][:, 0:T], 512)
                    root("kv", rsk[:, :], PS[3][:, 0:T], 512)
                if j == 14:
                    round_hi("lat", lath, ql, 2)
            for s in range(6):
                split("uq", s // 4, s % 4)
                act.wait_ge(slot_used, BASE["uq"] + s + 1)
                if s == 5:
                    act.wait_ge(sem("q_rot"), 1)
                for b in range(2):
                    dst = blk(qn, 4 * s + 2 * b, 2) if s < 4 else blk(qraw, 2 * b, 2)
                    ins = act.activation(dst, PS[2 * (s % 2) + b][:, :], ACT.Copy)
                ins.then_inc(evacuated, 1)
            for s in range(4):
                split("uk", 0, s)
                act.wait_ge(slot_used, BASE["uk"] + s + 1)
                for b in range(2):
                    ins = act.activation(blk(kn, 4 * s + 2 * b, 2), PS[2 * (s % 2) + b][:, :], ACT.Copy)
                ins.then_inc(evacuated, 1)
            for s in range(4):
                split("uv", 0, s)
                act.wait_ge(slot_used, BASE["uv"] + s + 1)
                for t in range(2):
                    ins = act.activation(v2[:, t * 2048 + s * 512:t * 2048 + (s + 1) * 512], PS[2 * (s % 2) + t][:, :], ACT.Copy)
                ins.then_inc(evacuated, 1)
            act.dma_start(maska[:, :], A["maska"]).then_inc(sem("maska_loaded"), 16)
            for n in range(NH + 3):
                if n < NH:
                    act.wait_ge(sem("s_max"), n + 1)
                    if n >= 3:
                        act.wait_ge(sem("p_turned"), n - 2)
                    for t, c in ((0, slice(0, P)), (1, slice(P, 3 * P))):
                        act.activation(p_[n % 3][:, c], s_[n % 2][:, c], ACT.Exp, bias=stat[:, 8 * n + t:8 * n + t + 1],
                                       scale=SM_SCALE, accum_out=stat[:, 8 * n + 2 + t:8 * n + 3 + t]).then_inc(sem("p_exp"), 1)
                if 2 <= n <= NH + 1:
                    h = n - 2
                    act.wait_ge(sem("p_turned"), h + 1)
                    if h >= 2:
                        act.wait_ge(sem("pv_done"), h - 1)
                    act.activation(pt[h % 2][:, :], PS[4 + h % 2][:, 0:3 * P], ACT.Copy).then_inc(sem("pt_ready"), 1)
                if n >= 3:
                    h = n - 3
                    act.wait_ge(sem("o_made"), h + 1)
                    act.activation(blk(y3h, h), yt[h % 2][:, :], ACT.Copy).then_inc(sem("y3_hi"), 1)
            p_operand(1, ptr1, pth1)
            for i, r in turns(act, 16):
                split("mla_out", i, r)
                act.wait_ge(slot_used, where("mla_out", i, r) + 1)
                act.activation(blk(O, 4 * i + r), PS[r % 2][:, 0:T], ACT.Copy).then_inc(evacuated, 1)
            after_block(1, pj1, ot1, fxh)
            gate(1, tail=4)

        @block.vector
        def _(dve):
            own = Steps(dve, sem("vector_steps"))

            def split(phase, i, r, ahead=2):
                t = where(phase, i, r) + ahead
                if isinstance(t, int) and t >= SLOTS:
                    return
                p = BASE[phase] + r + ahead
                for h in range(2):
                    c = slice(h * SLOT // 2, (h + 1) * SLOT // 2)
                    dve.wait_ge(hi_ready, 2 * t + h + 1)
                    dve.tensor_tensor(LO[p % PAIR][:, c], RAW[p % RING][:, c], HI[p % PAIR][:, c].bitcast(F32),
                                      ALU.subtract).then_inc(lo_ready, 1)

            def recip(name, dst):
                dve.wait_ge(sem("norm_root"), reached("root", name, 1))
                own.done(dve.reciprocal(dst, dst))
                own.wait()

            def rest(name, q, hi, lo, src, at=None):
                dve.wait_ge(sem("operand_hi"), reached("hi", name, q + 1))
                q = q if at is None else at
                dve.tensor_tensor(blk(lo, 4 * q, 4), blk(src, 4 * q, 4), blk(hi, 4 * q, 4).bitcast(F32),
                                  ALU.subtract).then_inc(sem("operand_rest"), 1)

            def normed(name, src, gain, dst, hi, lo, inv=None, shift=None, quads=4):
                for q in range(quads + 1):
                    if q < quads:
                        for b in range(4 * q, 4 * q + 4):
                            ins = dve.scalar_tensor_tensor(blk(dst, b), blk(src, b), gain(b),
                                                           (inv(b) if inv else rs)[:, :], ALU.mult, ALU.mult)
                            if shift:
                                own.done(ins)
                        if shift:
                            own.wait()
                            for b in range(4 * q, 4 * q + 4):
                                ins = dve.tensor_scalar(blk(dst, b), blk(dst, b), shift(b), None, ALU.add)
                        ins.then_inc(sem("operand_made"), 1)
                    if q:
                        rest(name, q - 1, hi, lo, dst)

            def accumulate(st, src, tmp, total=ssq):
                st.start()
                st.done(dve.tensor_tensor(tmp[:, :], src, src, ALU.mult))
                st.wait()
                st.done(dve.tensor_tensor(total[:, :], total[:, :], tmp[:, :], ALU.add))

            def gained_rest(name, q, src, gain, hi, lo):
                dve.wait_ge(sem("operand_hi"), reached("hi", name, q + 1))
                for b in range(4 * q, 4 * q + 4):
                    ins = dve.scalar_tensor_tensor(blk(lo, b), blk(src, b), v(gain, b), blk(hi, b).bitcast(F32),
                                                   ALU.mult, ALU.subtract)
                ins.then_inc(sem("operand_rest"), 1)

            def add_squares(name, src, count=4):
                dve.wait_ge(sem("squares_ready"), reached("squares", name, count))
                dve.tensor_reduce(ssq[:, :], src[:, 0:KD * T].rearrange("p (k t) -> p t k", t=T), AX,
                                  ALU.add).then_inc(sem("ssq_ready"), 1)

            def clear_ssq():
                own.done(dve.memset(ssq[:, :], 0.0))
                own.wait()

            dve.memset(ones[:, :], 1.0).then_inc(sem("ones_ready"), 1)
            own.done(dve.memset(cwin[:, :], 0.0))
            own.wait()
            dve.wait_ge(sem("c_act"), 1)
            mid = 2 * MGROUPS - 2
            dve.tensor_copy(cwin[:, :].rearrange("p (k w) -> p k w", w=MW)[:, :, mid:mid + 2],
                            csil[:, :].rearrange("p (k s) -> p k s", s=2)).then_inc(sem("c_ready"), 1)
            for s in range(2):
                dve.wait_ge(sem("squares_ready"), reached("squares", "n1", s + 1))
                dve.tensor_reduce(ssqx[:, s * T:(s + 1) * T], sq[s][:, :].rearrange("p (k t) -> p t k", t=T), AX,
                                  ALU.add).then_inc(sem("ssq_ready"), 1)
            recip("n1", rsx[:, :])
            for s in range(2):
                xs = blk(xf, KD * s, KD).rearrange("p (k t) -> p k t", t=T)
                own.done(dve.tensor_tensor(xs, xs, rsx[:, s * T:(s + 1) * T][:, None, :].to_broadcast([P, KD, T]), ALU.mult))
            mview = mods[:, :].rearrange("p (j s) -> p j s", s=2)

            def modulation(n):
                dve.wait_ge(sem("mod_turned"), n + 1)
                own.wait()
                a, b = MSTART[n], MSTART[n + 1]
                dve.tensor_tensor(mview[:, a:b, :].rearrange("p (g q) s -> p g q s", q=4),
                                  PS[turned_bank(n)][:, 0:8 * MGROUPS].rearrange("p (q g s) -> p g q s", q=4, s=2)[:, 0:ROUNDS[n]],
                                  v("b_mod", a, b - a).rearrange("p (g q) -> p g q", q=4)[:, :, :, None].to_broadcast([P, ROUNDS[n], 4, 2]),
                                  ALU.add).then_inc(sem("mods_ready"), 1)
                dve.wait_ge(sem("mods_ready"), n + 1)

            def gains(n, j, s, g):
                own.done(dve.scalar_tensor_tensor(amod[:, n * KD:(n + 1) * KD], mview[:, j:j + KD, s], 1.0,
                                                  v(g, 0, KD), ALU.add, ALU.mult))
            modulation(0)
            gains(0, 16, 0, "g1")
            gains(1, 16, 1, "g1")
            own.wait()
            for n in range(9):
                if n < 8:
                    for b in range(4 * (n // 2), 4 * (n // 2) + 4):
                        f, k = (n % 2) * KD + b, b
                        ins = dve.tensor_scalar(blk(xf, f), blk(xf, f), amod[:, f:f + 1], mview[:, k, n % 2:n % 2 + 1],
                                                ALU.mult, ALU.add)
                    ins.then_inc(sem("operand_made"), 1)
                if n:
                    rest("x1", n - 1, xh, xl, xf, x_quad(n - 1))
            split("lr", 0, 0, 0)
            split("lr", 0, 1, 0)
            modulation(1)
            for name in ("lr", "key", "value", "query", "gate"):
                for i, r in turns(dve, COUNT[name]):
                    split(name, i, r)

            for n in range(8):
                dve.wait_ge(sem("dec_z"), n + 1)
                own.done(dve.tensor_scalar(loga[:, n * 512:(n + 1) * 512], PS[n][:, :], v("lr_b", n), None, ALU.add))
            own.wait()
            dve.scalar_tensor_tensor(softp[:, :], loga[:, :], -1.0, loga[:, :], ALU.mult, ALU.max).then_inc(sem("dec_abs"), 1)
            dve.wait_ge(sem("dec_ln"), 1)
            own.done(dve.scalar_tensor_tensor(loga[:, :], loga[:, :], 0.0, softp[:, :], ALU.min, ALU.subtract))
            own.wait()
            for n in range(8):
                step = 1 if n < 4 else -1
                for s, dst in ((0, cumx), (1, cumc)):
                    src = loga[:, n * 512 + s * T:n * 512 + (s + 1) * T][:, ::step]
                    own.done(dve.tensor_tensor_scan(blk(dst, n)[:, ::step], src, src, 0.0, ALU.add, ALU.bypass))
            own.wait()
            qg, kg = Q[:, 0:4 * T], K[:, 0:4 * T]
            for d in range(2):
                end = T - 1 if d == 0 else 0
                if d:
                    dve.wait_ge(sem("kend_ready"), d)
                cc = blk(cumc, 4 * d, 4).rearrange("p (h t) -> p h t", t=T)
                dve.tensor_tensor(dec[0][:, :].rearrange("p (h t) -> p h t", t=T),
                                  cc[:, :, end:end + 1].to_broadcast([P, 4, T]), cc, ALU.subtract).then_inc(sem("kend_arg"), 1)
                dve.wait_ge(sem("kend_exp"), d + 1)
                if d:
                    dve.wait_ge(sem("kend_turned"), 2 * d)
                dve.tensor_tensor(kend[:, :], dec[0][:, :], K[:, 8 * T:12 * T], ALU.mult).then_inc(sem("kend_ready"), 1)
                dve.wait_ge(sem("qb_exp"), d + 1)
                dve.tensor_tensor(qb[d][:, :], dec[1][:, :], qg, ALU.mult).then_inc(sem("qb_ready"), 1)
            dve.wait_ge(sem("qb_ready"), 2)
            dve.wait_ge(sem("eye_loaded"), 16)
            for g in range(2):
                dve.wait_ge(sem("diag_done"), g + 1)
                for d in range(2):
                    ins = dve.tensor_tensor(att[d][:, g * 512:(g + 1) * 512].rearrange("p (a j) -> p a j", j=P),
                                            PS[4 + g][:, :].rearrange("p (a j) -> p a j", j=P),
                                            eye[:, :][:, None, :].to_broadcast([P, 4, P]), ALU.mult)
                    ins.then_inc(sem("diag_used"), 1)
            dve.wait_ge(sem("diag_used"), 4)
            dve.wait_ge(sem("tables_loaded"), 64)
            NL = len(LEVELS)
            for n in range(2 * NL + 1):
                if n < 2 * NL:
                    d, x = n // NL, LEVELS[n % NL]
                    qh, kh, ref = (1, 0, x - 1) if d == 0 else (0, 1, x)

                    def half(t, w):
                        return t.rearrange("p (b c x) -> p b c x", c=2, x=x)[:, :, w, :]
                    cum = blk(cumx, 4 * d, 4)
                    rv = cum.rearrange("p (b x) -> p b x", x=2 * x)[:, :, ref:ref + 1].to_broadcast([P, 2 * T // x, x])
                    if n >= 2:
                        dve.wait_ge(sem("lvl_ops"), n - 1)
                    dve.tensor_tensor(half(dec[n % 2][:, :], qh), half(cum, qh), rv, ALU.subtract)
                    dve.tensor_tensor(half(dec[n % 2][:, :], kh), rv, half(cum, kh), ALU.subtract).then_inc(sem("lvl_arg"), 1)
                if n >= 1 and (n - 1) % NL:
                    m = n - 1
                    d1, l1 = m // NL, m % NL
                    dve.wait_ge(sem("lvl_scores"), m + 1)
                    mask = lvl[:, (7 * d1 + l1 - 1) * P:(7 * d1 + l1) * P][:, None, :].to_broadcast([P, 4, P])
                    for g in range(2):
                        ins = dve.copy_predicated(att[d1][:, g * 512:(g + 1) * 512].rearrange("p (a j) -> p a j", j=P), mask,
                                                  PS[level_banks[m % 2][g]][:, :].rearrange("p (a j) -> p a j", j=P))
                        ins.then_inc(sem("lvl_merged"), 1)
                    dve.wait_ge(sem("lvl_merged"), 2 * (m - m // NL))
                if n < 2 * NL:
                    dve.wait_ge(sem("lvl_exp"), n + 1)
                    if n >= 2:
                        dve.wait_ge(sem("lvl_scores"), n - 1)
                    dve.tensor_tensor(half(qk[n % 2][:, :], qh), half(dec[n % 2][:, :], qh), half(qg, qh), ALU.mult)
                    dve.tensor_tensor(half(qk[n % 2][:, :], kh), half(dec[n % 2][:, :], kh), half(kg, kh),
                                      ALU.mult).then_inc(sem("lvl_ops"), 1)
            modulation(2)
            for g in range(2):
                dve.wait_ge(sem("gla_root"), g + 1)
                own.done(dve.reciprocal(rgrp[:, g * 512:(g + 1) * 512], rgrp[:, g * 512:(g + 1) * 512]))
                own.wait()
                for b in range(4 * g, 4 * g + 4):
                    own.done(dve.scalar_tensor_tensor(blk(yf, b), PS[b // 2][:, (b % 2) * T:(b % 2 + 1) * T],
                                                      v("gla_g", b % 2), blk(rgrp, b // 2), ALU.mult, ALU.mult))
                own.wait()
                dve.tensor_tensor(blk(yf, 4 * g, 4), blk(yf, 4 * g, 4), blk(gates, 4 * g, 4), ALU.mult).then_inc(sem("operand_made"), 1)

            dve.wait_ge(sem("if_rows"), 1)
            own.done(dve.tensor_scalar(ri[:, :], PS[5][0:64, :], v("gate_b", 0)[0:64, :], None, ALU.add))
            own.done(dve.tensor_scalar(rf[:, :], PS[6][0:64, :], v("gate_b", 1)[0:64, :], None, ALU.add))
            own.wait()
            dve.scalar_tensor_tensor(rl[:, :], rf[:, :], -1.0, rf[:, :], ALU.mult, ALU.max).then_inc(sem("f_abs"), 1)
            dve.wait_ge(sem("f_ln"), 1)
            own.done(dve.scalar_tensor_tensor(rf[:, :], rf[:, :], 0.0, rl[:, :], ALU.min, ALU.subtract))
            own.wait()

            def scan(dst, src, op):
                for row, st in ((0, 1), (32, -1)):
                    a = src[row:row + 32, T:2 * T][:, ::st]
                    own.done(dve.tensor_tensor_scan(dst[row:row + 32, T:2 * T][:, ::st], a, a, 0.0, op, ALU.bypass))
                own.wait()
                for row, st, last in ((0, 1, 2 * T - 1), (32, -1, T)):
                    a = src[row:row + 32, 0:T][:, ::st]
                    own.done(dve.tensor_tensor_scan(dst[row:row + 32, 0:T][:, ::st], a, a,
                                                    dst[row:row + 32, last:last + 1], op, ALU.bypass))
                own.wait()
            scan(rl, rf, ALU.add)
            own.done(dve.tensor_tensor(rg[:, :], ri[:, :], rl[:, :], ALU.subtract))
            own.wait()
            scan(rm, rg, ALU.max)
            own.done(dve.tensor_scalar(ri[:, 0:T], rm[:, 0:T], -1.0, None, ALU.mult))
            own.wait()
            dve.tensor_tensor(rm[:, 0:T], rm[:, 0:T], rl[:, 0:T], ALU.add).then_inc(sem("m_rows"), 1)
            dve.wait_ge(sem("maskn_loaded"), 16)
            dve.wait_ge(sem("gtok_ready"), 1)
            modulation(3)
            gains(2, 64, 0, "g2")
            for n in range(9):
                if n < 8:
                    h, d = n // 2, n % 2
                    W = wgt[n % 2]
                    if n >= 2:
                        dve.wait_ge(sem("ml_done"), n - 1)
                    for t in range(2):
                        c = t * 64 + 32 * d + h
                        ins = dve.scalar_tensor_tensor(W[:, t * T:(t + 1) * T], blk(neg_g, 4 * d + h), gtok[:, c:c + 1],
                                                       blk(maskn, 2 * d + t), ALU.add, ALU.add)
                    ins.then_inc(sem("w_arg"), 1)
                    dve.wait_ge(sem("w_x"), n + 1)
                    dve.wait_ge(sem("ml_scores"), h + 1)
                    for g in range(2):
                        ins = dve.tensor_tensor(W[:, g * 512:(g + 1) * 512], W[:, g * 512:(g + 1) * 512],
                                                PS[2 * (h % 2) + g][:, :], ALU.mult)
                    ins.then_inc(sem("ml_w"), 1)
                if n >= 1:
                    m = n - 1
                    h, d = m // 2, m % 2
                    dve.wait_ge(sem("ml_done"), m + 1)
                    den = PS[6][:, 0:T]
                    own.done(dve.tensor_tensor(rden[d][:, :], den, blk(em, 4 * d + h), ALU.max))
                    own.wait()
                    own.done(dve.scalar_tensor_tensor(rden[d][:, :], den, -1.0, rden[d][:, :], ALU.mult, ALU.max))
                    own.wait()
                    own.done(dve.reciprocal(rden[d][:, :], rden[d][:, :]))
                    own.wait()
                    o2 = blk(omix, 2 * h, 2).rearrange("p (a t) -> p a t", t=T)
                    t2 = tmpo[:, :].rearrange("p (a t) -> p a t", t=T)
                    n2 = PS[4 + d][:, :].rearrange("p (a t) -> p a t", t=T)
                    rb = rden[d][:, :][:, None, :].to_broadcast([P, 2, T])
                    if d == 0:
                        dve.tensor_tensor(o2, n2, rb, ALU.mult).then_inc(sem("ml_taken"), 1)
                        continue
                    dve.tensor_tensor(t2, n2, rb, ALU.mult).then_inc(sem("ml_taken"), 1)
                    dve.wait_ge(sem("ml_taken"), m + 1)
                    dve.tensor_tensor(o2, o2, t2, ALU.add).then_inc(sem("ml_h"), 1)
                    dve.wait_ge(sem("ml_root"), h + 1)
                    own.done(dve.reciprocal(rden[h % 2][:, :], rden[h % 2][:, :]))
                    own.wait()
                    for a in range(2):
                        own.done(dve.scalar_tensor_tensor(blk(yf, 8 + 2 * h + a), blk(omix, 2 * h + a), v("ml_g", a),
                                                          rden[h % 2][:, :], ALU.mult, ALU.mult))
                    own.wait()
                    ins = dve.tensor_tensor(blk(yf, 8 + 2 * h, 2), blk(yf, 8 + 2 * h, 2), blk(gates, 8 + 2 * h, 2), ALU.mult)
                    if h % 2:
                        ins.then_inc(sem("operand_made"), 1)
                    else:
                        own.done(ins)
            for q in range(4):
                rest("y", q, yh, yl, yf)

            clear_ssq()
            dve.wait_ge(sem("R_loaded"), 16)
            for i, r in turns(dve, 16):
                split("mix_out", i, r)
                u = 4 * i + r
                dve.wait_ge(slot_used, where("mix_out", i, r) + 1)
                dve.scalar_tensor_tensor(blk(R, u), PS[r % 2][:, 0:T], mods[:, bass.ds(64 + 2 * u, 1)], blk(R, u),
                                         ALU.mult, ALU.add).then_inc(evacuated, 1)
                dve.wait_ge(evacuated, EVAC["mix_out"] + u + 1)
                accumulate(Steps(dve, sem("square_steps"), reached("steps", "n2") + 2 * u), blk(R, u), tmpx)
            recip("n2", rs[:, :])
            normed("n2", R, lambda b: amod[:, 2 * KD + b:2 * KD + b + 1], tn, x2h, x2l,
                   shift=lambda b: mview[:, 48 + b, 0:1])
            own.done(dve.memset(pad[0][:, :], 0.0))
            dve.memset(pad[1][:, :], 0.0).then_inc(sem("pads_zeroed"), 1)

            def ff_product(j, b):
                dve.wait_ge(sem("ff_silu"), j + 1)
                dve.wait_ge(slot_used, BASE["up"] + 2 * j + 2)
                if not isinstance(j, int) or j >= 2:
                    dve.wait_ge(sem("ff_x"), j - 1)
                dve.tensor_tensor(ht[b][:, :], sil[b][:, :], PS[2 * b + 1][:, 0:T], ALU.mult).then_inc(sem("ff_made"), 1)

            def ff_rest(j, b):
                dve.wait_ge(sem("ff_hi"), j + 1)
                dve.tensor_tensor(blk(hl, j), ht[b][:, :], blk(hh, j).bitcast(F32), ALU.subtract).then_inc(sem("ff_x"), 1)

            TAPS = ((accb, 0), (acc, 1), (accb, 2), (acc, 3), (accb, 6), (acc, 5), (accb, 8), (acc, 7))

            def conv(j, b, steps):
                pv = pad[b][:, :].rearrange("p (y x) -> p y x", x=66)
                for n in steps:
                    if n >= 2:
                        dve.wait_ge(sem("conv"), 9 * j + (n if n == 8 else n - 1))
                    if n == 8:
                        dve.tensor_tensor(acc[b][:, :], acc[b][:, :], accb[b][:, :], ALU.add).then_inc(sem("conv"), 1)
                        continue
                    total, t = TAPS[n]
                    a3 = total[b][:, :].rearrange("p (y x) -> p y x", x=GRID_W)
                    window = pv[:, t // 3:t // 3 + GRID_H, t % 3:t % 3 + GRID_W]
                    tap = v("conv_w", 9 * j + t)
                    ins = dve.tensor_scalar(a3, window, tap, None, ALU.mult) if n == 0 else \
                        dve.scalar_tensor_tensor(a3, window, tap, a3, ALU.mult, ALU.add)
                    ins.then_inc(sem("conv"), 1)

            for i, r in turns(dve, 2 * KF, lead=1):
                split("up", i, r)
                j, b = 2 * i + r // 2, r // 2
                first = isinstance(i, int) and i == 0 and r < 2
                if r % 2 == 0:
                    if not first:
                        ff_product(j - 1, 1 - b)
                    dve.wait_ge(sem("gate_used"), j + 1)
                    if not isinstance(j, int) or j >= 2:
                        dve.wait_ge(sem("conv"), 9 * j - 9)
                    conv(j, b, range(5))
                else:
                    conv(j, b, range(5, 9))
                    if not first:
                        ff_rest(j - 1, 1 - b)
            ff_product(KF - 1, 0)
            ff_rest(KF - 1, 0)
            for i, r in turns(dve, KF):
                split("down", i, r)
            dve.wait_ge(slot_used, BASE["down"] + KF)
            for b in range(KD):
                ins = dve.scalar_tensor_tensor(blk(R, b), PS[b // 2][:, (b % 2) * T:(b % 2 + 1) * T],
                                               mods[:, 160 + 2 * b:161 + 2 * b], blk(R, b), ALU.mult, ALU.add)
                if b % 4 == 3:
                    ins.then_inc(sem("part_ready"), 1)
            recip("nf", rs[:, :])
            for q in range(5):
                if q < 4:
                    for b in range(4 * q, 4 * q + 4):
                        ins = dve.scalar_tensor_tensor(blk(R, b), blk(R, b), v("gfin", b), rs[:, :], ALU.mult, ALU.mult)
                    ins.then_inc(sem("part_ready"), 1)
                if q:
                    gained_rest("np", q - 1, R, "pre0", xph, xpl)
            add_squares("np", sqp)
            for t in (up[0], up[1], ws[0]):
                own.done(dve.memset(t[:, :], 0.0))
            dve.memset(ws[1][:, :], 0.0).then_inc(sem("ups_zeroed"), 1)
            dve.wait_ge(sem("ups_zeroed"), 1)
            recip("np", rs[:, :])

            for g in range(4):
                with dve.Fori(4 * g, 4 * g + 4) as i:
                    for r in range(4):
                        split("pool_in", i, r)
                        u = 2 * i + r // 2
                        if r % 2:
                            dve.wait_ge(slot_used, where("pool_in", i, r) + 1)
                            dve.tensor_tensor(blk(sg, u), PS[r][:, 0:T], rs[:, :], ALU.mult).then_inc(evacuated, 1)
                            dve.wait_ge(sem("pool_hi"), u + 1)
                            dve.tensor_tensor(blk(pl, u), pf[:, :], blk(ph, u).bitcast(F32), ALU.subtract).then_inc(sem("pool_x"), 1)
                            continue
                        buf = up[r // 2]
                        st = Steps(dve, sem("window_steps"), 8 * sum(range(2, g + 2)) + (g + 2) * (u - 8 * g))
                        dve.wait_ge(slot_used, where("pool_in", i, r) + 1)
                        dve.wait_ge(sem("pool_x"), u)
                        dve.tensor_tensor(buf[:, 16:UPW], PS[r][:, 0:T], rs[:, :], ALU.mult).then_inc(evacuated, 1)
                        dve.wait_ge(evacuated, EVAC["pool_in"] + (4 * i + (r + 1)))
                        src = buf
                        for l in range(g + 1):
                            dst, lag = ws[l % 2], 1 << l
                            st.done(dve.tensor_tensor(dst[:, 16:UPW], src[:, 16:UPW], src[:, 16 - lag:UPW - lag], ALU.add))
                            st.wait()
                            src = dst
                        st.done(dve.tensor_tensor(src[:, 16:32], src[:, 16:32], v("corr", 16 * g, 16), ALU.mult))
                        st.wait()
                        dve.scalar_tensor_tensor(pf[:, :], src[:, 16:UPW], 1.0 / WINDOWS[g], buf[:, 16:UPW],
                                                 ALU.mult, ALU.subtract).then_inc(sem("pool_made"), 1)
            dve.wait_ge(sem("sg_ready"), 32)
            for i, r in turns(dve, 16):
                split("group", i, r)
                s = 4 * i + r
                dve.wait_ge(slot_used, where("group", i, r) + 1)
                dve.wait_ge(sem("y2_x"), s)
                for a in range(2):
                    ins = dve.scalar_tensor_tensor(gt[r % 2][:, a * T:(a + 1) * T], PS[r % 2][:, a * T:(a + 1) * T],
                                                   vec[:, bass.ds(2 * s + (VEC["pscale"] + a), 1)], blk(sg, 2 * s + a),
                                                   ALU.mult, ALU.mult)
                ins.then_inc(evacuated, 1)
                dve.wait_ge(sem("y2_hi"), s + 1)
                dve.tensor_tensor(blk(y2l, 2 * s, 2), gt[r % 2][:, :], blk(y2h, 2 * s, 2).bitcast(F32),
                                  ALU.subtract).then_inc(sem("y2_x"), 1)
            def p_rest(tag, ptr, pth, ptl):
                dve.wait_ge(sem(f"p{tag}_hi"), 1)
                dve.tensor_tensor(ptl[:, :], ptr[:, :], pth[:, :].bitcast(F32), ALU.subtract).then_inc(sem(f"p{tag}_x"), 1)

            def after_block(tag, squares, xh_, xl_):
                split(f"proj{tag}", 0, 0)
                recip(f"post{tag}", rs[:, :])
                for q in range(5):
                    if q < 4:
                        for b in range(4 * q, 4 * q + 4):
                            own.done(dve.scalar_tensor_tensor(blk(O, b), blk(O, b), v(f"post{tag}", b), rs[:, :], ALU.mult, ALU.mult))
                        own.wait()
                        dve.tensor_tensor(blk(R, 4 * q, 4), blk(R, 4 * q, 4), blk(O, 4 * q, 4), ALU.add).then_inc(sem("part_ready"), 1)
                    if q:
                        gained_rest(f"ple{tag}", q - 1, R, f"ple{tag}", xh_, xl_)
                add_squares(f"ple{tag}", squares)
                split(f"proj{tag}", 0, 1)
                recip(f"ple{tag}", rs[:, :])

            def gated(tag, pj, tail=0):
                dve.memset(ssq[:, :], 0.0).then_inc(sem(f"gate{tag}_used"), 1)
                dve.wait_ge(sem(f"gate{tag}_used"), 1)

                def finish(u, b):
                    dve.wait_ge(sem(f"gate{tag}_ready"), u + 1)
                    dve.tensor_tensor(sgt[b][:, :], sgt[b][:, :], blk(pj, u), ALU.mult).then_inc(sem(f"gate{tag}_mult"), 1)
                    dve.wait_ge(sem(f"gate{tag}_mult"), u + 1)
                    dve.tensor_tensor(blk(R, u), blk(R, u), sgt[b][:, :], ALU.add).then_inc(sem(f"gate{tag}_used"), 1)
                    if tag == 0:
                        dve.wait_ge(sem(f"gate{tag}_used"), u + 2)
                        accumulate(Steps(dve, sem("square_steps"), reached("steps", "m") + 2 * u), blk(R, u), tmpg)

                def next_rest(u):
                    dve.wait_ge(sem("operand_hi"), reached("hi", "m", 1) + u)
                    dve.scalar_tensor_tensor(blk(xml, u), blk(R, u), v("pre1", u), blk(xmh, u).bitcast(F32),
                                             ALU.mult, ALU.subtract).then_inc(sem("operand_rest"), 1)

                for i, r in turns(dve, 16, tail, lead=1):
                    split(f"plegate{tag}", i, r)
                    u = 4 * i + r
                    dve.wait_ge(slot_used, where(f"plegate{tag}", i, r) + 1)
                    if not isinstance(u, int) or u >= 2:
                        dve.wait_ge(sem(f"gate{tag}_used"), u)
                    dve.tensor_tensor(sgt[r % 2][:, :], PS[r % 2][:, 0:T], rs[:, :], ALU.mult).then_inc(evacuated, 1)
                    if not isinstance(u, int) or u >= 1:
                        finish(u - 1, (r + 1) % 2)
                    if tag == 0 and (not isinstance(u, int) or u >= 2):
                        next_rest(u - 2)
                finish(KD - 1, 1)
                if tag == 0:
                    next_rest(KD - 2)
                    next_rest(KD - 1)

            p_rest(0, ptr0, pth0, ptl0)
            for i, r in turns(dve, 32):
                split("pool_out", i, r)
            dve.wait_ge(slot_used, BASE["pool_out"] + 32)
            for b in (4, 5, 6, 7, 0, 1, 2, 3):
                dve.tensor_copy(blk(O, 2 * b, 2), PS[b][:, :]).then_inc(sem("O_copied"), 1)
            after_block(0, ot, gxh, gxl)
            gated(0, pj0)

            dve.wait_ge(sem("pos_loaded"), 16)
            own.done(dve.tensor_copy(ang[2][:, :], post[:, :]))
            own.wait()
            own.done(dve.tensor_scalar(ang[0][:, :], ang[2][:, :], v("invf"), None, ALU.mult))
            own.wait()
            own.done(dve.tensor_scalar(ang[3][:, :], ang[0][:, :], float(1 / (2 * np.pi)), None, ALU.mult))
            own.wait()
            own.done(dve.tensor_scalar(ang[3][:, :], ang[3][:, :], 12582912.0, None, ALU.add))
            own.wait()
            own.done(dve.tensor_scalar(ang[3][:, :], ang[3][:, :], -12582912.0, None, ALU.add))
            own.wait()
            for part in TWO_PI:
                own.done(dve.scalar_tensor_tensor(ang[0][:, :], ang[3][:, :], -part, ang[0][:, :], ALU.mult, ALU.add))
                own.wait()
            own.done(dve.tensor_scalar(ang[0][:, :], ang[0][:, :], 3.1415925, -3.1415925, ALU.min, ALU.max))
            own.wait()
            dve.scalar_tensor_tensor(ang[1][:, :], ang[0][:, :], -1.0, ang[0][:, :], ALU.mult, ALU.max).then_inc(sem("ang_ready"), 1)
            recip("m", rs[:, :])
            own.done(dve.memset(ssqk[:, :], 0.0))
            clear_ssq()

            def rotate(d1, d2, x1, x2, signal=None):
                cos, sin = cs[:, 0:T], cs[:, T:2 * T]
                own.wait()
                for n, (a, c) in enumerate(((x1, cos), (x2, sin), (x2, cos), (x1, sin))):
                    own.done(dve.tensor_tensor(rt[n][:, :], a, c, ALU.mult))
                own.wait()
                own.done(dve.tensor_tensor(d1, rt[0][:, :], rt[1][:, :], ALU.subtract))
                ins = dve.tensor_tensor(d2, rt[2][:, :], rt[3][:, :], ALU.add)
                ins.then_inc(sem(signal), 1) if signal else own.done(ins)

            for j in range(26):
                split("mla_in", j // 4, j % 4)
                dst = blk(ql, j) if j < 8 else blk(kpr, j - 8) if j < 10 else blk(sg2, j - 10)
                dve.wait_ge(slot_used, BASE["mla_in"] + j + 1)
                dve.tensor_tensor(dst, PS[j % 2][:, 0:T], rs[:, :], ALU.mult).then_inc(evacuated, 1)
                if j < 10:
                    dve.wait_ge(evacuated, EVAC["mla_in"] + j + 1)
                if j < 8:
                    accumulate(Steps(dve, sem("square_steps"), reached("steps", "q") + 2 * j), blk(ql, j), rt[3], ssq if j < 4 else ssqk)
                if j == 14:
                    recip("q", rsq[:, :])
                    recip("kv", rsk[:, :])
                    normed("lat", ql, lambda b: v("q_norm", b) if b < 4 else v("kv_norm", b - 4), ql, lath, latl,
                           inv=lambda b: rsq if b < 4 else rsk, quads=2)
                if j == 9:
                    dve.wait_ge(sem("rope_cs"), 2)
                    dve.wait_ge(sem("square_steps"), reached("steps", "kv", 8))
                    rotate(kp[:, 0:T], kp[:, T:2 * T], kpr[:, 0:T], kpr[:, T:2 * T])
            dve.wait_ge(sem("operand_rest"), reached("x", "lat", 2))
            for s in range(6):
                split("uq", s // 4, s % 4)
                if s >= 4:
                    dve.wait_ge(evacuated, EVAC["uq"] + s + 1)
                    for a in range(2):
                        m = 2 * (s - 4) + a
                        rotate(blk(qp, m), blk(qp, 4 + m), blk(qraw, 2 * a), blk(qraw, 2 * a + 1), a and "q_rot")
            for name in ("uk", "uv"):
                for s in range(4):
                    split(name, 0, s)
            dve.wait_ge(sem("maska_loaded"), 16)
            dve.wait_ge(sem("sg2_ready"), 16)
            for n in range(NH + 4):
                if n < NH:
                    b = n % 2
                    c = 8 * n
                    dve.wait_ge(sem("scores_done"), n + 1)
                    if n >= 2:
                        dve.wait_ge(sem("p_exp"), 2 * (n - 1))
                    dve.tensor_tensor(s_[b][:, :], PS[b][:, 0:3 * P], maska[:, :], ALU.add).then_inc(sem("s_masked"), 1)
                    dve.wait_ge(sem("s_masked"), n + 1)
                    own.done(dve.reduce_max(stat[:, c + 4:c + 5], s_[b][:, 0:P], AX))
                    own.done(dve.reduce_max(stat[:, c + 5:c + 6], s_[b][:, P:3 * P], AX))
                    own.wait()
                    dve.tensor_scalar(stat[:, c:c + 2], stat[:, c + 4:c + 6], -SM_SCALE, None, ALU.mult).then_inc(sem("s_max"), 1)
                if 1 <= n <= NH:
                    h = n - 1
                    c, b = 8 * h, h % 3
                    dve.wait_ge(sem("p_exp"), 2 * h + 2)
                    own.done(dve.reciprocal(stat[:, c + 6:c + 8], stat[:, c + 2:c + 4]))
                    own.wait()
                    dve.tensor_scalar(p_[b][:, 0:P], p_[b][:, 0:P], stat[:, c + 6:c + 7], None, ALU.mult)
                    dve.tensor_scalar(p_[b][:, P:3 * P], p_[b][:, P:3 * P], stat[:, c + 7:c + 8], None,
                                      ALU.mult).then_inc(sem("p_norm"), 1)
                if 3 <= n <= NH + 2:
                    h = n - 3
                    dve.wait_ge(sem("pv_done"), h + 1)
                    if h >= 2:
                        dve.wait_ge(sem("y3_x"), h - 1)
                    dve.tensor_tensor(yt[h % 2][:, :], PS[2 + h % 2][:, 0:T], blk(sg2, h), ALU.mult).then_inc(sem("o_made"), 1)
                if n >= 4:
                    h = n - 4
                    dve.wait_ge(sem("y3_hi"), h + 1)
                    dve.tensor_tensor(blk(y3l, h), yt[h % 2][:, :], blk(y3h, h).bitcast(F32), ALU.subtract).then_inc(sem("y3_x"), 1)
            clear_ssq()
            p_rest(1, ptr1, pth1, ptl1)
            for i, r in turns(dve, 16):
                split("mla_out", i, r)
                u = 4 * i + r
                dve.wait_ge(evacuated, EVAC["mla_out"] + u + 1)
                accumulate(Steps(dve, sem("square_steps"), reached("steps", "post1") + 2 * u), blk(O, u), tmpq)
            after_block(1, ot1, fxh, fxl)
            gated(1, pj1, tail=4)

        @block.tensor
        def _(pe):
            def mm3(o, wh, wl, ah, al, start, stop, swap=False):
                kw = dict(skip_group_check=True)
                if swap:
                    pe.matmul(o, ah, wh, start=start, stop=False, **kw)
                    pe.matmul(o, ah, wl, start=False, stop=False, **kw)
                    return pe.matmul(o, al, wh, start=False, stop=stop, **kw)
                pe.matmul(o, wh, ah, start=start, stop=False, **kw)
                pe.matmul(o, wh, al, start=False, stop=False, **kw)
                return pe.matmul(o, wl, ah, start=False, stop=stop, **kw)

            def slot(phase, i, r, product, count=BLOCKS):
                s = where(phase, i, r)
                p = (BASE[phase] + r) % PAIR
                for n in range(count):
                    if n % (count // 2) == 0:
                        pe.wait_ge(lo_ready, 2 * s + n // (count // 2) + 1)
                    c = slice(n * SLOT // count, (n + 1) * SLOT // count)
                    ins = product(n, HI[p][:, c], LO[p][:, c])
                ins.then_inc(slot_used, 1)

            def out_block(phase, i, r, ah, al, bank, operand=None):
                def product(n, h, l):
                    if operand and isinstance(i, int) and i + r == 0:
                        if operand == "m":
                            pe.wait_ge(sem("operand_rest"), reached("x", operand, n + 1))
                        elif n % 4 == 0:
                            pe.wait_ge(sem("operand_rest"), reached("x", operand, n // 4 + 1))
                    return mm3(PS[bank][:, 0:T], h, l, blk(ah, n), blk(al, n), n == 0, n == 15)
                slot(phase, i, r, product)

            def out_major(phase, i, r, ah, al, operand=None):
                u = 4 * i + r
                if not isinstance(u, int) or EVAC[phase] + u - 1 > 0:
                    pe.wait_ge(evacuated, EVAC[phase] + u - 1)
                out_block(phase, i, r, ah, al, r % 2, operand)

            def sum_squares(name, kind, o=None, src=None):
                done = dict(SHARED[kind])[name]
                pe.wait_ge(sem({"steps": "square_steps", "ssq": "ssq_ready"}[kind]), reached(kind, name, done))
                src = ssq[:, :] if src is None else src
                o = PS[2][:, 0:T] if o is None else o
                pe.matmul(o, ones[:, :], src, start=True, stop=True, skip_group_check=True).then_inc(sem("norm_sum"), 1)

            def add_squares(name, src, o, quads=4):
                per = dict(SHARED["squares"])[name] // quads
                for q in range(quads):
                    pe.wait_ge(sem("squares_ready"), reached("squares", name, per * (q + 1)))
                    for b in range(KD // quads * q, KD // quads * (q + 1)):
                        ins = pe.matmul(o, ones[:, :], blk(src, b), start=b == 0, stop=b == KD - 1, skip_group_check=True)
                ins.then_inc(sem("norm_sum"), 1)

            def mod_block(u, n, place, g, start=False, stop=False):
                k = 4 * (u % 4) + n
                lo = k * MW + 2 * (MGROUPS - 1 - g)
                ins = pe.matmul(PS[7][0:16, :], cwin[:, lo:lo + 16], RAW[place][:, n * 512:(n + 1) * 512], start=start, stop=stop,
                                skip_group_check=True)
                if n == 3:
                    ins.then_inc(mod_used, 1)

            def turn_rows(n):
                pe.wait_ge(sem("mod_rows"), n + 1)
                for q in range(4):
                    ins = pe.transpose(PS[turned_bank(n)][:, q * 16:(q + 1) * 16], mrows[n][:, q * P:(q + 1) * P], eye[0:16, 0:16])
                ins.then_inc(sem("mod_turned"), 1)

            filled = [0]

            def fill(count):
                for _ in range(count):
                    c = filled[0]
                    filled[0] += 1
                    u, n = c // 4, c % 4
                    q = u if u < EARLY else MOD_AT + u
                    if n == 0:
                        pe.wait_ge(raw_loaded[q % RING], 16 * (q // RING + 1))
                    m = max(m for m in range(len(ROUNDS)) if MSTART[m] <= u)
                    mod_block(u, n, q % RING, (u - MSTART[m]) // 4, c == 4 * MSTART[m], c == 4 * MSTART[m + 1] - 1)

            pe.wait_ge(sem("c_ready"), 1)
            fill(2 * MSTART[1])
            pe.wait_ge(sem("ssq_ready"), reached("ssq", "n1", 2))
            pe.wait_ge(sem("ones_ready"), 1)
            pe.matmul(PS[2][:, :], ones[:, :], ssqx[:, :], start=True, stop=True).then_inc(sem("norm_sum"), 1)
            fill(2 * MSTART[1])
            pe.wait_ge(sem("eye_loaded"), 16)
            turn_rows(0)
            fill(4 * (EARLY - MSTART[1]))

            xhv = xh[:, :].rearrange("p (s k t) -> p s k t", s=2, k=KD)
            xlv = xl[:, :].rearrange("p (s k t) -> p s k t", s=2, k=KD)

            def both(phase, i, r, bank):
                o = PS[bank][:, :].rearrange("p (s t) -> p s t", s=2)

                def product(n, h, l):
                    if phase == "lr" and n % 4 == 0:
                        pe.wait_ge(sem("operand_rest"), reached("x", "x1", n // 2 + 2))
                    return mm3(o, h, l, xhv[:, :, n, :], xlv[:, :, n, :], n == 0, n == 15)
                slot(phase, i, r, product)
            both("lr", 0, 0, 0)
            pe.wait_ge(sem("mods_ready"), 1)
            turn_rows(1)
            for b in range(8):
                pe.wait_ge(evacuated, max(EVAC["key"] + b - 1, 1))
                both("key", b // 4, b % 4, b % 2)
            pe.wait_ge(evacuated, EVAC["value"])
            pe.wait_ge(sem("mods_ready"), 2)
            with pe.Fori(0, 2) as i:
                for r in range(8):
                    g, q = r // 4, r % 4
                    if q == 0:
                        pe.wait_ge(evacuated, EVAC["value"] + 8 * i + (4 * g - 4))

                    def product(n, h, l):
                        for tt in range(4):
                            k, s = 4 * q + n, tt // 2
                            c = slice((s * KD + k) * T + (tt % 2) * P, (s * KD + k) * T + (tt % 2 + 1) * P)
                            ins = mm3(PS[4 * g + tt][:, :], h, l, xh[:, c], xl[:, c], k == 0, k == 15, swap=True)
                        return ins
                    slot("value", 2 * i, r, product, count=4)
            pe.wait_ge(evacuated, EVAC["query"])
            for b in range(8):
                out_major("query", b // 4, b % 4, xh, xl)
            for i, r in turns(pe, 16):
                out_major("gate", i, r, xh, xl)

            pe.wait_ge(evacuated, EVAC["mix_out"])
            pe.wait_ge(sem("tables_loaded"), 64)
            for n in range(8):
                pe.matmul(PS[n][:, :], w_lr[:, n * P:(n + 1) * P], zlr[0:16, :], start=True, stop=True).then_inc(sem("dec_z"), 1)
            pe.wait_ge(sem("dec_abs"), 1)
            fill(FILL[0])
            for g in range(2):
                for a in range(4):
                    h, t = 2 * g + a // 2, a % 2
                    c = slice(h * T + t * P, h * T + (t + 1) * P)
                    ins = pe.matmul(PS[4 + g][:, a * P:(a + 1) * P], K[:, c], Q[:, c], start=True, stop=True)
                ins.then_inc(sem("diag_done"), 1)
            for d in range(2):
                fill(FILL[1])
                pe.wait_ge(sem("kend_ready"), d + 1)
                for t in range(2):
                    if d:
                        pe.wait_ge(sem("kend_t_ready"), 2)
                    for h in range(HEADS):
                        ins = pe.transpose(PS[t][:, h * P:(h + 1) * P], kend[:, h * T + t * P:h * T + (t + 1) * P], eye[:, :])
                    ins.then_inc(sem("kend_turned"), 1)
                fill(FILL[2])
                pe.wait_ge(sem("kend_t_ready"), 2 * d + 2)
                for g in range(2):
                    if d:
                        pe.wait_ge(sem("state_ready"), 2)
                    for h in (2 * g, 2 * g + 1):
                        for t in range(2):
                            ins = pe.matmul(PS[2 + g][:, (h % 2) * DV:(h % 2 + 1) * DV], kend_t[:, t * 512 + h * P:t * 512 + (h + 1) * P],
                                            V[:, (2 + t) * 2048 + h * DV:(2 + t) * 2048 + (h + 1) * DV], start=t == 0, stop=t == 1,
                                            skip_group_check=True)
                    ins.then_inc(sem("state_done"), 1)
            NL = len(LEVELS)
            pe.wait_ge(sem("diag_used"), 4)
            for n in range(2 * NL):
                d, l = n // NL, n % NL
                fill(min(FILL[3], 4 * MSTART[3] - filled[0]) if n < 2 * NL - 1 else 4 * MSTART[3] - filled[0])
                pe.wait_ge(sem("lvl_ops"), n + 1)
                if n == 1:
                    pe.wait_ge(sem("state_ready"), 4)
                if n >= 2:
                    m = n - 2
                    if m // NL or m % NL:
                        pe.wait_ge(sem("lvl_merged"), 2 * (m - m // NL))
                    pe.wait_ge(sem("cross_ready"), m // NL + 1)
                for a in range(4 if l == 0 else 8):
                    if l == 0:
                        kt, qt = (0, 1) if d == 0 else (1, 0)
                        ck, cq, o = a * T + kt * P, a * T + qt * P, PS[4][:, a * P:(a + 1) * P]
                    else:
                        ck = cq = a * P
                        o = PS[level_banks[n % 2][a // 4]][:, (a % 4) * P:(a % 4 + 1) * P]
                    ins = pe.matmul(o, qk[n % 2][:, ck:ck + P], qk[n % 2][:, cq:cq + P], start=True, stop=True,
                                    skip_group_check=True)
                ins.then_inc(sem("lvl_scores"), 1)
            pe.wait_ge(sem("lvl_merged"), 4 * (NL - 1))
            pe.wait_ge(sem("cross_ready"), 2)
            pe.wait_ge(sem("state_ready"), 4)
            for h in range(HEADS):
                for a in range(2):
                    o = PS[h][:, a * T:(a + 1) * T]
                    vc = h * DV + a * P
                    kw = dict(skip_group_check=True)
                    for d in range(2):
                        pe.matmul(o, state[d][:, vc:vc + P], qb[d][:, h * T:(h + 1) * T], start=d == 0, stop=False, **kw)
                    for d in range(2):
                        for t in range(2):
                            pe.matmul(o[:, t * P:(t + 1) * P], V[:, t * 2048 + vc:t * 2048 + vc + P],
                                      att[d][:, (2 * h + t) * P:(2 * h + t + 1) * P], start=False, stop=False, **kw)
                        kt, qt = (0, 1) if d == 0 else (1, 0)
                        ins = pe.matmul(o[:, qt * P:(qt + 1) * P], V[:, kt * 2048 + vc:kt * 2048 + vc + P],
                                        cross[d][:, h * P:(h + 1) * P], start=False, stop=d == 1, **kw)
                ins.then_inc(sem("gla_out"), 1)
                if h == 0:
                    turn_rows(2)
                fill(FILL[4])
            for g in range(2):
                for h in (2 * g, 2 * g + 1):
                    pe.wait_ge(sem("gla_sq"), h + 1)
                    for a in range(2):
                        ins = pe.matmul(PS[4 + g][:, (h % 2) * T:(h % 2 + 1) * T], ones[:, :], blk(osq, 2 * h + a),
                                        start=a == 0, stop=a == 1, skip_group_check=True)
                ins.then_inc(sem("gla_sum"), 1)
                fill(FILL[5])

            pe.wait_ge(sem("gla_root"), 2)
            pe.wait_ge(sem("mods_ready"), 3)
            for n in range(2):
                ins = pe.matmul(PS[5 + n][0:64, :], sel_if[:, n * 64:(n + 1) * 64], zlr[0:32, :], start=True, stop=True)
            ins.then_inc(sem("if_rows"), 1)
            fill(FILL[6])
            pe.wait_ge(sem("m_rows"), 1)
            for src, ready, done, banks in ((ri, "m_rows", "neg_g_rep", (0, 1, 2, 3)), (rm, "em_rows", "em_rep", (4, 5, 6, 3))):
                pe.wait_ge(sem(ready), 1)
                for n in range(8):
                    if n == 6 and src is rm:
                        pe.wait_ge(sem("neg_g_ready"), 4)
                    ins = pe.matmul(PS[banks[n // 2]][:, (n % 2) * T:(n % 2 + 1) * T], rep_sel[:, n * P:(n + 1) * P],
                                    src[:, 0:T], start=True, stop=True, skip_group_check=True)
                    if n % 2:
                        ins.then_inc(sem(done), 1)
            pe.wait_ge(sem("neg_g_ready"), 4)
            for t in range(4):
                ins = pe.transpose(PS[0][:, t * 64:(t + 1) * 64], rg[:, t * P:(t + 1) * P], eye[0:64, 0:64])
            ins.then_inc(sem("g_turned"), 1)
            fill(4 * MSLOTS - filled[0])
            turn_rows(3)
            pe.wait_ge(sem("gtok_ready"), 1)
            pe.wait_ge(sem("em_ready"), 4)

            def ml_scores(h):
                if h >= 2:
                    pe.wait_ge(sem("ml_w"), 2 * h - 2)
                for s in range(2):
                    for t in range(2):
                        c = (8 * s + 4 + h) * T + t * P
                        ins = pe.matmul(PS[2 * (h % 2) + s][:, t * T:(t + 1) * T], K[:, c:c + P], blk(Q, 4 + h),
                                        start=True, stop=True, skip_group_check=True)
                ins.then_inc(sem("ml_scores"), 1)
            ml_scores(0)
            for n in range(9):
                h, d = n // 2, n % 2
                if n < 8:
                    if d == 0 and h + 1 < HEADS:
                        ml_scores(h + 1)
                    W = wgt[n % 2]
                    pe.wait_ge(sem("ml_w"), n + 1)
                    if n >= 2:
                        pe.wait_ge(sem("ml_taken"), n - 1)
                    for a in range(3):
                        if a == 2 and n:
                            pe.wait_ge(sem("ml_taken"), n)
                        for t in range(4):
                            vc = t * 2048 + 1024 + h * DV + a * P
                            w = V[:, vc:vc + P] if a < 2 else ones[:, :]
                            o = PS[4 + d][:, a * T:(a + 1) * T] if a < 2 else PS[6][:, 0:T]
                            ins = pe.matmul(o, w, W[:, t * T:(t + 1) * T], start=t == 0, stop=t == 3, skip_group_check=True)
                    ins.then_inc(sem("ml_done"), 1)
                if n >= 2 and d == 0:
                    pe.wait_ge(sem("ml_sq"), h)
                    if h == 1:
                        pe.wait_ge(sem("mods_ready"), 4)
                    if h >= 2:
                        pe.wait_ge(sem("ml_root"), h - 1)
                    for a in range(2):
                        ins = pe.matmul(PS[7][:, 0:T], ones[:, :], tmpo[:, a * T:(a + 1) * T], start=a == 0, stop=a == 1)
                    ins.then_inc(sem("ml_sum"), 1)

            for i, r in turns(pe, 16, lead=1):
                out_major("mix_out", i, r, yh, yl, "y")
            sum_squares("n2", "steps")
            for i, r in turns(pe, 2 * KF, lead=1):
                if not isinstance(i, int) or i:
                    pe.wait_ge(sem("ff_made" if r % 2 else "gate_used"), 2 * i + (r // 2 - 1))
                out_block("up", i, r, x2h, x2l, r, "n2")
            pe.wait_ge(sem("gate_used"), KF)
            pe.wait_ge(sem("ff_made"), KF)
            pe.wait_ge(sem("ff_x"), KF)
            pe.wait_ge(sem("norm_root"), reached("root", "n2", 1))

            def k_major(phase, ah, al):
                def one(i, r, u, first=False):
                    return slot(phase, i, r, lambda n, h, l: mm3(
                        PS[n // 2][:, (n % 2) * T:(n % 2 + 1) * T], h, l, blk(ah, u), blk(al, u), first and n % 2 == 0, False))
                for r in range(4):
                    one(0, r, r, first=r == 0)
                n = COUNT[phase] // 4
                with pe.Fori(1, n) as i:
                    for r in range(4):
                        one(i, r, 4 * i + r)
                for u in range(4 * n, COUNT[phase]):
                    one(n, u % 4, u)
            k_major("down", hh, hl)
            add_squares("nf", tn, PS[0][:, 0:T])

            for i, r in turns(pe, 64, lead=1):
                if not isinstance(i, int) or i:
                    pe.wait_ge(evacuated, EVAC["pool_in"] + (4 * i + (r - 3)))
                out_block("pool_in", i, r, xph, xpl, r, "np")
                if isinstance(i, int) and i + r == 0:
                    sum_squares("np", "ssq", PS[4][:, 0:T])
            for i, r in turns(pe, 16):
                u = 4 * i + r
                pe.wait_ge(sem("pool_x"), 8 * i + 8)
                pe.wait_ge(evacuated, EVAC["group"] + u - 1)
                slot("group", i, r, lambda n, h, l: mm3(
                    PS[r % 2][:, (n // 8) * T:(n // 8 + 1) * T], h, l, blk(ph, 8 * i + n % 8), blk(pl, 8 * i + n % 8),
                    n % 8 == 0, n % 8 == 7))
            pe.wait_ge(sem("y2_x"), 16)
            k_major("pool_out", y2h, y2l)

            def proj(tag, pth, ptl, s):
                if s:
                    pe.wait_ge(evacuated, EVAC[f"proj{tag}"] + 1)
                slot(f"proj{tag}", 0, s, lambda n, h, l: mm3(
                    PS[4 + n // 4][:, (n // 2 % 2) * T:(n // 2 % 2 + 1) * T], h, l, blk(pth, n % 2), blk(ptl, n % 2),
                    n % 2 == 0, n % 2 == 1))

            def gate(tag, gh, gl, tail=0):
                for i, r in turns(pe, 16, tail, lead=1):
                    out_major(f"plegate{tag}", i, r, gh, gl, f"ple{tag}")
                    if isinstance(i, int) and i + r == 0:
                        sum_squares(f"ple{tag}", "ssq")

            pe.wait_ge(sem("p0_x"), 1)
            pe.wait_ge(sem("O_copied"), 4)
            proj(0, pth0, ptl0, 0)
            pe.wait_ge(sem("O_copied"), 8)
            add_squares("post0", ot, PS[2][:, 0:T], 1)
            proj(0, pth0, ptl0, 1)
            gate(0, gxh, gxl)

            for j in range(26):
                out_major("mla_in", j // 4, j % 4, xmh, xml, "m")
                if j == 0:
                    sum_squares("m", "steps")
                if j == 10:
                    sum_squares("q", "steps")
                    sum_squares("kv", "steps", PS[3][:, 0:T], ssqk[:, :])
            pe.wait_ge(sem("operand_rest"), reached("x", "lat", 2))
            pe.wait_ge(evacuated, EVAC["uq"])
            for name, n_slots, first in (("uq", 6, 0), ("uk", 4, 4)):
                for s in range(n_slots):
                    e = EVAC[name] + (s - 1)
                    pe.wait_ge(evacuated, e)
                    slot(name, s // 4, s % 4, lambda n, h, l: mm3(
                        PS[2 * (s % 2) + n // 8][:, (n // 4 % 2) * T:(n // 4 % 2 + 1) * T], h, l,
                        blk(lath, first + n % 4), blk(latl, first + n % 4), n % 4 == 0, n % 4 == 3))
            for s in range(4):
                pe.wait_ge(evacuated, EVAC["uv"] + s - 1)

                def product(n, h, l):
                    for t in range(2):
                        c = slice((4 + n) * T + t * P, (4 + n) * T + (t + 1) * P)
                        ins = mm3(PS[2 * (s % 2) + t][:, :], h, l, lath[:, c], latl[:, c], n == 0, n == 3, swap=True)
                    return ins
                slot("uv", 0, s, product, count=4)
            pe.wait_ge(evacuated, EVAC["mla_out"])
            pe.wait_ge(sem("q_rot"), 2)
            for n in range(NH + 3):
                if n < NH:
                    m, row = n // 4, 32 * (n % 4)
                    if n >= 2:
                        pe.wait_ge(sem("s_masked"), n - 1)
                    for t in range(2):
                        o = PS[n % 2][:, P * t:P * t + P * (t + 1)]
                        pe.matmul(o, qn[:, n * T + t * P:n * T + (t + 1) * P], kn[:, n * T:n * T + (t + 1) * P],
                                  start=True, stop=False, skip_group_check=True)
                        for a in range(2):
                            ins = pe.matmul(o, qp[row:row + 32, (4 * a + m) * T + t * P:(4 * a + m) * T + (t + 1) * P],
                                            kp[row:row + 32, a * T:a * T + (t + 1) * P], start=False, stop=a == 1,
                                            skip_group_check=True)
                    ins.then_inc(sem("scores_done"), 1)
                if 2 <= n <= NH + 1:
                    h = n - 2
                    pe.wait_ge(sem("p_norm"), h + 1)
                    if h >= 2:
                        pe.wait_ge(sem("pt_ready"), h - 1)
                    for t in range(3):
                        ins = pe.transpose(PS[4 + h % 2][:, t * P:(t + 1) * P], p_[h % 3][:, t * P:(t + 1) * P], eye[:, :])
                    ins.then_inc(sem("p_turned"), 1)
                if n >= 3:
                    h = n - 3
                    pe.wait_ge(sem("pt_ready"), h + 1)
                    if h >= 2:
                        pe.wait_ge(sem("o_made"), h - 1)
                    va, vb, w = v2[:, h * P:(h + 1) * P], v2[:, 2048 + h * P:2048 + (h + 1) * P], pt[h % 2]
                    o = PS[2 + h % 2]
                    pe.matmul(o[:, 0:P], va, w[:, 0:P], start=True, stop=True, skip_group_check=True)
                    pe.matmul(o[:, P:T], va, w[:, P:2 * P], start=True, stop=False, skip_group_check=True)
                    pe.matmul(o[:, P:T], vb, w[:, 2 * P:3 * P], start=False, stop=True,
                              skip_group_check=True).then_inc(sem("pv_done"), 1)
            pe.wait_ge(sem("y3_x"), 16)
            for i, r in turns(pe, 16):
                out_major("mla_out", i, r, y3h, y3l)
            pe.wait_ge(sem("p1_x"), 1)
            proj(1, pth1, ptl1, 0)
            sum_squares("post1", "steps")
            proj(1, pth1, ptl1, 1)
            gate(1, fxh, fxl, tail=4)


def blocks(w, outs=None):
    k, n = w.shape
    return w.reshape(k // P, P, n // P, P).transpose(2, 1, 0, 3)


def slots(w):
    b = blocks(w)
    n, _, kb, _ = b.shape
    per = BLOCKS // kb
    return b.reshape(n // per, per, P, kb, P).transpose(0, 2, 1, 3, 4).reshape(n // per, P, SLOT)


def k_slots(w):
    return w.reshape(-1, P, SLOT)


def wide_slots(w):
    k, n = w.shape
    return w.reshape(k // 512, 4, P, n // 512, 512).transpose(3, 0, 2, 1, 4).reshape(-1, P, SLOT)


def rows(a):
    return a.reshape(-1, P).T


def tokens(a):
    t, f = a.shape
    return a.reshape(t, f // P, P).transpose(2, 1, 0).reshape(P, -1)


def lay_out(x):
    A = {}
    w_in = x["w_in"][0]
    gq, gk, gv, gg, glr, mq, mk, mv, mo, mg = np.split(w_in, np.cumsum(
        [512, 512, 1024, 1024, 16, 512, 512, 1024, 1024]), axis=1)
    up_w = x["w_up"][0]
    gate_up = blocks(up_w).reshape(2, KF, P, SLOT).transpose(1, 0, 2, 3).reshape(2 * KF, P, SLOT)
    mi = x["mla_w_in_2"][0]
    k1, k2 = mi[:, 1024:1056], mi[:, 1056:1088]
    uq = x["mla_w_uq_2"][0].reshape(512, NH, 192)
    pe1 = uq[:, :, 128:160].reshape(512, 4, 1, P)
    pe2 = uq[:, :, 160:192].reshape(512, 4, 1, P)
    ukv = x["mla_w_ukv_2"][0].reshape(512, NH, 256)
    grp = x["pool_w_group_2"][0]
    mod = wide_slots(x["w_mod"][0])
    parts = [slots(np.concatenate([glr, mg, np.zeros((D, P - 32), np.float32)], 1)),
             slots(gk), slots(mk), wide_slots(np.concatenate([gv, mv], 1)), slots(gq), slots(mq), slots(gg), slots(mo),
             slots(x["w_out"][0]), gate_up, k_slots(x["w_down"][0]), 
             slots(x["pool_w_in_2"][0]).reshape(2, 32, P, SLOT).transpose(1, 0, 2, 3).reshape(64, P, SLOT)]
    parts += [slots(g) for g in grp]
    parts += [k_slots(x["pool_w_out_2"][0]), slots(x["ple_w_proj_2"][0]), slots(x["ple_w_gate_2"][0]),
              slots(np.concatenate([mi[:, :1024]] + [k1] * 4 + [k2] * 4 + [mi[:, 1088:]], 1)),
              slots(uq[:, :, :128].reshape(512, 2048)),
              slots(np.concatenate([pe1, pe2], 2).reshape(512, 1024)),
              slots(ukv[:, :, :128].reshape(512, 2048)), wide_slots(ukv[:, :, 128:].reshape(512, 2048)),
              slots(x["mla_w_out_2"][0]), slots(x["ple_w_proj_2"][1]), slots(x["ple_w_gate_2"][1])]
    w = np.concatenate(parts)
    A["weights"] = np.concatenate([mod[:EARLY], w[:MOD_AT], mod[EARLY:], w[MOD_AT:]])
    assert w.shape[0] == SLOTS and mod.shape[0] == MSLOTS

    c2 = np.stack([rows(x["c"][0]), rows(x["c_ctx"])], 2).reshape(P, 2 * KD)
    gate_b = np.zeros((P, 2), np.float32)
    for d in range(2):
        gate_b[32 * d:32 * d + HEADS] = x["mlstm_b_gate"][0, d].T
    one = np.ones((P, 1), np.float32)
    invf = (np.float32(10000.0) ** (-np.arange(0, 64, 2, dtype=np.float32) / np.float32(64))).astype(np.float32)
    corr = np.concatenate([w / np.minimum(np.arange(16) + 1, w) for w in WINDOWS]).astype(np.float32)
    cols = {"c2": c2, "b_mod": rows(x["b_mod"][0]), "g1": rows(x["g_norm1"][0]), "g2": rows(x["g_norm2"][0]),
            "gfin": rows(x["g_final"]), "conv_w": x["conv_w"][0].reshape(9, KF, P).transpose(2, 1, 0).reshape(P, -1),
            "conv_b": rows(x["conv_b"][0]), "lr_b": rows(x["gla_b_lr"][0].reshape(-1)), "gla_g": rows(x["gla_g_norm"][0]),
            "ml_g": rows(x["mlstm_g_norm"][0]), "pre0": rows(x["pre_norm_2"][0]), "pre1": rows(x["pre_norm_2"][1]),
            "post0": rows(x["post_norm_2"][0]), "post1": rows(x["post_norm_2"][1]), "pscale": rows(x["pool_scale_2"][0]),
            "ple0": rows(x["ple_norm_2"][0]), "ple1": rows(x["ple_norm_2"][1]), "q_norm": rows(x["mla_q_norm_2"][0]),
            "kv_norm": rows(x["mla_kv_norm_2"][0]), "gate_b": gate_b, "eps": one * np.float32(EPS),
            "invf": np.tile(invf, 4)[:, None], "halfpi": one * np.float32(np.pi / 2), "corr": one * corr[None]}
    A["vec"] = np.concatenate([cols[n] for n in VEC], 1).astype(np.float32, copy=False)
    A["eye"] = np.eye(P, dtype=np.float32)
    A["xt"] = np.concatenate([tokens(x["x"][0]), tokens(x["ctx"][0])], 1)
    A["pt"] = np.concatenate([tokens(x["p_2"][0, 0]), tokens(x["p_2"][1, 0])], 1)
    A["pos"] = np.broadcast_to(x["positions_2"].astype(np.int32, copy=False), (P, T))
    A["w_lr"] = x["gla_w_lr"][0].transpose(1, 0, 2).reshape(16, 8 * P)
    i, j = np.arange(P)[:, None], np.arange(P)[None, :]
    lv = []
    for d in range(2):
        for h in LEVELS[1:]:
            m = (i // (2 * h) == j // (2 * h)) & (i // h % 2 == 0) & (j // h % 2 == 1)
            lv.append(m if d == 0 else m.T)
    A["lvl"] = np.concatenate(lv, 1).astype(np.int8).view(np.int32)
    rep = np.zeros((64, 8, P), np.float32)
    for n in range(8):
        rep[32 * (n // 4) + n % 4, n] = 1.0
    A["rep_sel"] = rep.reshape(64, -1)
    sel = np.zeros((32, 2, 64), np.float32)
    for f in range(2):
        for d in range(2):
            for h in range(HEADS):
                sel[16 + 8 * d + 4 * f + h, f, 32 * d + h] = 1.0
    A["sel_if"] = sel.reshape(32, -1)
    jj = np.arange(T)[None, :]
    mn = [np.where((t * P + i <= jj) if d == 0 else (t * P + i >= jj), 0.0, NEG) for d in range(2) for t in range(2)]
    A["maskn"] = np.concatenate(mn, 1).astype(np.float32)
    causal = np.where(j <= i, 0.0, NEG)
    A["maska"] = np.concatenate([causal, np.zeros((P, P)), causal], 1).astype(np.float32)
    return {k: np.ascontiguousarray(a) for k, a in A.items()}


def kernel(**inputs):
    import concourse.bacc as _bacc
    from concourse.bass_utils import run_bass_kernel_spmd as _run

    x = {k: np.asarray(a) for k, a in inputs.items()}
    arrays = lay_out(x)
    nc = _bacc.Bacc("TRN2", target_bir_lowering=False, num_devices=1, dynamic_dma_scratch_size=1024)
    aps = {k: nc.dram_tensor(f"in_{k}", a.shape, mybir.dt.from_np(a.dtype), kind="ExternalInput").ap()
           for k, a in arrays.items()}
    out = nc.dram_tensor("out_0", (P, KD * T), F32, kind="ExternalOutput").ap()
    build(nc, aps, out)
    r = _run(nc, [{f"in_{k}": a for k, a in arrays.items()}], core_ids=[0])
    got = r.results[0]["out_0"]
    return np.ascontiguousarray(got.reshape(P, KD, T).transpose(2, 1, 0).reshape(1, T, D))
```
